# Optimizing a Trainium2 kernel written in Bass

```python
import math
import jax
import jax.numpy as jnp
from jax import lax
import numpy as np

D_MODEL = 1024
BATCH = 1
SEQ = 1024
DEPTH = 1

HEAD_DIM = 64
A_GROUPS = ((128, 1), (512, 4), (2048, 16))
A_HEADS = 4
A_QKV_COLS = len(A_GROUPS) * 3 * A_HEADS * HEAD_DIM
A_OUT = A_HEADS * HEAD_DIM
B_Q_HEADS = 8
B_KV_HEADS = 2
B_GROUP = B_Q_HEADS // B_KV_HEADS
B_WINDOW = 128
B_Q_COLS = B_Q_HEADS * HEAD_DIM
B_KV_COLS = B_KV_HEADS * HEAD_DIM
M_HEADS = 4
M_HEAD_DIM = 128
M_Q_COLS = M_HEADS * M_HEAD_DIM
MEM_LEN = 256
IN_SPLITS = (A_QKV_COLS,
             A_QKV_COLS + B_Q_COLS,
             A_QKV_COLS + B_Q_COLS + B_KV_COLS,
             A_QKV_COLS + B_Q_COLS + 2 * B_KV_COLS)
IN_COLS = IN_SPLITS[-1] + M_Q_COLS
N_BRANCH = 3
D_FF = 2816
CONV_WIDTH = 3
ROPE_THETA = 500000.0
ROPE_DIM_FRAC = 4
BLOCK = 128
EPS = 1e-6

kernel_name = 'hybrid_dilated_swa_memory_convffn'

def rmsnorm(t, gain):
    tf = t.astype(jnp.float32)
    y = tf * lax.rsqrt(jnp.mean(tf * tf, axis=-1, keepdims=True) + EPS)
    return (y * gain.astype(jnp.float32)).astype(t.dtype)

def rope_partial(t, positions):
    dh = t.shape[-1]
    rot = dh // ROPE_DIM_FRAC
    half = rot // 2
    freqs = jnp.exp(jnp.arange(half, dtype=jnp.float32) * (-2.0 * math.log(ROPE_THETA) / rot))
    ang = positions.astype(jnp.float32)[:, :, None, None] * freqs
    cos, sin = jnp.cos(ang), jnp.sin(ang)
    t1 = t[..., :half].astype(jnp.float32)
    t2 = t[..., half:rot].astype(jnp.float32)
    rotated = jnp.concatenate([t1 * cos - t2 * sin, t2 * cos + t1 * sin], axis=-1).astype(t.dtype)
    return jnp.concatenate([rotated, t[..., rot:]], axis=-1)

def banded_attn(q, k, v, max_dist, sink=None):
    assert max_dist <= BLOCK
    n, hk, g, L, dh = q.shape
    nb = -(-L // BLOCK)
    pad = nb * BLOCK - L
    q = jnp.pad(q, ((0, 0), (0, 0), (0, 0), (0, pad), (0, 0))).reshape(n, hk, g, nb, BLOCK, dh)
    k = jnp.pad(k, ((0, 0), (0, 0), (0, pad), (0, 0))).reshape(n, hk, nb, BLOCK, dh)
    v = jnp.pad(v, ((0, 0), (0, 0), (0, pad), (0, 0))).reshape(n, hk, nb, BLOCK, dh)

    def with_prev(t):
        prev = jnp.pad(t, ((0, 0), (0, 0), (1, 0), (0, 0), (0, 0)))[:, :, :-1]
        return jnp.concatenate([prev, t], axis=3)

    kw, vw = with_prev(k), with_prev(v)
    s = jnp.einsum('nhgbqd,nhbkd->nhgbqk', q, kw).astype(jnp.float32) * (dh ** -0.5)
    qi = jnp.arange(BLOCK)[:, None]
    kj = jnp.arange(2 * BLOCK)[None, :]
    dist = qi + BLOCK - kj
    band = (dist >= 0) & (dist <= max_dist)
    blk = jnp.arange(nb)[:, None, None]
    mask = band[None] & ((blk > 0) | (kj[None] >= BLOCK))
    s = jnp.where(mask, s, -jnp.inf)
    lse = jax.nn.logsumexp(s, axis=-1)
    if sink is not None:
        lse = jnp.logaddexp(lse, sink.astype(jnp.float32)[None, :, :, None, None])
    p = jnp.exp(s - lse[..., None])
    o = jnp.einsum('nhgbqk,nhbkd->nhgbqd', p.astype(v.dtype), vw)
    o = o.reshape(n, hk, g, nb * BLOCK, dh)[:, :, :, :L]
    lse = lse.reshape(n, hk, g, nb * BLOCK)[:, :, :, :L]
    return o, lse

def to_residue(t, d):
    b, s, h, dh = t.shape
    return t.reshape(b, s // d, d, h, dh).transpose(0, 2, 3, 1, 4).reshape(b * d, h, s // d, dh)

def from_residue(t, d):
    nd, h, L = t.shape[:3]
    rest = t.shape[3:]
    t = t.reshape(nd // d, d, h, L, *rest)
    t = jnp.moveaxis(t, 3, 1)
    return t.reshape(nd // d, L * d, h, *rest)

def dilated_mixture_attn(qkv_a, positions, q_gain, k_gain):
    b, s = qkv_a.shape[:2]
    outs, lses = [], []
    for gi, (window, dil) in enumerate(A_GROUPS):
        q = rope_partial(rmsnorm(qkv_a[:, :, gi, 0], q_gain[gi]), positions)
        k = rope_partial(rmsnorm(qkv_a[:, :, gi, 1], k_gain[gi]), positions)
        v = qkv_a[:, :, gi, 2]
        o, lse = banded_attn(to_residue(q, dil)[:, :, None], to_residue(k, dil),
                             to_residue(v, dil), window // dil)
        outs.append(from_residue(o[:, :, 0], dil))
        lses.append(from_residue(lse[:, :, 0], dil))
    w = jax.nn.softmax(jnp.stack(lses), axis=0)
    o = jnp.einsum('gbshd,gbsh->bshd', jnp.stack(outs), w.astype(qkv_a.dtype))
    return o.reshape(b, s, A_OUT)

def sink_swa_gqa(q, k, v, positions, q_gain, k_gain, sinks):
    b, s = q.shape[:2]
    q = rope_partial(rmsnorm(q, q_gain), positions)
    k = rope_partial(rmsnorm(k, k_gain), positions)
    qg = q.reshape(b, s, B_KV_HEADS, B_GROUP, HEAD_DIM).transpose(0, 2, 3, 1, 4)
    o, _ = banded_attn(qg, k.transpose(0, 2, 1, 3), v.transpose(0, 2, 1, 3),
                       B_WINDOW - 1, sink=sinks.reshape(B_KV_HEADS, B_GROUP))
    return o.transpose(0, 3, 1, 2, 4).reshape(b, s, B_Q_COLS)

def memory_attn(mq, mem, mem_gain, w_kv, q_gain, k_gain):
    b, s = mq.shape[:2]
    m = mem.shape[1]
    kv = (rmsnorm(mem, mem_gain) @ w_kv).reshape(b, m, 2, M_HEADS, M_HEAD_DIM)
    mk = rmsnorm(kv[:, :, 0], k_gain)
    mv = kv[:, :, 1]
    q = rmsnorm(mq.reshape(b, s, M_HEADS, M_HEAD_DIM), q_gain)
    sc = jnp.einsum('bshd,bmhd->bhsm', q, mk).astype(jnp.float32) * (M_HEAD_DIM ** -0.5)
    p = jax.nn.softmax(sc, axis=-1)
    o = jnp.einsum('bhsm,bmhd->bshd', p.astype(mv.dtype), mv)
    return o.reshape(b, s, M_Q_COLS)

def conv_ffn(h, w_up, conv_w, conv_b, w_down):
    s = h.shape[1]
    u = h @ w_up
    up = jnp.pad(u, ((0, 0), (CONV_WIDTH - 1, 0), (0, 0)))
    c = conv_b
    for j in range(CONV_WIDTH):
        c = c + conv_w[j] * up[:, j:j + s]
    a, g = jnp.split(c, 2, axis=-1)
    return (jax.nn.silu(a) * g) @ w_down

def setup_inputs(seed: int = 0) -> dict:
    key = jax.random.key(seed)
    ks = jax.random.split(key, 32)
    f32 = jnp.float32
    L = DEPTH

    def w(k, shape, fan_in):
        return jax.random.normal(k, shape, f32) * (fan_in ** -0.5)

    def gain(k, shape):
        return 1.0 + 0.02 * jax.random.normal(k, shape, f32)

    positions = (jax.random.randint(ks[2], (BATCH, 1), 0, 1024, dtype=jnp.int32)
                 + jnp.arange(SEQ, dtype=jnp.int32)[None, :])
    return {
        'x': jax.random.normal(ks[0], (BATCH, SEQ, D_MODEL), f32),
        'mem': jax.random.normal(ks[1], (BATCH, MEM_LEN, D_MODEL), f32),
        'positions': positions,
        'attn_norm': gain(ks[3], (L, D_MODEL)),
        'w_in': w(ks[4], (L, D_MODEL, IN_COLS), D_MODEL),
        'a_q_norm': gain(ks[5], (L, len(A_GROUPS), HEAD_DIM)),
        'a_k_norm': gain(ks[6], (L, len(A_GROUPS), HEAD_DIM)),
        'b_q_norm': gain(ks[7], (L, HEAD_DIM)),
        'b_k_norm': gain(ks[8], (L, HEAD_DIM)),
        'b_sinks': jax.random.normal(ks[9], (L, B_Q_HEADS), f32),
        'mem_norm': gain(ks[10], (L, D_MODEL)),
        'w_mem_kv': w(ks[11], (L, D_MODEL, 2 * M_Q_COLS), D_MODEL),
        'm_q_norm': gain(ks[12], (L, M_HEAD_DIM)),
        'm_k_norm': gain(ks[13], (L, M_HEAD_DIM)),
        'w_o_a': w(ks[14], (L, A_OUT, D_MODEL), A_OUT),
        'w_o_b': w(ks[15], (L, B_Q_COLS, D_MODEL), B_Q_COLS),
        'w_o_m': w(ks[16], (L, M_Q_COLS, D_MODEL), M_Q_COLS),
        'w_gate': w(ks[17], (L, D_MODEL, N_BRANCH * D_MODEL), D_MODEL),
        'b_gate': 0.01 * jax.random.normal(ks[18], (L, N_BRANCH * D_MODEL), f32),
        'w_out': w(ks[19], (L, D_MODEL, D_MODEL), D_MODEL),
        'ffn_norm': gain(ks[20], (L, D_MODEL)),
        'w_up': w(ks[21], (L, D_MODEL, 2 * D_FF), D_MODEL),
        'conv_w': w(ks[22], (L, CONV_WIDTH, 2 * D_FF), CONV_WIDTH),
        'conv_b': 0.01 * jax.random.normal(ks[23], (L, 2 * D_FF), f32),
        'w_down': w(ks[24], (L, D_FF, D_MODEL), D_FF),
    }

def reference(x, mem, positions, attn_norm, w_in, a_q_norm, a_k_norm, b_q_norm, b_k_norm,
              b_sinks, mem_norm, w_mem_kv, m_q_norm, m_k_norm, w_o_a, w_o_b, w_o_m,
              w_gate, b_gate, w_out, ffn_norm, w_up, conv_w, conv_b, w_down):
    b, s, _ = x.shape
    for l in range(DEPTH):
        h = rmsnorm(x, attn_norm[l])
        proj = h @ w_in[l]
        qkv_a, b_q, b_k, b_v, m_q = jnp.split(proj, IN_SPLITS, axis=-1)
        qkv_a = qkv_a.reshape(b, s, len(A_GROUPS), 3, A_HEADS, HEAD_DIM)
        o_a = dilated_mixture_attn(qkv_a, positions, a_q_norm[l], a_k_norm[l])
        o_b = sink_swa_gqa(b_q.reshape(b, s, B_Q_HEADS, HEAD_DIM),
                           b_k.reshape(b, s, B_KV_HEADS, HEAD_DIM),
                           b_v.reshape(b, s, B_KV_HEADS, HEAD_DIM),
                           positions, b_q_norm[l], b_k_norm[l], b_sinks[l])
        o_m = memory_attn(m_q, mem, mem_norm[l], w_mem_kv[l], m_q_norm[l], m_k_norm[l])
        gates = jax.nn.sigmoid((h @ w_gate[l] + b_gate[l]).astype(jnp.float32))
        gates = gates.astype(x.dtype).reshape(b, s, N_BRANCH, D_MODEL)
        merged = (gates[:, :, 0] * (o_a @ w_o_a[l])
                  + gates[:, :, 1] * (o_b @ w_o_b[l])
                  + gates[:, :, 2] * (o_m @ w_o_m[l]))
        x = x + merged @ w_out[l]
        x = x + conv_ffn(rmsnorm(x, ffn_norm[l]), w_up[l], conv_w[l], conv_b[l], w_down[l])
    return x


_drawn_inputs = setup_inputs


def setup_inputs(seed=0):
    import zlib

    import numpy as np

    out = dict(_drawn_inputs(seed))
    spreads = {}
    factors = {'attn_norm': 8.0,
     'a_q_norm': 8.0,
     'a_k_norm': 8.0,
     'b_q_norm': 8.0,
     'b_k_norm': 8.0,
     'b_sinks': 55.203,
     'mem_norm': 8.0,
     'm_q_norm': 8.0,
     'm_k_norm': 8.0,
     'b_gate': 33.767,
     'ffn_norm': 10.677,
     'conv_b': 20.917}
    for name, (base, spread) in spreads.items():
        noise = np.random.default_rng([zlib.crc32(name.encode()), seed]).standard_normal(out[name].shape)
        drawn = base * np.exp(spread * noise) if base else spread * noise
        out[name] = jnp.asarray(drawn.astype(out[name].dtype))
    for name, factor in factors.items():
        out[name] = (out[name] * factor).astype(out[name].dtype)
    return out
```

```python
import math
from contextlib import ExitStack

import concourse.bass as bass
import numpy as np
from concourse import mybir

F32 = mybir.dt.float32
F32R = mybir.dt.float32r
I32 = mybir.dt.int32
ALU = mybir.AluOpType
ACT = mybir.ActivationFunctionType
AX = mybir.AxisListType

P = 128
EPS = 1e-6
MASKED = 1e30
START_MIN = 3e38
ROPE_THETA = 500000.0
ROT = 16
HALF = ROT // 2

STAGES = [
    ("memk", 0, 0, 0, 512, 0, 2),
    ("memv", 0, 0, 512, 512, 0, 2),
    ("A", 0, 0, 0, 512, 256, 8),
    ("A", 1, 1, 768, 512, 256, 8),
    ("A", 2, 2, 1536, 512, 256, 8),
    ("B", 0, 0, 2304, 512, 256, 8),
    ("M", 0, 0, 3072, 512, 0, 8),
]
JOBS = [(s, t) for s, st in enumerate(STAGES) for t in range(st[6])]
KIND = [STAGES[s][0] for s, _ in JOBS]
NJ = len(JOBS)
UNITS_OF = {"memk": 0, "memv": 0, "A": 2, "B": 4, "M": 2}
UNITS = [(j, u) for j in range(NJ) for u in range(UNITS_OF[KIND[j]])]
NU = len(UNITS)
LAG = 2
NRAW = 2
RQ, RK = 3, 4
BATCHES = {"memk": 1, "memv": 0, "A": 1, "B": 2, "M": 1}


def count(kinds, upto):
    return sum(k in kinds for k in KIND[:max(upto, 0)])


QK_KINDS = ("memk", "A", "B", "M")
V_KINDS = ("memv", "A", "B")
HAS_Q = ("A", "B", "M")
HAS_K = ("memk", "A", "B")


def batches(upto):
    return sum(BATCHES[k] for k in KIND[:max(upto, 0)])


def units_before(j):
    return sum(UNITS_OF[k] for k in KIND[:max(j, 0)])


def has_prev(j):
    s, t = JOBS[j]
    kind, order = STAGES[s][:2]
    if kind == "M":
        return True
    return t > 0 if order == 0 else (t % 2 == 1 if order == 1 else False)


def step_slices(j):
    n = UNITS_OF[KIND[j - LAG]] if 0 <= j - LAG < NJ else 0
    return {0: [], 2: [1, 4], 4: [0, 2, 4, 6]}[n]


def token_tile(ap, order, tile):
    if order == 0:
        return ap[:, tile * P:(tile + 1) * P]
    if order == 1:
        return ap.rearrange("p (b i r) -> p r b i", b=2, r=4)[:, tile // 2, tile % 2, :]
    return ap.rearrange("p (i t) -> p t i", t=8)[:, tile]


def layer(nc, x, mem, positions, attn_norm, w_in, a_q_norm, a_k_norm, b_q_norm, b_k_norm, b_sinks,
          mem_norm, w_mem_kv, m_q_norm, m_k_norm, w_o_a, w_o_b, w_o_m, w_gate, b_gate, w_out,
          ffn_norm, w_up, conv_w, conv_b, w_down, out):
    S, D = x.shape[1], x.shape[2]
    NT, NK = S // P, D // P
    FF = w_down.shape[1]
    x_t = x[0].rearrange("(t p) d -> t p d", p=P)
    mem_t = mem[0].rearrange("(t p) d -> t p d", p=P)
    out_t = out[0].rearrange("(t p) d -> t p d", p=P)

    stats_dram = [nc.dram_tensor(f"stats_{g}", (S, 8), F32, kind="Internal").ap() for g in (1, 2)]

    with ExitStack() as whole:
        def sb(name, shape, dt=F32, ctx=whole):
            return ctx.enter_context(nc.sbuf_tensor(name, shape, dt))

        def sem(name):
            return whole.enter_context(nc.semaphore(name))

        ps = whole.enter_context(nc.psum_tensor("ps", [P, 8, 512], F32))
        act_hi = sb("act_hi", [P, NK, S], F32R)
        act_lo = sb("act_lo", [P, NK, S], F32R)
        ident = sb("ident", [P, P])
        ident_ready = sem("ident_ready")
        half_power = sb("half_power", [P, 16])

        attn_out = sb("attn_out", [P, 10, S])
        x1, spare = attn_out[:, 0:NT, :], attn_out[:, NT:NT + 2, :]

        input_projections(nc, x_t, mem_t, positions, attn_norm, w_in, a_q_norm, a_k_norm, b_q_norm,
                          b_k_norm, b_sinks, mem_norm, w_mem_kv, m_q_norm, m_k_norm, stats_dram,
                          ps, act_hi, act_lo, ident, ident_ready, half_power, attn_out)
        with ExitStack() as middle:
            merged = sb("merged", [P, NK, S], ctx=middle)
            gated_outputs(nc, w_gate, b_gate, w_o_a, w_o_b, w_o_m, ps, act_hi, act_lo, attn_out, merged)
            output_projection(nc, x_t, w_out, ffn_norm, ps, act_hi, act_lo, ident, half_power, merged, x1)
        feed_forward(nc, w_up, conv_w, conv_b, w_down, out_t, ps, act_hi, act_lo, ident, x1, spare)


def input_projections(nc, x_t, mem_t, positions, attn_norm, w_in, a_q_norm, a_k_norm, b_q_norm, b_k_norm,
                      b_sinks, mem_norm, w_mem_kv, m_q_norm, m_k_norm, stats_dram, ps, act_hi, act_lo,
                      ident, ident_ready, half_power, attn_out):
    NK, S = act_hi.shape[1], act_hi.shape[2]
    NX = 10
    inv_d = 1.0 / (NK * P)
    with ExitStack() as ctx:
        def sb(name, shape, dt=F32):
            return ctx.enter_context(nc.sbuf_tensor(name, shape, dt))

        def sem(name):
            return ctx.enter_context(nc.semaphore(name))

        w_raw = sb("w_raw", [P, NRAW, 768])
        w_hi = sb("w_hi", [P, NK, 768], F32R)
        w_lo = sb("w_lo", [P, NK, 768], F32R)
        k_mem = sb("k_mem", [P, 4, 256])
        v_mem = sb("v_mem", [P, 2, 512])
        masks = sb("masks", [P, 4, P])
        rope_cos = sb("rope_cos", [P, 3, 8, ROT])
        rope_sin = sb("rope_sin", [P, 3, 8, ROT])
        gains = sb("gains", [P, 768])
        norm_gain = sb("norm_gain", [P, 2, NK])
        neg_sink = sb("neg_sink", [P, 8])
        row_sums = sb("row_sums", [P, 16])
        row_rstd = sb("row_rstd", [P, 16])
        stats = sb("stats", [P, 3, 8, 8])
        with ExitStack() as early:
            mem_hi = early.enter_context(nc.sbuf_tensor("mem_hi", [P, NK, 256], F32R))
            mem_lo = early.enter_context(nc.sbuf_tensor("mem_lo", [P, NK, 256], F32R))
        q_ring = sb("q_ring", [P, RQ, 4, P])
        k_ring = sb("k_ring", [P, RK, 2, P])
        v_ring = sb("v_ring", [P, RK, 256])
        prob = sb("prob", [P, 2, 2, 256])
        prob_t = sb("prob_t", [P, 2, 2, 2, P])
        square = sb("square", [P, 640])
        qk = sb("qk", [P, 2, 640])
        rope_a = sb("rope_a", [P, 10, ROT])
        rope_b = sb("rope_b", [P, 10, ROT])
        head_ss = sb("head_ss", [P, 2, 10])
        head_rstd = sb("head_rstd", [P, 2, 10])
        small = sb("small", [P, 2, 12])
        parity = sb("parity", [P, 2])
        pos_i = sb("pos_i", [P, 3, 8], I32)
        pos_f = sb("pos_f", [P, 3, 8])
        angle = prob[:, 1, :, :].rearrange("p a b -> p (a b)")[:, 0:384].rearrange("p (s n) -> p s n", s=2)
        turns = prob_t[:, 0, :, :, :].rearrange("p e b n -> p (e b n)")[:, 0:384].rearrange("p (s n) -> p s n", s=2)
        merge = {n: sb(f"merge_{n}", [P, w]) for n, w in
                 (("max", 32), ("e", 96), ("total", 32), ("f", 96))}

        x_in = [sem(f"x_in{n}") for n in range(NX)]
        const_in = sem("const_in")
        pos_in = sem("pos_in")
        masks_built = sem("masks_built")
        x_sq, x_rstd, x_scaled, x_turned, x_gained, x_hi, x_lo = (
            sem(n) for n in ("x_sq", "x_rstd", "x_scaled", "x_turned", "x_gained", "x_hi", "x_lo"))
        angles_ready, sines_ready, rope_ready = sem("angles_ready"), sem("sines_ready"), sem("rope_ready")
        sink_ready = sem("sink_ready")
        raw_in = [sem(f"raw_in{n}") for n in range(NRAW)]
        w_hi_done, w_lo_done, w_used = sem("w_hi_done"), sem("w_lo_done"), sem("w_used")
        proj_done, sq_done, ss_done, rstd_done, normed, roped = (
            sem(n) for n in ("proj_done", "sq_done", "ss_done", "rstd_done", "normed", "roped"))
        v_done, turned, q_done, k_done = (sem(n) for n in ("v_done", "turned", "q_done", "k_done"))
        scored, min_done, exp_done, prob_done, prob_turned, prob_copied, pv_done, o_done, sink_gap, sink_exp = (
            sem(n) for n in ("scored", "min_done", "exp_done", "prob_done", "prob_turned", "prob_copied",
                             "pv_done", "o_done", "sink_gap", "sink_exp"))
        spread_done, first_scored = sem("spread_done"), sem("first_scored")
        stats_out, stats_in, shift_ready, shift_exp, factors_ready, factor_turned, factor_used = (
            sem(n) for n in ("stats_out", "stats_in", "shift_ready", "shift_exp", "factors_ready",
                             "factor_turned", "factor_used"))
        dve_chain, act_chain, pool_chain = sem("dve_chain"), sem("act_chain"), sem("pool_chain")

        TQ, SC, PT, OB = 4, 5, 6, 7

        def proj_a(j):
            return ps[:, 2 * (j % 2), :]

        def proj_b(j):
            return ps[:, 2 * (j % 2) + 1, 0:256]

        def wide(n):
            return ps[:, 2 * (n % 2):2 * (n % 2) + 2, :].rearrange("p b n -> p (b n)")

        scores = ps[:, SC, :].rearrange("p (e n) -> p e n", e=2)
        prob_turn = ps[:, PT, :].rearrange("p (e b n) -> p e b n", e=2, b=2)

        last_job_of = {s: max(j for j in range(NJ) if JOBS[j][0] == s) for s in range(len(STAGES))}
        merge_from = next(j for j in range(NJ) if KIND[j] == "B") + 4
        merge_at = {merge_from + 1 + i // 3: [3 * (i // 3) + n for n in range(3)] for i in range(12)}

        def merge_batch(m):
            return m // 6, (m // 3) % 2, m % 3

        x_slot = [attn_out[:, n, :] for n in range(NX)]

        def x_low(pool, n):
            pool.wait_ge(x_hi, n + 1)
            hi, lo, c = (mem_hi, mem_lo, n) if n < 2 else (act_hi, act_lo, n - 2)
            pool.tensor_tensor(lo[:, :, c * P:(c + 1) * P], x_slot[n].rearrange("p (k n) -> p k n", n=P),
                               hi[:, :, c * P:(c + 1) * P].bitcast(F32), ALU.subtract).then_inc(x_lo, 1)

        def v_wait(eng, j):
            before = units_before(j - RK + 2)
            if before:
                eng.wait_ge(pv_done, before)

        def count_b(n):
            return sum(KIND[j] == "B" for j, _ in UNITS[:n])

        def count_ab(n):
            return sum(KIND[j] != "M" for j, _ in UNITS[:n])

        def count_bm(n):
            return sum(KIND[j] != "A" for j, _ in UNITS[:n])

        def unit_stats(n, e):
            j, u = UNITS[n]
            s, t = JOBS[j]
            if KIND[j] == "A":
                g = STAGES[s][2]
                h = 2 * u + e
                return stats[:, g, t, h:h + 1], stats[:, g, t, 4 + h:5 + h]
            return small[:, n % 2, e:e + 1], small[:, n % 2, 2 + e:3 + e]

        block = ctx.enter_context(nc.Block())

        @block.sync
        def _(sp):
            for n in range(NX):
                sp.dma_start(x_slot[n], mem_t[n] if n < 2 else x_t[n - 2]).then_inc(x_in[n], 16)
                if n == 1:
                    with nc.allow_non_contiguous_dma(reason="one gain per partition"):
                        sp.dma_start(norm_gain[:, 0, :], attn_norm[0].rearrange("(k p) -> p k", p=P)).then_inc(const_in, 16)
                        sp.dma_start(norm_gain[:, 1, :], mem_norm[0].rearrange("(k p) -> p k", p=P)).then_inc(const_in, 16)
            def reorder_stats():
                last_a1 = units_before(last_job_of[3] + 1)
                last_a2 = units_before(last_job_of[4] + 1)
                sp.wait_ge(exp_done, last_a1)
                for b in range(2):
                    sp.dma_start(stats_dram[0].rearrange("(b i r) c -> b i r c", b=2, r=4)[b],
                                 stats[:, 1].rearrange("p (r b) c -> p b r c", b=2)[:, b]).then_inc(stats_out, 16)
                sp.wait_ge(exp_done, last_a2)
                sp.dma_start(stats_dram[1].rearrange("(i t) c -> i t c", t=8), stats[:, 2]).then_inc(stats_out, 16)
                sp.wait_ge(stats_out, 48)
                for g in range(2):
                    sp.dma_start(stats[:, 1 + g], stats_dram[g].rearrange("(t p) c -> p t c", p=P)).then_inc(stats_in, 16)

            for n in range(8 * len(STAGES)):
                kind, _, _, col, na, nb, _ = STAGES[n // 8]
                src = w_mem_kv if kind in ("memk", "memv") else w_in
                k = n % 8
                if n == 8 * 6:
                    reorder_stats()
                if n >= NRAW:
                    sp.wait_ge(w_lo_done, n - NRAW + 1)
                sp.dma_start(w_raw[:, n % NRAW, 0:na + nb],
                             src[0, k * P:(k + 1) * P, col:col + na + nb]).then_inc(raw_in[n % NRAW], 16)

        @block.gpsimd
        def _(pool):
            chain = [0]

            def link(ins):
                chain[0] += 1
                ins.then_inc(pool_chain, 1)
                pool.wait_ge(pool_chain, chain[0])

            link(pool.memset(ident[:], 0.0))
            pool.affine_select(out=ident[:], in_=ident[:], compare_op=ALU.not_equal, fill=1.0, base=0,
                               pattern=[[-1, P]], channel_multiplier=1).then_inc(ident_ready, 1)
            link(pool.memset(half_power[:], -0.5))
            link(pool.memset(masks[:], 0.0))
            for m, sign, base in ((0, 1, -1), (1, 1, 0), (2, -1, 0), (3, -1, 0)):
                link(pool.affine_select(out=masks[:, m, :], in_=masks[:, m, :], compare_op=ALU.is_ge, fill=MASKED,
                                        base=base, pattern=[[sign, P]], channel_multiplier=-sign))
            link(pool.memset(prob[:, 1, 1, 0:64], 0.0))
            pool.affine_select(out=prob[:, 1, 1, 0:64], in_=prob[:, 1, 1, 0:64], compare_op=ALU.not_equal, fill=MASKED,
                               base=0, pattern=[[-2, 64]], channel_multiplier=1).then_inc(masks_built, 1)

            for n in range(NX):
                pool.wait_ge(x_sq, n + 1)
                link(pool.tensor_scalar(row_rstd[:, n:n + 1], row_sums[:, n:n + 1], inv_d, EPS, ALU.mult, ALU.add))
                pool.tensor_tensor(row_rstd[:, n:n + 1], row_rstd[:, n:n + 1], half_power[:, 0:1],
                                   ALU.pow).then_inc(x_rstd, 1)
                if n >= 2:
                    x_low(pool, n - 2)
            x_low(pool, NX - 2)
            x_low(pool, NX - 1)

            def split_slice(n):
                kind, _, _, col, na, nb, _ = STAGES[n // 8]
                pool.wait_ge(w_hi_done, n + 1)
                pool.tensor_tensor(w_lo[:, n % 8, 0:na + nb], w_raw[:, n % NRAW, 0:na + nb],
                                   w_hi[:, n % 8, 0:na + nb].bitcast(F32), ALU.subtract).then_inc(w_lo_done, 1)

            def norm_and_rope(j):
                s, t = JOBS[j]
                kind, order, g = STAGES[s][:3]
                if kind not in QK_KINDS:
                    return
                i = count(QK_KINDS, j)
                nh, dh = {"memk": (4, 128), "A": (8, 64), "B": (10, 64), "M": (4, 128)}[kind]
                pool.wait_ge(ss_done, i + 1)
                link(pool.tensor_scalar(head_rstd[:, i % 2, 0:nh], head_ss[:, i % 2, 0:nh], 1.0 / dh, EPS,
                                        ALU.mult, ALU.add))
                pool.tensor_tensor(head_rstd[:, i % 2, 0:nh], head_rstd[:, i % 2, 0:nh], half_power[:, 0:nh],
                                   ALU.pow).then_inc(rstd_done, 1)
                buf = qk[:, i % 2, 0:nh * dh].rearrange("p (h d) -> p h d", d=dh)
                pool.wait_ge(normed, i + 1)
                if i == 0:
                    pool.wait_ge(const_in, 16 * 9)
                parts = {"memk": ((0, 4, 640),), "A": ((0, 4, 64 * g), (4, 8, 192 + 64 * g)),
                         "B": ((0, 8, 384), (8, 10, 448)), "M": ((0, 4, 512),)}[kind]
                for h0, h1, off in parts:
                    ins = pool.tensor_tensor(buf[:, h0:h1, :], buf[:, h0:h1, :],
                                             gains[:, off:off + dh].unsqueeze(1).to_broadcast([P, h1 - h0, dh]), ALU.mult)
                    if dh == 64 or (h0, h1, off) != parts[-1]:
                        link(ins)
                if dh == 128:
                    ins.then_inc(roped, 1)
                    return
                if kind == "A" and g == 0 and t == 0:
                    pool.wait_ge(rope_ready, 1)
                cos = rope_cos[:, order, t, :].unsqueeze(1).to_broadcast([P, nh, ROT])
                sin = rope_sin[:, order, t, :].unsqueeze(1)
                link(pool.tensor_tensor(rope_a[:, 0:nh, :], buf[:, :, 0:ROT], cos, ALU.mult))
                link(pool.tensor_tensor(rope_b[:, 0:nh, 0:HALF], buf[:, :, HALF:ROT],
                                        sin[:, :, 0:HALF].to_broadcast([P, nh, HALF]), ALU.mult))
                link(pool.tensor_tensor(rope_b[:, 0:nh, HALF:ROT], buf[:, :, 0:HALF],
                                        sin[:, :, HALF:ROT].to_broadcast([P, nh, HALF]), ALU.mult))
                pool.tensor_tensor(buf[:, :, 0:ROT], rope_a[:, 0:nh, :], rope_b[:, 0:nh, :],
                                   ALU.add).then_inc(roped, 1)

            for k in range(8):
                split_slice(k)
            for j in range(NJ + LAG + 1):
                if 0 <= j - 1 < NJ:
                    norm_and_rope(j - 1)
                for s in last_job_of:
                    if last_job_of[s] == j and s + 1 < len(STAGES):
                        for k in range(8):
                            split_slice(8 * (s + 1) + k)

        @block.scalar
        def _(act):
            with nc.allow_non_contiguous_dma(reason="positions and gains, once"):
                p0 = positions[0]
                act.dma_start(pos_i[:, 0, :], p0.rearrange("(t p) -> p t", p=P)).then_inc(pos_in, 16)
                for b in range(2):
                    act.dma_start(pos_i[:, 1, :].rearrange("p (r b) -> p b r", b=2)[:, b],
                                  p0.rearrange("(b i r) -> b i r", b=2, r=4)[b]).then_inc(pos_in, 16)
                act.dma_start(pos_i[:, 2, :], p0.rearrange("(i t) -> i t", t=8)).then_inc(pos_in, 16)
                for off, src in ((0, a_q_norm[0].rearrange("g d -> (g d)")), (192, a_k_norm[0].rearrange("g d -> (g d)")),
                                 (384, b_q_norm[0]), (448, b_k_norm[0]), (512, m_q_norm[0]), (640, m_k_norm[0])):
                    act.dma_start(gains[:, off:off + src.shape[0]], src.partition_broadcast(P)).then_inc(const_in, 16)
                act.dma_start(neg_sink[:, :], b_sinks[0].partition_broadcast(P)).then_inc(const_in, 16)

            junk = ps[:, PT:OB + 1, :].rearrange("p b n -> p (b n)")

            def x_high(n):
                act.wait_ge(x_gained, n + 1)
                hi, c = (mem_hi, n) if n < 2 else (act_hi, n - 2)
                act.activation(hi[:, :, c * P:(c + 1) * P], x_slot[n].rearrange("p (k n) -> p k n", n=P),
                               ACT.Copy).then_inc(x_hi, 1)

            chain = [0]

            def link(ins):
                chain[0] += 1
                ins.then_inc(act_chain, 1)
                act.wait_ge(act_chain, chain[0])

            for n in range(NX):
                act.wait_ge(x_in[n], 16)
                if n >= 1:
                    act.wait_ge(x_sq, n)
                act.activation(junk, x_slot[n], ACT.Square, accum_out=row_sums[:, n:n + 1]).then_inc(x_sq, 1)
                if n >= 2:
                    x_high(n - 2)
            x_high(NX - 2)
            x_high(NX - 1)
            act.wait_ge(angles_ready, 1)
            sines = angle
            act.activation(turns[:, :, :], sines, ACT.Sin).then_inc(sines_ready, 1)

            def cast_slice(n):
                _, _, _, col, na, nb, _ = STAGES[n // 8]
                act.wait_ge(raw_in[n % NRAW], 16 * (n // NRAW + 1))
                if n >= 8:
                    act.wait_ge(w_used, n - 7)
                act.activation(w_hi[:, n % 8, 0:na + nb], w_raw[:, n % NRAW, 0:na + nb], ACT.Copy).then_inc(w_hi_done, 1)

            def squares(j):
                kind = KIND[j]
                act.wait_ge(proj_done, j + 1)
                if kind in QK_KINDS:
                    i = count(QK_KINDS, j)
                    if i >= 1:
                        act.wait_ge(ss_done, i)
                    spreads = sum(len(v) for jj, v in merge_at.items() if jj <= j)
                    if spreads:
                        act.wait_ge(factor_turned, spreads)
                    ins = act.activation(square[:, 0:512], proj_a(j), ACT.Square)
                    if kind == "B":
                        ins = act.activation(square[:, 512:640], proj_b(j)[:, 0:128], ACT.Square)
                    ins.then_inc(sq_done, 1)
                    if kind == "B":
                        act.wait_ge(sq_done, i + 1)
                if kind in V_KINDS:
                    t = JOBS[j][1]
                    if kind == "memv":
                        ins = act.activation(v_mem[:, t, :], proj_a(j), ACT.Copy)
                    else:
                        v_wait(act, j)
                        c0 = 0 if kind == "A" else 128
                        ins = act.activation(v_ring[:, j % RK, 0:256 - c0], proj_b(j)[:, c0:256], ACT.Copy)
                    ins.then_inc(v_done, 1)

            def copy_q(j):
                kind = KIND[j]
                if kind not in HAS_Q:
                    return
                act.wait_ge(turned, batches(j) + 1)
                before = units_before(j - RQ + 1)
                if before:
                    act.wait_ge(scored, before)
                nb = 2 if kind == "A" else 4
                scale = -(1.0 / math.sqrt(128 if kind == "M" else 64))
                act.activation(q_ring[:, j % RQ, 0:nb, :], ps[:, TQ, :].rearrange("p (b n) -> p b n", n=P)[:, 0:nb, :],
                               ACT.Copy, scale=scale).then_inc(q_done, 1)

            def exps(n):
                j, u = UNITS[n]
                kind, (s, t) = KIND[j], JOBS[j]
                act.wait_ge(min_done, n + 1)
                c0 = 0 if has_prev(j) else P
                for e in range(2):
                    low, total = unit_stats(n, e)
                    src = scores[:, e, :] if kind == "M" else prob[:, n % 2, e, c0:256]
                    if kind == "M" and n >= 2 and e == 0:
                        act.wait_ge(prob_turned, n - 1)
                    ins = act.activation(prob[:, n % 2, e, c0:256], src, ACT.Exp, bias=low, scale=-1.0, accum_out=total)
                    if e == 0:
                        link(ins)
                ins.then_inc(exp_done, 1)
                if kind == "B":
                    b = count_b(n)
                    act.wait_ge(sink_gap, b + 1)
                    act.activation(small[:, n % 2, 4:6], small[:, n % 2, 4:6], ACT.Exp).then_inc(sink_exp, 1)

            def copy_probs(n):
                c0 = 0 if has_prev(UNITS[n][0]) else 1
                act.wait_ge(prob_turned, n + 1)
                if n >= 2:
                    act.wait_ge(pv_done, n - 1)
                act.activation(prob_t[:, n % 2, :, c0:2, :], prob_turn[:, :, c0:2, :], ACT.Copy).then_inc(prob_copied, 1)

            def spread_factors(m, j):
                pair, half, g = merge_batch(m)
                if m == 0:
                    act.wait_ge(factors_ready, 1)
                    act.wait_ge(ss_done, count(QK_KINDS, j))
                else:
                    act.wait_ge(factor_turned, m)
                f = merge["f"][:].rearrange("p (g t h) -> p g t h", g=3, h=4)
                act.activation(square[:, 0:512].rearrange("p (t e d) -> p t e d", t=4, e=2),
                               f[:, g, 4 * half:4 * half + 4, 2 * pair:2 * pair + 2].unsqueeze(3).to_broadcast([P, 4, 2, 64]),
                               ACT.Copy).then_inc(spread_done, 1)

            for k in range(8):
                cast_slice(k)
            n = 0
            for j in range(NJ + LAG + 1):
                if 0 <= j - 1 < NJ:
                    squares(j - 1)
                for k in range(8):
                    if k in step_slices(j):
                        exps(n)
                        if n >= 1:
                            copy_probs(n - 1)
                        n += 1
                    if k == 5 and 0 <= j - 1 < NJ:
                        copy_q(j - 1)
                    if j in last_job_of.values() and JOBS[j][0] + 1 < len(STAGES):
                        cast_slice(8 * (JOBS[j][0] + 1) + k)
                if j == merge_from:
                    act.wait_ge(shift_ready, 1)
                    act.activation(merge["e"][:], merge["e"][:], ACT.Exp).then_inc(shift_exp, 1)
                for m in merge_at.get(j, ()):
                    if m == merge_at[j][0]:
                        act.wait_ge(ss_done, count(QK_KINDS, j))
                    spread_factors(m, j)
            copy_probs(NU - 1)

        @block.vector
        def _(dve):
            chain = [0]

            def link(ins):
                chain[0] += 1
                ins.then_inc(dve_chain, 1)
                dve.wait_ge(dve_chain, chain[0])

            dve.wait_ge(const_in, 16 * 9)

            def x_scale(n):
                dve.wait_ge(x_rstd, n + 1)
                dve.tensor_scalar(x_slot[n], x_slot[n], row_rstd[:, n:n + 1], None, ALU.mult).then_inc(x_scaled, 1)

            def x_gain(n):
                dve.wait_ge(x_turned, n + 1)
                g = norm_gain[:, 1 if n < 2 else 0, :].unsqueeze(2).to_broadcast([P, NK, P])
                dve.tensor_tensor(x_slot[n].rearrange("p (k n) -> p k n", n=P),
                                  wide(n).rearrange("p (k n) -> p k n", n=P), g, ALU.mult).then_inc(x_gained, 1)

            for n in range(NX):
                x_scale(n)
                if n >= 1:
                    x_gain(n - 1)
            x_gain(NX - 1)
            link(dve.tensor_scalar(neg_sink[:, :], neg_sink[:, :], -1.0, None, ALU.mult))
            dve.wait_ge(masks_built, 1)
            link(dve.tensor_reduce(parity[:, 1:2], prob[:, 1, 1, 0:64], AX.X, ALU.add))
            link(dve.tensor_scalar(parity[:, 0:1], parity[:, 1:2], -1.0, MASKED, ALU.mult, ALU.add))
            own = masks[:, 3, :].rearrange("p (i h) -> p h i", h=2)
            for h in range(2):
                ins = dve.tensor_scalar(own[:, h, :], own[:, h, :], parity[:, h:h + 1], None, ALU.max)
                if h == 0:
                    link(ins)
            link(ins)

            dve.wait_ge(pos_in, 16 * 4)
            link(dve.tensor_copy(pos_f[:], pos_i[:]))
            freqs = np.exp(np.arange(HALF, dtype=np.float32) * np.float32(-2.0 * math.log(ROPE_THETA) / ROT))
            cosine = angle[:, 0, :].rearrange("p (o f) -> p o f", f=HALF)
            sine = angle[:, 1, :].rearrange("p (o f) -> p o f", f=HALF)
            for f in range(HALF):
                for part in (cosine, sine):
                    ins = dve.tensor_scalar(part[:, :, f], pos_f[:].rearrange("p o t -> p (o t)"), float(freqs[f]), None, ALU.mult)
                    link(ins)
            magic = 1.5 * 2.0 ** 23
            two_pi = 2.0 * math.pi
            part1 = 6.28125
            part2 = 507.0 / 262144.0
            part3 = two_pi - part1 - part2
            link(dve.tensor_scalar(turns[:, 0, :], angle[:, 0, :], 1.0 / two_pi, 0.25, ALU.mult, ALU.add))
            link(dve.tensor_scalar(turns[:, 0, :], turns[:, 0, :], magic, None, ALU.add))
            link(dve.tensor_scalar(turns[:, 1, :], angle[:, 1, :], 1.0 / two_pi, magic, ALU.mult, ALU.add))
            link(dve.tensor_scalar(turns[:, :, :], turns[:, :, :], -magic, None, ALU.add))
            for part in (part1, part2, part3):
                link(dve.scalar_tensor_tensor(out=angle[:, :, :], in0=turns[:, :, :], scalar=-part, in1=angle[:, :, :],
                                              op0=ALU.mult, op1=ALU.add))
            link(dve.tensor_scalar(angle[:, 0, :], angle[:, 0, :], math.pi / 2, None, ALU.add))
            dve.tensor_scalar(angle[:, :, :], angle[:, :, :], 3.1415925, -3.1415925, ALU.min, ALU.max).then_inc(angles_ready, 1)
            dve.wait_ge(sines_ready, 1)
            cos_v = turns[:, 0, :].rearrange("p (o f) -> p o f", f=HALF)
            sin_v = turns[:, 1, :].rearrange("p (o f) -> p o f", f=HALF)
            rc = rope_cos[:].rearrange("p o t f -> p (o t) f")
            rs = rope_sin[:].rearrange("p o t f -> p (o t) f")
            link(dve.tensor_copy(rc[:, :, 0:HALF], cos_v))
            link(dve.tensor_copy(rc[:, :, HALF:ROT], cos_v))
            link(dve.tensor_scalar(rs[:, :, 0:HALF], sin_v, -1.0, None, ALU.mult))
            dve.tensor_copy(rs[:, :, HALF:ROT], sin_v).then_inc(rope_ready, 1)
            dve.wait_ge(rope_ready, 1)

            def normalise(j):
                kind = KIND[j]
                if kind not in QK_KINDS:
                    return
                i = count(QK_KINDS, j)
                nh, dh = {"memk": (4, 128), "A": (8, 64), "B": (10, 64), "M": (4, 128)}[kind]
                dve.wait_ge(sq_done, i + 1)
                if i >= 2:
                    dve.wait_ge(rstd_done, i - 1)
                dve.tensor_reduce(head_ss[:, i % 2, 0:nh], square[:, 0:nh * dh].rearrange("p (h d) -> p h d", d=dh),
                                  AX.X, ALU.add).then_inc(ss_done, 1)
                dve.wait_ge(rstd_done, i + 1)
                if i >= 2:
                    dve.wait_ge(turned, batches(qk_job(i - 1)))
                na = min(nh * dh, 512)
                rstd = head_rstd[:, i % 2, 0:nh].unsqueeze(2).to_broadcast([P, nh, dh])
                buf = qk[:, i % 2, 0:nh * dh].rearrange("p (h d) -> p h d", d=dh)
                ha = na // dh
                if kind == "B":
                    dve.wait_ge(v_done, count(V_KINDS, j + 1))
                    link(dve.tensor_tensor(buf[:, 0:ha, :].rearrange("p (u e) d -> p e u d", e=2),
                                           proj_a(j).rearrange("p (e u d) -> p e u d", e=2, d=dh),
                                           head_rstd[:, i % 2, 0:ha].rearrange("p (e u) -> p e u", e=2).unsqueeze(3)
                                           .to_broadcast([P, 2, 4, dh]), ALU.mult))
                else:
                    ins = dve.tensor_tensor(buf[:, 0:ha, :], proj_a(j).rearrange("p (h d) -> p h d", d=dh), rstd[:, 0:ha, :], ALU.mult)
                if kind == "B":
                    ins = dve.tensor_tensor(buf[:, ha:nh, :], proj_b(j)[:, 0:P].rearrange("p (h d) -> p h d", d=dh),
                                            rstd[:, ha:nh, :], ALU.mult)
                ins.then_inc(normed, 1)

            def qk_job(i):
                return [j for j in range(NJ) if KIND[j] in QK_KINDS][i]

            def copy_k(j):
                kind, t = KIND[j], JOBS[j][1]
                if kind not in HAS_K:
                    return
                dve.wait_ge(turned, batches(j + 1))
                if kind in HAS_Q:
                    dve.wait_ge(q_done, count(HAS_Q, j + 1))
                bank = ps[:, TQ, :].rearrange("p (b n) -> p b n", n=P)
                if kind == "memk":
                    ins = dve.tensor_copy(k_mem[:, :, t * P:(t + 1) * P], bank)
                else:
                    v_wait(dve, j)
                    if kind == "A":
                        ins = dve.tensor_copy(k_ring[:, j % RK, :, :], bank[:, 2:4, :])
                    else:
                        ins = dve.tensor_copy(k_ring[:, j % RK, 0, :], bank[:, 0, :])
                ins.then_inc(k_done, 1)

            def minima(n):
                j, u = UNITS[n]
                kind, (s, t) = KIND[j], JOBS[j]
                order = STAGES[s][1]
                dve.wait_ge(scored, n + 1)
                if n >= 2:
                    dve.wait_ge(prob_turned, n - 1)
                if kind == "M":
                    dve.tensor_reduce(small[:, n % 2, 0:2], scores, AX.X, ALU.min).then_inc(min_done, 1)
                    return
                c0 = 0 if has_prev(j) else P
                mask = (masks[:, 3:4, :] if order == 2 else masks[:, 2:3, :] if c0 else
                        masks[:, 1:3, :] if kind == "A" else masks[:, 0:3:2, :])
                for e in range(2):
                    low, _ = unit_stats(n, e)
                    start = START_MIN if kind == "A" else neg_sink[:, u + 4 * e:u + 4 * e + 1]
                    ins = dve.tensor_tensor_reduce(prob[:, n % 2, e, c0:256].rearrange("p (b n) -> p b n", n=P),
                                                   scores[:, e, c0:256].rearrange("p (b n) -> p b n", n=P), mask, 1.0, start,
                                                   ALU.add, ALU.min, low)
                    if e == 0:
                        link(ins)
                ins.then_inc(min_done, 1)
                if kind == "B":
                    dve.wait_ge(min_done, n + 1)
                    dve.tensor_tensor(small[:, n % 2, 4:6], small[:, n % 2, 0:2], neg_sink[:, u:u + 5:4],
                                      ALU.subtract).then_inc(sink_gap, 1)

            def divide(n):
                j, u = UNITS[n]
                kind = KIND[j]
                if kind == "A":
                    return
                dve.wait_ge(exp_done, n + 1)
                total = small[:, n % 2, 2:4]
                if kind == "B":
                    dve.wait_ge(sink_exp, count_b(n) + 1)
                    link(dve.tensor_tensor(small[:, n % 2, 6:8], total, small[:, n % 2, 4:6], ALU.add))
                    total = small[:, n % 2, 6:8]
                link(dve.reciprocal(small[:, n % 2, 8:10], total))
                c0 = 0 if has_prev(j) else P
                for e in range(2):
                    ins = dve.tensor_scalar(prob[:, n % 2, e, c0:256], prob[:, n % 2, e, c0:256],
                                            small[:, n % 2, 8 + e:9 + e], None, ALU.mult)
                    if e == 0:
                        link(ins)
                ins.then_inc(prob_done, 1)

            def copy_out(n):
                j, u = UNITS[n]
                kind, (s, t) = KIND[j], JOBS[j]
                dve.wait_ge(pv_done, n + 1)
                if kind == "M":
                    dst = attn_out[:, 2 + 2 * u:4 + 2 * u, t * P:(t + 1) * P]
                    src = ps[:, OB, 0:256].rearrange("p (e n) -> p e n", e=2)
                else:
                    base = 2 * STAGES[s][2] if kind == "A" else 6
                    dst = attn_out[:, base + u, t * P:(t + 1) * P]
                    src = ps[:, OB, 0:P]
                dve.tensor_copy(dst, src).then_inc(o_done, 1)

            def merge_factors():
                dve.wait_ge(stats_in, 32)
                lows = [stats[:, g, :, 0:4] for g in range(3)]
                sums = [stats[:, g, :, 4:8] for g in range(3)]
                mx = merge["max"][:].rearrange("p (t h) -> p t h", h=4)
                e = merge["e"][:].rearrange("p (g t h) -> p g t h", g=3, h=4)
                f = merge["f"][:].rearrange("p (g t h) -> p g t h", g=3, h=4)
                total = merge["total"][:].rearrange("p (t h) -> p t h", h=4)
                link(dve.tensor_tensor(mx, lows[0], lows[1], ALU.min))
                link(dve.tensor_tensor(mx, mx, lows[2], ALU.min))
                for g in range(3):
                    ins = dve.tensor_tensor(e[:, g], mx, lows[g], ALU.subtract)
                    if g < 2:
                        link(ins)
                ins.then_inc(shift_ready, 1)
                dve.wait_ge(shift_exp, 1)
                for g in range(3):
                    link(dve.tensor_tensor(f[:, g], e[:, g], sums[g], ALU.mult))
                link(dve.tensor_tensor(total, f[:, 0], f[:, 1], ALU.add))
                link(dve.tensor_tensor(total, total, f[:, 2], ALU.add))
                link(dve.reciprocal(total, total))
                for g in range(3):
                    ins = dve.tensor_tensor(f[:, g], e[:, g], total, ALU.mult)
                    if g < 2:
                        link(ins)
                ins.then_inc(factors_ready, 1)

            def merge_use(m):
                pair, half, g = merge_batch(m)
                dve.wait_ge(factor_turned, m + 1)
                dst = attn_out[:, pair, half * 512:(half + 1) * 512]
                bank = ps[:, TQ, :]
                if g == 0:
                    dve.tensor_tensor(dst, bank, dst, ALU.mult).then_inc(factor_used, 1)
                    dve.wait_ge(factor_used, m + 1)
                    return
                src = attn_out[:, 2 * g + pair, :]
                if g == 1:
                    src = src.rearrange("p (r b i) -> p b i r", r=4, b=2)[:, half]
                    bank, dst = (a.rearrange("p (i r) -> p i r", r=4) for a in (bank, dst))
                else:
                    src = src.rearrange("p (t i) -> p i t", t=8)[:, half * 64:(half + 1) * 64]
                    bank, dst = (a.rearrange("p (i t) -> p i t", t=8) for a in (bank, dst))
                dve.tensor_tensor(src, bank, src, ALU.mult).then_inc(factor_used, 1)
                dve.wait_ge(factor_used, m + 1)
                link(dve.tensor_tensor(dst, dst, src, ALU.add))

            n = 0
            for j in range(NJ + LAG + 1):
                if 0 <= j - 1 < NJ:
                    normalise(j - 1)
                for k in range(8):
                    if k in step_slices(j):
                        minima(n)
                        divide(n)
                        if n >= 2:
                            copy_out(n - 2)
                        n += 1
                    if k == 7 and 0 <= j - 1 < NJ:
                        copy_k(j - 1)
                if j == merge_from:
                    merge_factors()
                for m in merge_at.get(j, ()):
                    merge_use(m)
            copy_out(NU - 2)
            copy_out(NU - 1)

        @block.tensor
        def _(pe):
            pe.wait_ge(ident_ready, 1)
            for n in range(NX):
                pe.wait_ge(x_scaled, n + 1)
                if n >= 2:
                    pe.wait_ge(x_gained, n - 1)
                for k in range(NK):
                    ins = pe.transpose(wide(n)[:, k * P:(k + 1) * P], x_slot[n][:, k * P:(k + 1) * P], ident[:])
                ins.then_inc(x_turned, 1)

            def project(j, k):
                s, t = JOBS[j]
                kind, order, _, _, na, nb, tiles = STAGES[s]
                n = 8 * s + k
                if k == 0:
                    if kind in ("memk", "memv"):
                        pe.wait_ge(x_lo, 2)
                    elif s == 2:
                        pe.wait_ge(x_lo, 3 + t)
                    if j >= 2:
                        if count(QK_KINDS, j - 1):
                            pe.wait_ge(sq_done, count(QK_KINDS, j - 1))
                            pe.wait_ge(normed, count(QK_KINDS, j - 1))
                        if count(V_KINDS, j - 1):
                            pe.wait_ge(v_done, count(V_KINDS, j - 1))
                    else:
                        pe.wait_ge(x_gained, NX)
                if t == 0:
                    pe.wait_ge(w_lo_done, n + 1)
                if kind in ("memk", "memv"):
                    hi, lo = (m[:, k, t * P:(t + 1) * P] for m in (mem_hi, mem_lo))
                else:
                    hi, lo = (token_tile(m[:, k, :], order, t) for m in (act_hi, act_lo))
                for i, (lhs, w) in enumerate(((hi, w_hi), (hi, w_lo), (lo, w_hi))):
                    ins = pe.matmul(proj_a(j)[:, 0:na], lhs, w[:, k, 0:na], start=(k == 0 and i == 0), stop=(k == 7 and i == 2))
                    if nb:
                        ins = pe.matmul(proj_b(j), lhs, w[:, k, na:na + nb], start=(k == 0 and i == 0), stop=(k == 7 and i == 2))
                if t == tiles - 1:
                    ins.then_inc(w_used, 1)
                    if k == 7:
                        pe.wait_ge(w_used, n + 1)
                        pe.nop().then_inc(proj_done, 1)
                elif k == 7:
                    ins.then_inc(proj_done, 1)

            def turn(j, batch):
                kind = KIND[j]
                if batch >= BATCHES[kind]:
                    return
                i = count(QK_KINDS, j)
                pe.wait_ge(roped, i + 1)
                bank_free(j, batch)
                bank = ps[:, TQ, :].rearrange("p (b n) -> p b n", n=P)
                buf = qk[:, i % 2, :]
                if kind == "B" and batch == 1:
                    ins = pe.transpose(bank[:, 0, :], buf[:, 512:640], ident[:])
                else:
                    for b in range(4):
                        ins = pe.transpose(bank[:, b, :], buf[:, b * P:(b + 1) * P], ident[:])
                ins.then_inc(turned, 1)

            def bank_free(j, batch):
                q = count(HAS_Q, j + (1 if batch else 0))
                k = count(HAS_K, j)
                if q:
                    pe.wait_ge(q_done, q)
                if k:
                    pe.wait_ge(k_done, k)
                used = sum(len(v) for jj, v in merge_at.items() if jj < j + 1)
                if used:
                    pe.wait_ge(factor_used, used)

            def score(n):
                j, u = UNITS[n]
                kind = KIND[j]
                if kind != "M" or u == 0:
                    pe.wait_ge(q_done, count(HAS_Q, j) + 1)
                    pe.wait_ge(k_done, count(HAS_K, j) + (kind != "M"))
                if n >= 1:
                    if KIND[UNITS[n - 1][0]] == "M":
                        pe.wait_ge(exp_done, n)
                    else:
                        pe.wait_ge(min_done, n)
                for e in range(2):
                    if kind == "M":
                        h = 2 * u + e
                        ins = pe.matmul(scores[:, e, :], q_ring[:, j % RQ, h, :], k_mem[:, h, :], start=True, stop=True)
                        continue
                    if e == 1:
                        pe.wait_ge(first_scored, count_ab(n) + 1)
                    rows = slice(64 * e, 64 * e + 64)
                    q = q_ring[rows, j % RQ, u, :]
                    kk = u if kind == "A" else 0
                    if has_prev(j):
                        pe.matmul(scores[:, e, 0:P], q, k_ring[rows, (j - 1) % RK, kk, :], start=True, stop=True)
                    ins = pe.matmul(scores[:, e, P:256], q, k_ring[rows, j % RK, kk, :], start=True, stop=True)
                    if e == 0:
                        ins.then_inc(first_scored, 1)
                ins.then_inc(scored, 1)

            def turn_probs(n):
                j = UNITS[n][0]
                if KIND[j] == "A":
                    pe.wait_ge(exp_done, n + 1)
                else:
                    pe.wait_ge(prob_done, count_bm(n) + 1)
                if n >= 1:
                    pe.wait_ge(prob_copied, n)
                for e in range(2):
                    for b in range(0 if has_prev(j) else 1, 2):
                        ins = pe.transpose(prob_turn[:, e, b, :], prob[:, n % 2, e, b * P:(b + 1) * P], ident[:])
                ins.then_inc(prob_turned, 1)

            def weigh_values(n):
                j, u = UNITS[n]
                kind = KIND[j]
                pe.wait_ge(prob_copied, n + 1)
                if n >= 1:
                    pe.wait_ge(o_done, n)
                if kind != "M":
                    pe.wait_ge(v_done, count(V_KINDS, j + 1))
                first = 0 if has_prev(j) else 1
                for e in range(2):
                    for b in range(first, 2):
                        if kind == "M":
                            h = 2 * u + e
                            v = v_mem[:, b, h * P:(h + 1) * P]
                            dst = ps[:, OB, e * P:(e + 1) * P]
                        else:
                            c = 64 * (2 * u + e if kind == "A" else e)
                            v = v_ring[:, (j - 1 + b) % RK, c:c + 64]
                            dst = ps[64 * e:64 * e + 64, OB, 0:P]
                        ins = pe.matmul(dst, v, prob_t[:, n % 2, e, b, :], start=(b == first), stop=(b == 1))
                ins.then_inc(pv_done, 1)

            def turn_factors(m, j):
                pair, half, g = merge_batch(m)
                pe.wait_ge(q_done, count(HAS_Q, j))
                pe.wait_ge(k_done, count(HAS_K, j))
                if m:
                    pe.wait_ge(factor_used, m)
                pe.wait_ge(spread_done, m + 1)
                for i in range(4):
                    ins = pe.transpose(ps[:, TQ, i * P:(i + 1) * P], square[:, i * P:(i + 1) * P], ident[:])
                ins.then_inc(factor_turned, 1)

            n = 0
            for j in range(NJ + LAG + 1):
                for k in range(8):
                    if j < NJ:
                        project(j, k)
                    if k in step_slices(j):
                        score(n)
                        if n >= 1:
                            turn_probs(n - 1)
                        if n >= 2:
                            weigh_values(n - 2)
                        n += 1
                    if k == 5 and 0 <= j - 1 < NJ:
                        turn(j - 1, 0)
                    if k == 7 and 0 <= j - 1 < NJ:
                        turn(j - 1, 1)
                for m in merge_at.get(j, ()):
                    turn_factors(m, j)
            turn_probs(NU - 1)
            weigh_values(NU - 2)
            weigh_values(NU - 1)


def gated_outputs(nc, w_gate, b_gate, w_o_a, w_o_b, w_o_m, ps, act_hi, act_lo, attn_out, merged):
    NK = act_hi.shape[1]
    BR = 3
    BRANCH_TILES = [(0, 2), (6, 4), (2, 4)]
    O_SLOT = [0, 2, 6]
    UN = 2 * BR
    with ExitStack() as ctx:
        def sb(name, shape, dt=F32):
            return ctx.enter_context(nc.sbuf_tensor(name, shape, dt))

        def sem(name):
            return ctx.enter_context(nc.semaphore(name))

        g_raw = sb("g_raw", [P, BR, NK, P])
        g_hi = sb("g_hi", [P, BR, NK, P], F32R)
        g_lo = sb("g_lo", [P, BR, NK, P], F32R)
        o_raw = sb("o_raw", [P, 10, P])
        o_w = sb("o_w", [P, 10, P])
        bias = sb("gate_bias", [P, 2 * BR * NK])
        gate = sb("gate", [P, 2, 512])
        g_in = [sem(f"g_in{b}") for b in range(BR)]
        g_hi_done = [sem(f"g_hi_done{b}") for b in range(BR)]
        g_lo_done = [sem(f"g_lo_done{b}") for b in range(BR)]
        g_used = [sem(f"g_used{b}") for b in range(BR)]
        o_in, o_copied, bias_in = sem("o_in"), sem("o_copied"), sem("bias_in")
        gate_summed, out_summed, gate_done, weighed, added = (
            sem(n) for n in ("gate_summed", "out_summed", "gate_done", "weighed", "added"))
        block = ctx.enter_context(nc.Block())

        @block.sync
        def _(sp):
            with nc.allow_non_contiguous_dma(reason="one bias per partition"):
                for half in range(2):
                    sp.dma_start(bias[:, half * BR * NK:(half + 1) * BR * NK], b_gate[0].rearrange("(k p) -> p k", p=P)
                                 ).then_inc(bias_in, 16)

            def load_tile(f):
                cols = bass.ds(f * P, P)
                for b in range(BR):
                    sp.wait_ge(g_lo_done[b], f)
                    sp.dma_start(g_raw[:, b], w_gate[0].rearrange("(k p) n -> p k n", p=P)[:, :, bass.ds(f * P + b * NK * P, P)]
                                 ).then_inc(g_in[b], 16)
                sp.wait_ge(o_copied, f)
                sp.dma_start(o_raw[:, 0:2], w_o_a[0].rearrange("(k p) n -> p k n", p=P)[:, :, cols]).then_inc(o_in, 16)
                for e in range(2):
                    sp.dma_start(o_raw[64 * e:64 * e + 64, 2:6],
                                 w_o_b[0].rearrange("(e j d) n -> e d j n", e=2, d=64)[e][:, :, cols]).then_inc(o_in, 16)
                sp.dma_start(o_raw[:, 6:10], w_o_m[0].rearrange("(k p) n -> p k n", p=P)[:, :, cols]).then_inc(o_in, 16)

            load_tile(0)
            with sp.Fori(1, NK) as f:
                load_tile(f)

        @block.scalar
        def _(act):
            def cast(f, b):
                act.wait_ge(g_in[b], 16 * (f + 1))
                act.wait_ge(g_used[b], f)
                act.activation(g_hi[:, b], g_raw[:, b], ACT.Copy).then_inc(g_hi_done[b], 1)

            def copy_weights(f):
                act.wait_ge(o_in, 64 * (f + 1))
                act.wait_ge(out_summed, UN * f)
                act.activation(o_w[:], o_raw[:], ACT.Copy).then_inc(o_copied, 1)

            def tile(f, first, last):
                for b in range(BR):
                    for half in range(2):
                        u = 2 * b + half
                        act.wait_ge(gate_summed, UN * f + u + 1)
                        if not first or u >= 2:
                            act.wait_ge(added, UN * f + u - 1)
                        column = f + (half * BR + b) * NK
                        column = column if isinstance(f, int) else act.snap(column)
                        act.activation(gate[:, u % 2, :], ps[:, 2 * (u % 3), :], ACT.Sigmoid,
                                       bias=bias[:, bass.ds(column, 1)]).then_inc(gate_done, 1)
                    if not last:
                        cast(f + 1, b)
                if not last:
                    copy_weights(f + 1)

            for b in range(BR):
                cast(0, b)
            copy_weights(0)
            act.wait_ge(bias_in, 32)
            tile(0, True, False)
            with act.Fori(1, NK - 1) as f:
                tile(f, False, False)
            tile(NK - 1, False, True)

        @block.gpsimd
        def _(pool):
            with pool.Fori(0, NK) as f:
                for b in range(BR):
                    pool.wait_ge(g_hi_done[b], f + 1)
                    pool.tensor_tensor(g_lo[:, b], g_raw[:, b], g_hi[:, b].bitcast(F32), ALU.subtract).then_inc(g_lo_done[b], 1)

        @block.vector
        def _(dve):
            def tile(f, first):
                for u in range(UN):
                    b, half = u // 2, u % 2
                    at = UN * f + u
                    dve.wait_ge(gate_done, at + 1)
                    dve.wait_ge(out_summed, at + 1)
                    dve.tensor_tensor(gate[:, u % 2, :], ps[:, 2 * (u % 3) + 1, :], gate[:, u % 2, :], ALU.mult).then_inc(weighed, 1)
                    dve.wait_ge(weighed, at + 1)
                    dst = merged[:, bass.ds(f, 1), half * 512:(half + 1) * 512]
                    src = gate[:, u % 2:u % 2 + 1, :]
                    if b == 0:
                        dve.tensor_copy(dst, src).then_inc(added, 1)
                    else:
                        dve.wait_ge(added, at - 1)
                        dve.tensor_tensor(dst, dst, src, ALU.add).then_inc(added, 1)

            with dve.Fori(0, NK) as f:
                tile(f, False)

        @block.tensor
        def _(pe):
            def tile(f, first):
                for u in range(UN):
                    b, half = u // 2, u % 2
                    at = UN * f + u
                    cols = slice(half * 512, (half + 1) * 512)
                    if half == 0:
                        pe.wait_ge(g_lo_done[b], f + 1)
                    if not first or u >= 3:
                        pe.wait_ge(weighed, at - 2)
                    for k in range(NK):
                        for i, (w, a) in enumerate(((g_hi, act_hi), (g_hi, act_lo), (g_lo, act_hi))):
                            ins = pe.matmul(ps[:, 2 * (u % 3), :], w[:, b, k, :], a[:, k, cols],
                                            start=(k == 0 and i == 0), stop=(k == NK - 1 and i == 2))
                    ins.then_inc(gate_summed, 1)
                    if half == 1:
                        pe.wait_ge(gate_summed, at + 1)
                        pe.nop().then_inc(g_used[b], 1)
                    if u == 0:
                        pe.wait_ge(o_copied, f + 1)
                    t0, tiles = BRANCH_TILES[b]
                    for i in range(tiles):
                        ins = pe.matmul(ps[:, 2 * (u % 3) + 1, :], o_w[:, O_SLOT[b] + i, :], attn_out[:, t0 + i, cols],
                                        start=(i == 0), stop=(i == tiles - 1))
                    ins.then_inc(out_summed, 1)

            tile(0, True)
            with pe.Fori(1, NK) as f:
                tile(f, False)


def output_projection(nc, x_t, w_out, ffn_norm, ps, act_hi, act_lo, ident, half_power, merged, x1):
    NT, NK, D = x1.shape[1], act_hi.shape[1], x1.shape[2]
    NRAW_O = 3
    with ExitStack() as ctx:
        def sb(name, shape, dt=F32):
            return ctx.enter_context(nc.sbuf_tensor(name, shape, dt))

        def sem(name):
            return ctx.enter_context(nc.semaphore(name))

        wo_hi = sb("wo_hi", [P, 2, NK, 512], F32R)
        wo_lo = sb("wo_lo", [P, 2, NK, 512], F32R)
        wo_raw = sb("wo_raw", [P, NRAW_O, 512])
        gain = sb("ffn_gain", [P, NK])
        sums = sb("x1_sums", [P, NT])
        rstd = sb("x1_rstd", [P, NT])
        wo_in = [sem(f"wo_in{n}") for n in range(NRAW_O)]
        res_in = [sem(f"res_in{t}") for t in range(NT)]
        gain_in, wo_hi_done, wo_lo_done, m_hi, m_lo = (sem(n) for n in ("gain_in", "wo_hi_done", "wo_lo_done", "m_hi", "m_lo"))
        out_done, x1_done, x1_sq, x1_ms, x1_rs, x1_scaled, x1_turned, x1_gained, h_hi, h_lo = (
            sem(n) for n in ("out_done", "x1_done", "x1_sq", "x1_ms", "x1_rs", "x1_scaled", "x1_turned", "x1_gained", "h_hi", "h_lo"))
        NS = 2 * NK

        def turned(t):
            return ps[:, 4 + 2 * (t % 2):6 + 2 * (t % 2), :].rearrange("p b n -> p (b n)")

        block = ctx.enter_context(nc.Block())

        @block.sync
        def _(sp):
            for n in range(NS):
                half, k = n // NK, n % NK
                if n >= NRAW_O:
                    sp.wait_ge(wo_lo_done, n - NRAW_O + 1)
                sp.dma_start(wo_raw[:, n % NRAW_O, :], w_out[0, k * P:(k + 1) * P, half * 512:(half + 1) * 512]
                             ).then_inc(wo_in[n % NRAW_O], 16)
                if half:
                    sp.dma_start(x1[:, k, :], x_t[k]).then_inc(res_in[k], 16)
            with nc.allow_non_contiguous_dma(reason="one gain per partition"):
                sp.dma_start(gain[:, :], ffn_norm[0].rearrange("(k p) -> p k", p=P)).then_inc(gain_in, 16)

        @block.scalar
        def _(act):
            for n in range(NS):
                if n < NK:
                    act.activation(act_hi[:, n, :], merged[:, n, :], ACT.Copy).then_inc(m_hi, 1)
                act.wait_ge(wo_in[n % NRAW_O], 16 * (n // NRAW_O + 1))
                act.activation(wo_hi[:, n // NK, n % NK, :], wo_raw[:, n % NRAW_O, :], ACT.Copy).then_inc(wo_hi_done, 1)

            def high(t):
                act.wait_ge(x1_gained, t + 1)
                act.activation(act_hi[:, :, t * P:(t + 1) * P], merged[:, t, :].rearrange("p (k n) -> p k n", n=P),
                               ACT.Copy).then_inc(h_hi, 1)

            for t in range(NT):
                if t == 0:
                    act.wait_ge(m_lo, NK)
                act.wait_ge(x1_done, 2 * (t + 1))
                act.activation(merged[:, t, :], x1[:, t, :], ACT.Square, accum_out=sums[:, t:t + 1]).then_inc(x1_sq, 1)
                if t >= 1:
                    high(t - 1)
            high(NT - 1)

        @block.gpsimd
        def _(pool):
            for n in range(NS):
                if n < NK:
                    pool.wait_ge(m_hi, n + 1)
                    pool.tensor_tensor(act_lo[:, n, :], merged[:, n, :], act_hi[:, n, :].bitcast(F32), ALU.subtract).then_inc(m_lo, 1)
                pool.wait_ge(wo_hi_done, n + 1)
                pool.tensor_tensor(wo_lo[:, n // NK, n % NK, :], wo_raw[:, n % NRAW_O, :],
                                   wo_hi[:, n // NK, n % NK, :].bitcast(F32), ALU.subtract).then_inc(wo_lo_done, 1)

            def low(t):
                pool.wait_ge(h_hi, t + 1)
                pool.tensor_tensor(act_lo[:, :, t * P:(t + 1) * P], merged[:, t, :].rearrange("p (k n) -> p k n", n=P),
                                   act_hi[:, :, t * P:(t + 1) * P].bitcast(F32), ALU.subtract).then_inc(h_lo, 1)

            for t in range(NT):
                pool.wait_ge(x1_sq, t + 1)
                pool.tensor_scalar(rstd[:, t:t + 1], sums[:, t:t + 1], 1.0 / D, EPS, ALU.mult, ALU.add).then_inc(x1_ms, 1)
                pool.wait_ge(x1_ms, t + 1)
                pool.tensor_tensor(rstd[:, t:t + 1], rstd[:, t:t + 1], half_power[:, 0:1], ALU.pow).then_inc(x1_rs, 1)
                if t >= 1:
                    low(t - 1)
            low(NT - 1)

        @block.vector
        def _(dve):
            def gained(t):
                dve.wait_ge(x1_turned, t + 1)
                dve.tensor_tensor(merged[:, t, :].rearrange("p (k n) -> p k n", n=P),
                                  turned(t).rearrange("p (k n) -> p k n", n=P),
                                  gain[:].unsqueeze(2).to_broadcast([P, NK, P]), ALU.mult).then_inc(x1_gained, 1)

            dve.wait_ge(gain_in, 16)
            for t in range(NT):
                dve.wait_ge(res_in[t], 16)
                for half in range(2):
                    n = 2 * t + half
                    dve.wait_ge(out_done, n + 1)
                    dst = x1[:, t, half * 512:(half + 1) * 512]
                    dve.tensor_tensor(dst, ps[:, n % 4, :], dst, ALU.add).then_inc(x1_done, 1)
                if t >= 1:
                    gained(t - 1)
                dve.wait_ge(x1_rs, t + 1)
                dve.tensor_scalar(merged[:, t, :], x1[:, t, :], rstd[:, t:t + 1], None, ALU.mult).then_inc(x1_scaled, 1)
            gained(NT - 1)

        @block.tensor
        def _(pe):
            def turn(t):
                pe.wait_ge(x1_scaled, t + 1)
                if t >= 2:
                    pe.wait_ge(x1_gained, t - 1)
                for k in range(NK):
                    ins = pe.transpose(turned(t)[:, k * P:(k + 1) * P], merged[:, t, k * P:(k + 1) * P], ident[:])
                ins.then_inc(x1_turned, 1)

            for t in range(NT):
                for half in range(2):
                    n = 2 * t + half
                    if n >= 4:
                        pe.wait_ge(x1_done, n - 3)
                    for k in range(NK):
                        if t == 0:
                            if half == 0:
                                pe.wait_ge(m_lo, k + 1)
                            pe.wait_ge(wo_lo_done, NK * half + k + 1)
                        for i, (a, w) in enumerate(((act_hi, wo_hi), (act_hi, wo_lo), (act_lo, wo_hi))):
                            ins = pe.matmul(ps[:, n % 4, :], a[:, k, t * P:(t + 1) * P], w[:, half, k, :],
                                            start=(k == 0 and i == 0), stop=(k == NK - 1 and i == 2))
                    ins.then_inc(out_done, 1)
                if t >= 1:
                    turn(t - 1)
            turn(NT - 1)


def feed_forward(nc, w_up, conv_w, conv_b, w_down, out_t, ps, act_hi, act_lo, ident, x1, spare):
    NK, S, NT = act_hi.shape[1], act_hi.shape[2], x1.shape[1]
    FF = w_down.shape[1]
    FT = FF // P
    NC = FT // 2
    YN = 2 * NT
    with ExitStack() as ctx:
        def sb(name, shape, dt=F32):
            return ctx.enter_context(nc.sbuf_tensor(name, shape, dt))

        def sem(name):
            return ctx.enter_context(nc.semaphore(name))

        f_raw = sb("f_raw", [P, 6, 1024])
        f_hi = sb("f_hi", [P, 6, 1024], F32R)
        f_lo = sb("f_lo", [P, 6, 1024], F32R)
        z_hi = sb("z_hi", [P, 2, S], F32R)
        z_lo = sb("z_lo", [P, 2, S], F32R)
        conv0 = sb("conv0", [P, 2, S])
        conv = [conv0[:, :, :], spare]
        taps = sb("taps", [P, 4, 2 * FT])
        taps_raw = conv0[0:2 * FT, 0, 0:4 * P].rearrange("p (j n) -> p j n", j=4)

        taps_in, taps_turned, taps_ready = sem("taps_in"), sem("taps_turned"), sem("taps_ready")
        f_in = [sem(f"f_in{b}") for b in range(6)]
        f_hi_done = [sem(f"f_hi_done{b}") for b in range(6)]
        f_lo_done = [sem(f"f_lo_done{b}") for b in range(6)]
        u_done = [sem(f"u_done{q}") for q in range(4)]
        tap2_done = [sem(f"tap2_done{q}") for q in range(4)]
        tap1_done = [sem(f"tap1_done{q}") for q in range(4)]
        tap0_done = [sem(f"tap0_done{q}") for q in range(4)]
        silu_done = [sem(f"silu_done{p}") for p in range(2)]
        z_done = [sem(f"z_done{p}") for p in range(2)]
        z_hi_done = [sem(f"z_hi_done{p}") for p in range(2)]
        z_lo_done = [sem(f"z_lo_done{p}") for p in range(2)]
        y_done, y_added, stored = sem("y_done"), sem("y_added"), sem("stored")

        def up_psum(q):
            return ps[:, 2 * q:2 * q + 2, :].rearrange("p b n -> p (b n)")

        block = ctx.enter_context(nc.Block())

        @block.sync
        def _(sp):
            for j in range(3):
                sp.dma_start(taps_raw[:, j, :], conv_w[0, j].rearrange("(t n) -> t n", n=P)).then_inc(taps_in, 16)
            sp.dma_start(taps_raw[:, 3, :], conv_b[0].rearrange("(t n) -> t n", n=P)).then_inc(taps_in, 16)

            def load(b, c):
                sp.wait_ge(f_lo_done[b], c)
                if b < 4:
                    col = (2 * c + b // 2) * P + (b % 2) * FF
                    sp.dma_start(f_raw[:, b, :].rearrange("p (k n) -> p k n", n=P),
                                 w_up[0].rearrange("(k p) n -> p k n", p=P)[:, :, bass.ds(col, P)]).then_inc(f_in[b], 16)
                else:
                    sp.dma_start(f_raw[:, b, :], w_down[0, bass.ds((2 * c + b - 4) * P, P), :]).then_inc(f_in[b], 16)

            def chunk(c, down, more):
                if down:
                    load(4, c - 1)
                    load(5, c - 1)
                load(2, c)
                load(3, c)
                if more:
                    load(0, c + 1)
                    load(1, c + 1)

            load(0, 0)
            load(1, 0)
            chunk(0, False, True)
            chunk(1, True, True)
            with sp.Fori(2, NC - 1) as c:
                chunk(c, True, True)
            chunk(NC - 1, True, False)
            load(4, NC - 1)
            load(5, NC - 1)
            for t in range(NT):
                sp.wait_ge(y_added, YN * (NC - 1) + 2 * t + 2)
                sp.dma_start(out_t[t], x1[:, t, :]).then_inc(stored, 16)
            sp.wait_ge(stored, 16 * NT)

        @block.gpsimd
        def _(pool):
            def low(b, c):
                pool.wait_ge(f_hi_done[b], c + 1)
                pool.tensor_tensor(f_lo[:, b, :], f_raw[:, b, :], f_hi[:, b, :].bitcast(F32), ALU.subtract).then_inc(f_lo_done[b], 1)

            def z_low(p, c):
                pool.wait_ge(z_hi_done[p], c + 1)
                pool.tensor_tensor(z_lo[:, p, :], conv[p][:, 0, :], z_hi[:, p, :].bitcast(F32), ALU.subtract).then_inc(z_lo_done[p], 1)

            def chunk(c, down, more):
                if down:
                    z_low(1, c - 1)
                    low(4, c - 1)
                    low(5, c - 1)
                low(2, c)
                low(3, c)
                if more:
                    low(0, c + 1)
                    low(1, c + 1)
                z_low(0, c)

            low(0, 0)
            low(1, 0)
            chunk(0, False, True)
            with pool.Fori(1, NC - 1) as c:
                chunk(c, True, True)
            chunk(NC - 1, True, False)
            z_low(1, NC - 1)
            low(4, NC - 1)
            low(5, NC - 1)

        @block.scalar
        def _(act):
            def high(b, c):
                act.wait_ge(f_in[b], 16 * (c + 1))
                if b < 4:
                    act.wait_ge(u_done[b], c)
                else:
                    act.wait_ge(y_done, YN * c)
                act.activation(f_hi[:, b, :], f_raw[:, b, :], ACT.Copy).then_inc(f_hi_done[b], 1)

            def own_tap(p, c):
                for e in range(2):
                    q = 2 * p + e
                    act.wait_ge(u_done[q], c + 1)
                    if e == 0:
                        act.wait_ge(z_lo_done[p], c)
                    feature = 2 * c + p + e * FT if isinstance(c, int) else act.snap(2 * c + p + e * FT)
                    act.activation(conv[p][:, e, :], up_psum(q), ACT.Identity, scale=taps[:, 2, bass.ds(feature, 1)],
                                   bias=taps[:, 3, bass.ds(feature, 1)]).then_inc(tap2_done[q], 1)
                act.wait_ge(tap0_done[2 * p], c + 1)
                act.activation(conv[p][:, 0, :], conv[p][:, 0, :], ACT.Silu).then_inc(silu_done[p], 1)

            def z_high(p, c):
                act.wait_ge(z_done[p], c + 1)
                act.wait_ge(y_done, YN * c)
                act.activation(z_hi[:, p, :], conv[p][:, 0, :], ACT.Copy).then_inc(z_hi_done[p], 1)

            def chunk(c, down, more):
                if down:
                    own_tap(1, c - 1)
                    z_high(1, c - 1)
                    high(4, c - 1)
                    high(5, c - 1)
                high(2, c)
                high(3, c)
                own_tap(0, c)
                if more:
                    high(0, c + 1)
                    high(1, c + 1)
                z_high(0, c)

            high(0, 0)
            high(1, 0)
            act.wait_ge(taps_turned, 1)
            act.activation(taps[:].rearrange("p j n -> p (j n)"), ps[:, 7, 0:8 * FT], ACT.Copy).then_inc(taps_ready, 1)
            act.wait_ge(taps_ready, 1)
            chunk(0, False, True)
            chunk(1, True, True)
            with act.Fori(2, NC - 1) as c:
                chunk(c, True, True)
            chunk(NC - 1, True, False)
            own_tap(1, NC - 1)
            z_high(1, NC - 1)
            high(4, NC - 1)
            high(5, NC - 1)

        @block.vector
        def _(dve):
            def other_taps(q, c):
                p, e = q // 2, q % 2
                dst = conv[p][:, e, :]
                feature = 2 * c + p + e * FT
                dve.wait_ge(tap2_done[q], c + 1)
                dve.scalar_tensor_tensor(out=dst[:, 1:S], in0=up_psum(q)[:, 0:S - 1], scalar=taps[:, 1, bass.ds(feature, 1)],
                                         in1=dst[:, 1:S], op0=ALU.mult, op1=ALU.add).then_inc(tap1_done[q], 1)
                dve.wait_ge(tap1_done[q], c + 1)
                dve.scalar_tensor_tensor(out=dst[:, 2:S], in0=up_psum(q)[:, 0:S - 2], scalar=taps[:, 0, bass.ds(feature, 1)],
                                         in1=dst[:, 2:S], op0=ALU.mult, op1=ALU.add).then_inc(tap0_done[q], 1)

            def product(p, c):
                dve.wait_ge(silu_done[p], c + 1)
                dve.wait_ge(tap0_done[2 * p + 1], c + 1)
                dve.tensor_tensor(conv[p][:, 0, :], conv[p][:, 0, :], conv[p][:, 1, :], ALU.mult).then_inc(z_done[p], 1)

            def add(i, c):
                dst = x1[:, i // 2, (i % 2) * 512:(i % 2 + 1) * 512]
                dve.wait_ge(y_done, YN * c + i + 1)
                dve.tensor_tensor(dst, ps[:, 4 + i % 4, :], dst, ALU.add).then_inc(y_added, 1)

            def chunk(c, down):
                if down:
                    other_taps(2, c - 1)
                    other_taps(3, c - 1)
                    product(1, c - 1)
                other_taps(0, c)
                if down:
                    add(0, c - 1)
                other_taps(1, c)
                if down:
                    for i in range(1, 4):
                        add(i, c - 1)
                product(0, c)
                if down:
                    for i in range(4, YN):
                        add(i, c - 1)
                    dve.wait_ge(y_added, YN * c)

            chunk(0, False)
            chunk(1, True)
            with dve.Fori(2, NC) as c:
                chunk(c, True)
            other_taps(2, NC - 1)
            other_taps(3, NC - 1)
            product(1, NC - 1)
            for i in range(YN):
                add(i, NC - 1)

        @block.tensor
        def _(pe):
            def up(q, c, first):
                pe.wait_ge(f_lo_done[q], c + 1)
                if q < 2:
                    pe.wait_ge(tap0_done[q], c)
                elif not first and q == 2:
                    pe.wait_ge(y_added, YN * c)
                for half in range(2):
                    for k in range(NK):
                        for i, (w, a) in enumerate(((f_hi, act_hi), (f_hi, act_lo), (f_lo, act_hi))):
                            ins = pe.matmul(ps[:, 2 * q + half, :], w[:, q, k * P:(k + 1) * P],
                                            a[:, k, half * 512:(half + 1) * 512],
                                            start=(k == 0 and i == 0), stop=(k == NK - 1 and i == 2))
                ins.then_inc(u_done[q], 1)

            def down(c):
                for p in range(2):
                    pe.wait_ge(z_lo_done[p], c + 1)
                    pe.wait_ge(f_lo_done[4 + p], c + 1)
                    pe.wait_ge(tap0_done[2 + p], c + 1)
                for i in range(YN):
                    t, half = i // 2, i % 2
                    if i >= 4:
                        pe.wait_ge(y_added, YN * c + i - 3)
                    for p in range(2):
                        for m, (z, w) in enumerate(((z_hi, f_hi), (z_hi, f_lo), (z_lo, f_hi))):
                            ins = pe.matmul(ps[:, 4 + i % 4, :], z[:, p, t * P:(t + 1) * P],
                                            w[:, 4 + p, half * 512:(half + 1) * 512],
                                            start=(p == 0 and m == 0), stop=(p == 1 and m == 2))
                    ins.then_inc(y_done, 1)

            pe.wait_ge(taps_in, 64)
            for j in range(4):
                ins = pe.transpose(ps[:, 7, j * 2 * FT:(j + 1) * 2 * FT], taps_raw[:, j, :], ident[0:2 * FT, 0:2 * FT])
            ins.then_inc(taps_turned, 1)
            up(0, 0, True)
            up(1, 0, True)
            pe.wait_ge(taps_ready, 1)
            up(2, 0, True)
            up(3, 0, True)
            with pe.Fori(1, NC) as c:
                up(0, c, False)
                up(1, c, False)
                down(c - 1)
                up(2, c, False)
                up(3, c, False)
            down(NC - 1)


_INS = ['x', 'mem', 'positions', 'attn_norm', 'w_in', 'a_q_norm', 'a_k_norm', 'b_q_norm', 'b_k_norm', 'b_sinks',
        'mem_norm', 'w_mem_kv', 'm_q_norm', 'm_k_norm', 'w_o_a', 'w_o_b', 'w_o_m', 'w_gate', 'b_gate', 'w_out',
        'ffn_norm', 'w_up', 'conv_w', 'conv_b', 'w_down']
_OUTS = [((1, 1024, 1024), 'float32')]


def kernel(**inputs):
    import numpy as _np
    import concourse.bacc as _bacc
    from concourse import mybir as _mybir
    from concourse.bass_utils import run_bass_kernel_spmd as _run

    nc = _bacc.Bacc("TRN2", target_bir_lowering=False, num_devices=1)
    arrays, args = {}, []
    for name in _INS:
        a = _np.ascontiguousarray(inputs[name])
        arrays[f"in_{name}_dram"] = a
        args.append(nc.dram_tensor(f"in_{name}_dram", a.shape, _mybir.dt.from_np(a.dtype), kind="ExternalInput").ap())
    for i, (shape, dtype) in enumerate(_OUTS):
        dt = _mybir.dt.from_np(_np.dtype(dtype))
        args.append(nc.dram_tensor(f"out_{i}_dram", shape, dt, kind="ExternalOutput").ap())
    layer(nc, *args)
    r = _run(nc, [arrays], core_ids=[0])
    return r.results[0]["out_0_dram"]
```

```python
import math
from contextlib import ExitStack

import concourse.bass as bass
import numpy as np
from concourse import mybir

F32 = mybir.dt.float32
F32R = mybir.dt.float32r
I32 = mybir.dt.int32
ALU = mybir.AluOpType
ACT = mybir.ActivationFunctionType
AX = mybir.AxisListType

P = 128
EPS = 1e-6
MASKED = 1e30
START_MIN = 3e38
ROPE_THETA = 500000.0
ROT = 16
HALF = ROT // 2

STAGES = [
    ("memk", 0, 0, 0, 512, 0, 2),
    ("memv", 0, 0, 512, 512, 0, 2),
    ("A", 0, 0, 0, 512, 256, 8),
    ("A", 1, 1, 768, 512, 256, 8),
    ("A", 2, 2, 1536, 512, 256, 8),
    ("B", 0, 0, 2304, 512, 256, 8),
    ("M", 0, 0, 3072, 512, 0, 8),
]
JOBS = [(s, t) for s, st in enumerate(STAGES) for t in range(st[6])]
KIND = [STAGES[s][0] for s, _ in JOBS]
NJ = len(JOBS)
UNITS_OF = {"memk": 0, "memv": 0, "A": 2, "B": 4, "M": 2}
UNITS = [(j, u) for j in range(NJ) for u in range(UNITS_OF[KIND[j]])]
NU = len(UNITS)
LAG = 2
RQ, RK = 3, 4
BATCHES = {"memk": 1, "memv": 0, "A": 1, "B": 2, "M": 1}


def count(kinds, upto):
    return sum(k in kinds for k in KIND[:max(upto, 0)])


QK_KINDS = ("memk", "A", "B", "M")
V_KINDS = ("memv", "A", "B")
HAS_Q = ("A", "B", "M")
HAS_K = ("memk", "A", "B")


def batches(upto):
    return sum(BATCHES[k] for k in KIND[:max(upto, 0)])


def units_before(j):
    return sum(UNITS_OF[k] for k in KIND[:max(j, 0)])


def raw_slot(n):
    if n < 24:
        first, places = 0, (0, 1, 2, 3)
    elif n < 48:
        first, places = 24, (0, 1, 8, 9, 10, 11)
    else:
        first, places = 48, (0, 1, 4, 6)
    return places[(n - first) % len(places)]


def raw_group(n):
    place = raw_slot(n)
    return place if place < 4 else 2 + place % 4


def raw_before(n):
    return next((m for m in range(n - 1, -1, -1) if raw_group(m) == raw_group(n)), None)


def raw_uses(n):
    return sum(raw_group(m) == raw_group(n) for m in range(n + 1))


def has_prev(j):
    s, t = JOBS[j]
    kind, order = STAGES[s][:2]
    if kind == "M":
        return True
    return t > 0 if order == 0 else (t % 2 == 1 if order == 1 else False)


def step_slices(j):
    n = UNITS_OF[KIND[j - LAG]] if 0 <= j - LAG < NJ else 0
    return {0: [], 2: [1, 4], 4: [0, 2, 4, 6]}[n]


def turn_slices(j):
    return 5, 7


def slot_of(n):
    j, u = UNITS[n]
    return j + LAG, step_slices(j + LAG)[u]


def units_scored(slot, k):
    return sum(slot_of(n) <= (slot, k) for n in range(NU))


def token_tile(ap, order, tile):
    if order == 0:
        return ap[:, tile * P:(tile + 1) * P]
    if order == 1:
        return ap.rearrange("p (b i r) -> p r b i", b=2, r=4)[:, tile // 2, tile % 2, :]
    return ap.rearrange("p (i t) -> p t i", t=8)[:, tile]


def layer(nc, x, mem, positions, attn_norm, w_in, a_q_norm, a_k_norm, b_q_norm, b_k_norm, b_sinks,
          mem_norm, w_mem_kv, m_q_norm, m_k_norm, w_o_a, w_o_b, w_o_m, w_gate, b_gate, w_out,
          ffn_norm, w_up, conv_w, conv_b, w_down, out):
    S, D = x.shape[1], x.shape[2]
    NT, NK = S // P, D // P
    FF = w_down.shape[1]
    x_t = x[0].rearrange("(t p) d -> t p d", p=P)
    mem_t = mem[0].rearrange("(t p) d -> t p d", p=P)
    out_t = out[0].rearrange("(t p) d -> t p d", p=P)

    stats_dram = [nc.dram_tensor(f"stats_{g}", (S, 8), F32, kind="Internal").ap() for g in (1, 2)]

    with ExitStack() as whole:
        def sb(name, shape, dt=F32, ctx=whole):
            return ctx.enter_context(nc.sbuf_tensor(name, shape, dt))

        def sem(name):
            return whole.enter_context(nc.semaphore(name))

        ps = whole.enter_context(nc.psum_tensor("ps", [P, 8, 512], F32))
        act_hi = sb("act_hi", [P, NK, S], F32R)
        act_lo = sb("act_lo", [P, NK, S], F32R)
        ident = sb("ident", [P, P])
        ident_ready = sem("ident_ready")
        half_power = sb("half_power", [P, 16])

        attn_out = sb("attn_out", [P, 10, S])
        x1, spare = attn_out[:, 0:NT, :], attn_out[:, NT:NT + 2, :]

        input_projections(nc, x_t, mem_t, positions, attn_norm, w_in, a_q_norm, a_k_norm, b_q_norm,
                          b_k_norm, b_sinks, mem_norm, w_mem_kv, m_q_norm, m_k_norm, stats_dram,
                          ps, act_hi, act_lo, ident, ident_ready, half_power, attn_out)
        with ExitStack() as middle:
            merged = sb("merged", [P, NK, S], ctx=middle)
            gated_outputs(nc, w_gate, b_gate, w_o_a, w_o_b, w_o_m, ps, act_hi, act_lo, attn_out, merged)
            output_projection(nc, x_t, w_out, ffn_norm, ps, act_hi, act_lo, ident, half_power, merged, x1)
        feed_forward(nc, w_up, conv_w, conv_b, w_down, out_t, ps, act_hi, act_lo, ident, x1, spare)


def input_projections(nc, x_t, mem_t, positions, attn_norm, w_in, a_q_norm, a_k_norm, b_q_norm, b_k_norm,
                      b_sinks, mem_norm, w_mem_kv, m_q_norm, m_k_norm, stats_dram, ps, act_hi, act_lo,
                      ident, ident_ready, half_power, attn_out):
    NK, S = act_hi.shape[1], act_hi.shape[2]
    NX = 10
    inv_d = 1.0 / (NK * P)
    with ExitStack() as ctx:
        def sb(name, shape, dt=F32):
            return ctx.enter_context(nc.sbuf_tensor(name, shape, dt))

        def sem(name):
            return ctx.enter_context(nc.semaphore(name))

        w_raw = sb("w_raw", [P, 2, 768])
        w_hi = sb("w_hi", [P, NK, 768], F32R)
        w_lo = sb("w_lo", [P, NK, 768], F32R)
        k_mem = sb("k_mem", [P, 4, 256])
        v_mem = sb("v_mem", [P, 2, 512])
        masks = sb("masks", [P, 4, P])
        rope_cos = sb("rope_cos", [P, 3, 8, ROT])
        rope_sin = sb("rope_sin", [P, 3, 8, ROT])
        gains = sb("gains", [P, 768])
        norm_gain = sb("norm_gain", [P, 2, NK])
        neg_sink = sb("neg_sink", [P, 8])
        row_sums = sb("row_sums", [P, 16])
        row_rstd = sb("row_rstd", [P, 16])
        stats = sb("stats", [P, 3, 8, 8])
        with ExitStack() as early:
            mem_hi = early.enter_context(nc.sbuf_tensor("mem_hi", [P, NK, 256], F32R))
            mem_lo = early.enter_context(nc.sbuf_tensor("mem_lo", [P, NK, 256], F32R))
        q_ring = sb("q_ring", [P, RQ, 4, P])
        k_ring = sb("k_ring", [P, RK, 2, P])
        v_ring = sb("v_ring", [P, RK, 256])
        prob = sb("prob", [P, 2, 2, 256])
        prob_t = sb("prob_t", [P, 2, 2, 2, P])
        square = sb("square", [P, 640])
        qk = sb("qk", [P, 2, 640])
        rope_a = sb("rope_a", [P, 10, ROT])
        rope_b = sb("rope_b", [P, 10, ROT])
        head_ss = sb("head_ss", [P, 2, 10])
        head_rstd = sb("head_rstd", [P, 2, 10])
        small = sb("small", [P, 2, 12])
        parity = sb("parity", [P, 2])
        pos_i = sb("pos_i", [P, 3, 8], I32)
        pos_f = sb("pos_f", [P, 3, 8])
        angle = prob[:, 1, :, :].rearrange("p a b -> p (a b)")[:, 0:384].rearrange("p (s n) -> p s n", s=2)
        turns = prob_t[:, 0, :, :, :].rearrange("p e b n -> p (e b n)")[:, 0:384].rearrange("p (s n) -> p s n", s=2)
        merge = {n: sb(f"merge_{n}", [P, w]) for n, w in
                 (("max", 32), ("e", 96), ("total", 32), ("f", 96))}

        mem_in = [sem(f"mem_in{n}") for n in range(2)]
        x_in = [sem(f"x_in{n}") for n in range(4)]
        const_in = sem("const_in")
        pos_in = sem("pos_in")
        masks_built = sem("masks_built")
        gain_in, gain_turned, gain_ready = sem("gain_in"), sem("gain_turned"), sem("gain_ready")
        x_sq, x_rstd, x_scaled, x_turned, x_gained, x_hi, x_lo_even, x_lo_odd = (
            sem(n) for n in ("x_sq", "x_rstd", "x_scaled", "x_turned", "x_gained", "x_hi", "x_lo_even", "x_lo_odd"))
        angles_ready, sines_ready, rope_ready = sem("angles_ready"), sem("sines_ready"), sem("rope_ready")
        sink_ready = sem("sink_ready")
        raw_in = [sem(f"raw_in{n}") for n in range(6)]
        w_hi_done, w_lo_even, w_lo_odd, w_used = (sem(n) for n in ("w_hi_done", "w_lo_even", "w_lo_odd", "w_used"))
        proj_done, sq_done, ss_done, rstd_done, normed, roped = (
            sem(n) for n in ("proj_done", "sq_done", "ss_done", "rstd_done", "normed", "roped"))
        v_done, turned, q_done, k_done = (sem(n) for n in ("v_done", "turned", "q_done", "k_done"))
        scored, min_done, exp_done, prob_done, prob_turned, prob_copied, pv_done, o_done, sink_gap, sink_exp = (
            sem(n) for n in ("scored", "min_done", "exp_done", "prob_done", "prob_turned", "prob_copied",
                             "pv_done", "o_done", "sink_gap", "sink_exp"))
        spread_done = sem("spread_done")
        stats_out, stats_in, shift_ready, shift_exp, factors_ready, factor_turned, factor_used = (
            sem(n) for n in ("stats_out", "stats_in", "shift_ready", "shift_exp", "factors_ready",
                             "factor_turned", "factor_used"))
        group_added = sem("group_added")
        dve_chain, act_chain, pool_chain = sem("dve_chain"), sem("act_chain"), sem("pool_chain")

        TQ, SC, PT, OB = 4, 5, 6, 7

        def proj_a(j):
            return ps[:, 2 * (j % 2), :]

        def proj_b(j):
            return ps[:, 2 * (j % 2) + 1, 0:256]

        def wide(n):
            return ps[:, 4 + 2 * (n % 2):6 + 2 * (n % 2), :].rearrange("p b n -> p (b n)")

        scores = ps[:, TQ:SC + 1, 0:256]
        prob_turn = ps[:, PT, :].rearrange("p (e b n) -> p e b n", e=2, b=2)

        last_job_of = {s: max(j for j in range(NJ) if JOBS[j][0] == s) for s in range(len(STAGES))}
        merge_from = next(j for j in range(NJ) if KIND[j] == "B") + 2
        MERGE_AT = [(merge_from + 1 + m // 2, (3, 5)[m % 2]) for m in range(12)]

        def merges_before(slot, k):
            return sum(at < (slot, k) for at in MERGE_AT)

        def merge_batch(m):
            return m // 6, (m // 3) % 2, m % 3

        x_slot = [attn_out[:, n, :] for n in range(NX)]
        gain_rows = square[0:2 * NK, 0:P]
        squares_junk = square[:, :].bitcast(mybir.dt.bfloat16)[:, 0:NK * P]

        def raw(n):
            return w_raw[:, raw_slot(n), :] if raw_slot(n) < 2 else attn_out[:, raw_slot(n) - 2, :]

        def x_split(eng, n):
            eng.wait_ge(x_lo_even, (n + 1) // 2)
            eng.wait_ge(x_lo_odd, n // 2)

        def pair_of(slot):
            return (2 * slot + 2, 2 * slot + 3) if 0 <= slot < 4 else ()

        def x_low(eng, n):
            eng.wait_ge(x_hi, n + 1)
            hi, lo, c = (mem_hi, mem_lo, n) if n < 2 else (act_hi, act_lo, n - 2)
            eng.tensor_tensor(lo[:, :, c * P:(c + 1) * P], x_slot[n].rearrange("p (k n) -> p k n", n=P),
                              hi[:, :, c * P:(c + 1) * P].bitcast(F32), ALU.subtract
                              ).then_inc(x_lo_odd if n % 2 else x_lo_even, 1)

        def w_split(eng, n):
            eng.wait_ge(w_lo_odd if n % 2 else w_lo_even, n // 2 + 1)

        def w_low(eng, n):
            na, nb = STAGES[n // 8][4:6]
            eng.wait_ge(w_hi_done, n + 1)
            eng.tensor_tensor(w_lo[:, n % 8, 0:na + nb], raw(n)[:, 0:na + nb],
                              w_hi[:, n % 8, 0:na + nb].bitcast(F32), ALU.subtract
                              ).then_inc(w_lo_odd if n % 2 else w_lo_even, 1)

        def v_wait(eng, j):
            before = units_before(j - RK + 2)
            if before:
                eng.wait_ge(pv_done, before)

        def count_b(n):
            return sum(KIND[j] == "B" for j, _ in UNITS[:n])

        def count_bm(n):
            return sum(KIND[j] != "A" for j, _ in UNITS[:n])

        def unit_stats(n, e):
            j, u = UNITS[n]
            s, t = JOBS[j]
            if KIND[j] == "A":
                g = STAGES[s][2]
                h = 2 * u + e
                return stats[:, g, t, h:h + 1], stats[:, g, t, 4 + h:5 + h]
            return small[:, n % 2, e:e + 1], small[:, n % 2, 2 + e:3 + e]

        block = ctx.enter_context(nc.Block())

        @block.sync
        def _(sp):
            for n in range(2):
                sp.dma_start(x_slot[n], mem_t[n]).then_inc(mem_in[n], 16)
            sp.dma_start(gain_rows[0:NK, :], attn_norm[0].rearrange("(k p) -> k p", p=P)).then_inc(gain_in, 16)
            sp.dma_start(gain_rows[NK:2 * NK, :], mem_norm[0].rearrange("(k p) -> k p", p=P)).then_inc(gain_in, 16)

            def reorder_stats():
                last_a1 = units_before(last_job_of[3] + 1)
                last_a2 = units_before(last_job_of[4] + 1)
                sp.wait_ge(exp_done, last_a1)
                for b in range(2):
                    sp.dma_start(stats_dram[0].rearrange("(b i r) c -> b i r c", b=2, r=4)[b],
                                 stats[:, 1].rearrange("p (r b) c -> p b r c", b=2)[:, b]).then_inc(stats_out, 16)
                sp.wait_ge(exp_done, last_a2)
                sp.dma_start(stats_dram[1].rearrange("(i t) c -> i t c", t=8), stats[:, 2]).then_inc(stats_out, 16)
                sp.wait_ge(stats_out, 48)
                for g in range(2):
                    sp.dma_start(stats[:, 1 + g], stats_dram[g].rearrange("(t p) c -> p t c", p=P)).then_inc(stats_in, 16)

            for n in range(8 * len(STAGES)):
                kind, _, _, col, na, nb, _ = STAGES[n // 8]
                src = w_mem_kv if kind in ("memk", "memv") else w_in
                k = n % 8
                if n == 8 * 6:
                    reorder_stats()
                if raw_before(n) is not None:
                    w_split(sp, raw_before(n))
                if n // 8 == 0 and raw_slot(n) >= 2:
                    x_split(sp, 2)
                if n in (2, 4, 6, 8):
                    for m in (n, n + 1):
                        sp.dma_start(x_slot[m], x_t[m - 2]).then_inc(x_in[m // 2 - 1], 16)
                if n == 24 + 2:
                    x_split(sp, NX)
                if n == 48 + 2:
                    sp.wait_ge(group_added, 4)
                sp.dma_start(raw(n)[:, 0:na + nb],
                             src[0, k * P:(k + 1) * P, col:col + na + nb]).then_inc(raw_in[raw_group(n)], 16)

        @block.gpsimd
        def _(pool):
            chain = [0]

            def link(ins):
                chain[0] += 1
                ins.then_inc(pool_chain, 1)
                pool.wait_ge(pool_chain, chain[0])

            link(pool.memset(ident[:], 0.0))
            pool.affine_select(out=ident[:], in_=ident[:], compare_op=ALU.not_equal, fill=1.0, base=0,
                               pattern=[[-1, P]], channel_multiplier=1).then_inc(ident_ready, 1)
            link(pool.memset(half_power[:], -0.5))
            link(pool.memset(masks[:], 0.0))
            for m, sign, base in ((0, 1, -1), (1, 1, 0), (2, -1, 0), (3, -1, 0)):
                link(pool.affine_select(out=masks[:, m, :], in_=masks[:, m, :], compare_op=ALU.is_ge, fill=MASKED,
                                        base=base, pattern=[[sign, P]], channel_multiplier=-sign))
            link(pool.memset(prob[:, 1, 1, 0:64], 0.0))
            pool.affine_select(out=prob[:, 1, 1, 0:64], in_=prob[:, 1, 1, 0:64], compare_op=ALU.not_equal, fill=MASKED,
                               base=0, pattern=[[-2, 64]], channel_multiplier=1).then_inc(masks_built, 1)

            def x_rms(n):
                pool.wait_ge(x_sq, n + 1)
                link(pool.tensor_scalar(row_rstd[:, n:n + 1], row_sums[:, n:n + 1], inv_d, EPS, ALU.mult, ALU.add))
                pool.tensor_tensor(row_rstd[:, n:n + 1], row_rstd[:, n:n + 1], half_power[:, 0:1],
                                   ALU.pow).then_inc(x_rstd, 1)

            for n in (0, 1):
                x_rms(n)
            x_low(pool, 0)

            def norm_and_rope(j):
                s, t = JOBS[j]
                kind, order, g = STAGES[s][:3]
                if kind not in QK_KINDS:
                    return
                i = count(QK_KINDS, j)
                nh, dh = {"memk": (4, 128), "A": (8, 64), "B": (10, 64), "M": (4, 128)}[kind]
                pool.wait_ge(ss_done, i + 1)
                link(pool.tensor_scalar(head_rstd[:, i % 2, 0:nh], head_ss[:, i % 2, 0:nh], 1.0 / dh, EPS,
                                        ALU.mult, ALU.add))
                pool.tensor_tensor(head_rstd[:, i % 2, 0:nh], head_rstd[:, i % 2, 0:nh], half_power[:, 0:nh],
                                   ALU.pow).then_inc(rstd_done, 1)
                buf = qk[:, i % 2, 0:nh * dh].rearrange("p (h d) -> p h d", d=dh)
                pool.wait_ge(normed, i + 1)
                if i == 0:
                    pool.wait_ge(const_in, 16 * 7)
                parts = {"memk": ((0, 4, 640),), "A": ((0, 4, 64 * g), (4, 8, 192 + 64 * g)),
                         "B": ((0, 8, 384), (8, 10, 448)), "M": ((0, 4, 512),)}[kind]
                for h0, h1, off in parts:
                    ins = pool.tensor_tensor(buf[:, h0:h1, :], buf[:, h0:h1, :],
                                             gains[:, off:off + dh].unsqueeze(1).to_broadcast([P, h1 - h0, dh]), ALU.mult)
                    if dh == 64 or (h0, h1, off) != parts[-1]:
                        link(ins)
                if dh == 128:
                    ins.then_inc(roped, 1)
                    return
                if kind == "A" and g == 0 and t == 0:
                    pool.wait_ge(rope_ready, 1)
                cos = rope_cos[:, order, t, :].unsqueeze(1).to_broadcast([P, nh, ROT])
                sin = rope_sin[:, order, t, :].unsqueeze(1)
                link(pool.tensor_tensor(rope_a[:, 0:nh, :], buf[:, :, 0:ROT], cos, ALU.mult))
                link(pool.tensor_tensor(rope_b[:, 0:nh, 0:HALF], buf[:, :, HALF:ROT],
                                        sin[:, :, 0:HALF].to_broadcast([P, nh, HALF]), ALU.mult))
                link(pool.tensor_tensor(rope_b[:, 0:nh, HALF:ROT], buf[:, :, 0:HALF],
                                        sin[:, :, HALF:ROT].to_broadcast([P, nh, HALF]), ALU.mult))
                pool.tensor_tensor(buf[:, :, 0:ROT], rope_a[:, 0:nh, :], rope_b[:, 0:nh, :],
                                   ALU.add).then_inc(roped, 1)

            for k in range(0, 8, 2):
                w_low(pool, k)
            for n in pair_of(0):
                x_rms(n)
            for j in range(NJ + LAG + 1):
                for n in pair_of(j + 1):
                    x_rms(n)
                if 0 <= j - 1 < NJ:
                    norm_and_rope(j - 1)
                for n in pair_of(j)[:1]:
                    x_low(pool, n)
                for s in last_job_of:
                    if last_job_of[s] == j and s + 1 < len(STAGES):
                        for k in range(0, 8, 2):
                            w_low(pool, 8 * (s + 1) + k)

        @block.scalar
        def _(act):
            with nc.allow_non_contiguous_dma(reason="positions and gains, once"):
                p0 = positions[0]
                act.dma_start(pos_i[:, 0, :], p0.rearrange("(t p) -> p t", p=P)).then_inc(pos_in, 16)
                for b in range(2):
                    act.dma_start(pos_i[:, 1, :].rearrange("p (r b) -> p b r", b=2)[:, b],
                                  p0.rearrange("(b i r) -> b i r", b=2, r=4)[b]).then_inc(pos_in, 16)
                act.dma_start(pos_i[:, 2, :], p0.rearrange("(i t) -> i t", t=8)).then_inc(pos_in, 16)
                for off, src in ((0, a_q_norm[0].rearrange("g d -> (g d)")), (192, a_k_norm[0].rearrange("g d -> (g d)")),
                                 (384, b_q_norm[0]), (448, b_k_norm[0]), (512, m_q_norm[0]), (640, m_k_norm[0])):
                    act.dma_start(gains[:, off:off + src.shape[0]], src.partition_broadcast(P)).then_inc(const_in, 16)
                act.dma_start(neg_sink[:, :], b_sinks[0].partition_broadcast(P)).then_inc(const_in, 16)

            def x_high(n):
                act.wait_ge(x_gained, n + 1)
                hi, c = (mem_hi, n) if n < 2 else (act_hi, n - 2)
                act.activation(hi[:, :, c * P:(c + 1) * P], x_slot[n].rearrange("p (k n) -> p k n", n=P),
                               ACT.Copy).then_inc(x_hi, 1)

            chain = [0]

            def link(ins):
                chain[0] += 1
                ins.then_inc(act_chain, 1)
                act.wait_ge(act_chain, chain[0])

            def x_square(n):
                if n < 2:
                    act.wait_ge(mem_in[n], 16)
                else:
                    act.wait_ge(x_in[n // 2 - 1], 32)
                if n >= 1:
                    act.wait_ge(x_sq, n)
                before = count(QK_KINDS, (n - 2) // 2 - 1)
                if before:
                    act.wait_ge(ss_done, before)
                act.activation(squares_junk, x_slot[n], ACT.Square, accum_out=row_sums[:, n:n + 1]).then_inc(x_sq, 1)

            def sines():
                act.wait_ge(angles_ready, 1)
                act.activation(turns[:, :, :], angle[:, :, :], ACT.Sin).then_inc(sines_ready, 1)

            def cast_slice(n):
                _, _, _, col, na, nb, _ = STAGES[n // 8]
                act.wait_ge(raw_in[raw_group(n)], 16 * raw_uses(n))
                if n >= 8:
                    act.wait_ge(w_used, n - 7)
                act.activation(w_hi[:, n % 8, 0:na + nb], raw(n)[:, 0:na + nb], ACT.Copy).then_inc(w_hi_done, 1)

            def squares(j):
                kind = KIND[j]
                act.wait_ge(proj_done, j + 1)
                if kind in QK_KINDS:
                    i = count(QK_KINDS, j)
                    if i >= 1:
                        act.wait_ge(ss_done, i)
                    spreads = merges_before(j + 1, 0)
                    if spreads:
                        act.wait_ge(factor_turned, spreads)
                    if j < 4:
                        act.wait_ge(x_sq, min(2 * j + 6, NX))
                    ins = act.activation(square[:, 0:512], proj_a(j), ACT.Square)
                    if kind == "B":
                        ins = act.activation(square[:, 512:640], proj_b(j)[:, 0:128], ACT.Square)
                    ins.then_inc(sq_done, 1)
                    if kind == "B":
                        act.wait_ge(sq_done, i + 1)
                if kind in V_KINDS:
                    t = JOBS[j][1]
                    if kind == "memv":
                        ins = act.activation(v_mem[:, t, :], proj_a(j), ACT.Copy)
                    else:
                        v_wait(act, j)
                        c0 = 0 if kind == "A" else 128
                        ins = act.activation(v_ring[:, j % RK, 0:256 - c0], proj_b(j)[:, c0:256], ACT.Copy)
                    ins.then_inc(v_done, 1)

            def copy_q(j):
                kind = KIND[j]
                if kind not in HAS_Q:
                    return
                act.wait_ge(turned, batches(j) + 1)
                before = units_before(j - RQ + 1)
                if before:
                    act.wait_ge(scored, before)
                nb = 2 if kind == "A" else 4
                scale = -(1.0 / math.sqrt(128 if kind == "M" else 64))
                act.activation(q_ring[:, j % RQ, 0:nb, :], ps[:, TQ, :].rearrange("p (b n) -> p b n", n=P)[:, 0:nb, :],
                               ACT.Copy, scale=scale).then_inc(q_done, 1)

            def exps(n):
                j, u = UNITS[n]
                kind, (s, t) = KIND[j], JOBS[j]
                act.wait_ge(min_done, n + 1)
                c0 = 0 if has_prev(j) else P
                for e in range(2):
                    low, total = unit_stats(n, e)
                    src = scores[:, e, :] if kind == "M" else prob[:, n % 2, e, c0:256]
                    if kind == "M" and n >= 2 and e == 0:
                        act.wait_ge(prob_turned, n - 1)
                    ins = act.activation(prob[:, n % 2, e, c0:256], src, ACT.Exp, bias=low, scale=-1.0, accum_out=total)
                    if e == 0:
                        link(ins)
                ins.then_inc(exp_done, 1)
                if kind == "B":
                    b = count_b(n)
                    act.wait_ge(sink_gap, b + 1)
                    act.activation(small[:, n % 2, 4:6], small[:, n % 2, 4:6], ACT.Exp).then_inc(sink_exp, 1)

            def copy_probs(n):
                c0 = 0 if has_prev(UNITS[n][0]) else 1
                act.wait_ge(prob_turned, n + 1)
                if n >= 2:
                    act.wait_ge(pv_done, n - 1)
                act.activation(prob_t[:, n % 2, :, c0:2, :], prob_turn[:, :, c0:2, :], ACT.Copy).then_inc(prob_copied, 1)

            def spread_factors(m, j):
                pair, half, g = merge_batch(m)
                if m == 0:
                    act.wait_ge(factors_ready, 1)
                else:
                    act.wait_ge(factor_turned, m)
                act.wait_ge(ss_done, count(QK_KINDS, j))
                f = merge["f"][:].rearrange("p (g t h) -> p g t h", g=3, h=4)
                act.activation(square[:, 0:512].rearrange("p (t e d) -> p t e d", t=4, e=2),
                               f[:, g, 4 * half:4 * half + 4, 2 * pair:2 * pair + 2].unsqueeze(3).to_broadcast([P, 4, 2, 64]),
                               ACT.Copy).then_inc(spread_done, 1)

            act.wait_ge(gain_turned, 1)
            act.activation(norm_gain[:].rearrange("p a k -> p (a k)"), ps[:, OB, 0:2 * NK], ACT.Copy).then_inc(gain_ready, 1)
            for n in (0, 1):
                x_square(n)
            for n in (0, 1):
                x_high(n)
            for k in range(8):
                cast_slice(k)
            for n in pair_of(0):
                x_square(n)
            n = 0
            for j in range(NJ + LAG + 1):
                if 0 <= j - 1 < NJ:
                    squares(j - 1)
                for m in pair_of(j + 1):
                    x_square(m)
                if j == 4:
                    sines()
                for k in range(8):
                    if k in step_slices(j):
                        exps(n)
                        if n >= 1:
                            copy_probs(n - 1)
                        n += 1
                    if k == 4:
                        for m in pair_of(j):
                            x_high(m)
                    if k == turn_slices(j)[0] and 0 <= j - 1 < NJ:
                        copy_q(j - 1)
                    if j in last_job_of.values() and JOBS[j][0] + 1 < len(STAGES):
                        cast_slice(8 * (JOBS[j][0] + 1) + k)
                    if (j, k) in MERGE_AT:
                        spread_factors(MERGE_AT.index((j, k)), j)
                if j == merge_from:
                    act.wait_ge(shift_ready, 1)
                    act.activation(merge["e"][:], merge["e"][:], ACT.Exp).then_inc(shift_exp, 1)
            copy_probs(NU - 1)

        @block.vector
        def _(dve):
            chain = [0]

            def link(ins):
                chain[0] += 1
                ins.then_inc(dve_chain, 1)
                dve.wait_ge(dve_chain, chain[0])

            def x_scale(n):
                dve.wait_ge(x_rstd, n + 1)
                dve.tensor_scalar(x_slot[n], x_slot[n], row_rstd[:, n:n + 1], None, ALU.mult).then_inc(x_scaled, 1)

            def x_gain(n):
                dve.wait_ge(x_turned, n + 1)
                if n == 0:
                    dve.wait_ge(gain_ready, 1)
                g = norm_gain[:, 1 if n < 2 else 0, :].unsqueeze(2).to_broadcast([P, NK, P])
                dve.tensor_tensor(x_slot[n].rearrange("p (k n) -> p k n", n=P),
                                  wide(n).rearrange("p (k n) -> p k n", n=P), g, ALU.mult).then_inc(x_gained, 1)

            def tables():
                dve.wait_ge(const_in, 16 * 7)
                link(dve.tensor_scalar(neg_sink[:, :], neg_sink[:, :], -1.0, None, ALU.mult))
                dve.wait_ge(masks_built, 1)
                link(dve.tensor_reduce(parity[:, 1:2], prob[:, 1, 1, 0:64], AX.X, ALU.add))
                link(dve.tensor_scalar(parity[:, 0:1], parity[:, 1:2], -1.0, MASKED, ALU.mult, ALU.add))
                own = masks[:, 3, :].rearrange("p (i h) -> p h i", h=2)
                for h in range(2):
                    ins = dve.tensor_scalar(own[:, h, :], own[:, h, :], parity[:, h:h + 1], None, ALU.max)
                    if h == 0:
                        link(ins)
                link(ins)

                dve.wait_ge(pos_in, 16 * 4)
                link(dve.tensor_copy(pos_f[:], pos_i[:]))
                freqs = np.exp(np.arange(HALF, dtype=np.float32) * np.float32(-2.0 * math.log(ROPE_THETA) / ROT))
                cosine = angle[:, 0, :].rearrange("p (o f) -> p o f", f=HALF)
                sine = angle[:, 1, :].rearrange("p (o f) -> p o f", f=HALF)
                for f in range(HALF):
                    for part in (cosine, sine):
                        ins = dve.tensor_scalar(part[:, :, f], pos_f[:].rearrange("p o t -> p (o t)"), float(freqs[f]), None, ALU.mult)
                        link(ins)
                magic = 1.5 * 2.0 ** 23
                two_pi = 2.0 * math.pi
                part1 = 6.28125
                part2 = 507.0 / 262144.0
                part3 = two_pi - part1 - part2
                link(dve.tensor_scalar(turns[:, 0, :], angle[:, 0, :], 1.0 / two_pi, 0.25, ALU.mult, ALU.add))
                link(dve.tensor_scalar(turns[:, 0, :], turns[:, 0, :], magic, None, ALU.add))
                link(dve.tensor_scalar(turns[:, 1, :], angle[:, 1, :], 1.0 / two_pi, magic, ALU.mult, ALU.add))
                link(dve.tensor_scalar(turns[:, :, :], turns[:, :, :], -magic, None, ALU.add))
                for part in (part1, part2, part3):
                    link(dve.scalar_tensor_tensor(out=angle[:, :, :], in0=turns[:, :, :], scalar=-part, in1=angle[:, :, :],
                                                  op0=ALU.mult, op1=ALU.add))
                link(dve.tensor_scalar(angle[:, 0, :], angle[:, 0, :], math.pi / 2, None, ALU.add))
                dve.tensor_scalar(angle[:, :, :], angle[:, :, :], 3.1415925, -3.1415925, ALU.min, ALU.max).then_inc(angles_ready, 1)
                dve.wait_ge(sines_ready, 1)
                cos_v = turns[:, 0, :].rearrange("p (o f) -> p o f", f=HALF)
                sin_v = turns[:, 1, :].rearrange("p (o f) -> p o f", f=HALF)
                rc = rope_cos[:].rearrange("p o t f -> p (o t) f")
                rs = rope_sin[:].rearrange("p o t f -> p (o t) f")
                link(dve.tensor_copy(rc[:, :, 0:HALF], cos_v))
                link(dve.tensor_copy(rc[:, :, HALF:ROT], cos_v))
                link(dve.tensor_scalar(rs[:, :, 0:HALF], sin_v, -1.0, None, ALU.mult))
                dve.tensor_copy(rs[:, :, HALF:ROT], sin_v).then_inc(rope_ready, 1)
                dve.wait_ge(rope_ready, 1)

            def sum_squares(j):
                kind = KIND[j]
                if kind not in QK_KINDS:
                    return
                i = count(QK_KINDS, j)
                nh, dh = {"memk": (4, 128), "A": (8, 64), "B": (10, 64), "M": (4, 128)}[kind]
                dve.wait_ge(sq_done, i + 1)
                if i >= 2:
                    dve.wait_ge(rstd_done, i - 1)
                dve.tensor_reduce(head_ss[:, i % 2, 0:nh], square[:, 0:nh * dh].rearrange("p (h d) -> p h d", d=dh),
                                  AX.X, ALU.add).then_inc(ss_done, 1)

            def normalise(j):
                kind = KIND[j]
                if kind not in QK_KINDS:
                    return
                i = count(QK_KINDS, j)
                nh, dh = {"memk": (4, 128), "A": (8, 64), "B": (10, 64), "M": (4, 128)}[kind]
                dve.wait_ge(rstd_done, i + 1)
                if i >= 2:
                    dve.wait_ge(turned, batches(qk_job(i - 1)))
                na = min(nh * dh, 512)
                rstd = head_rstd[:, i % 2, 0:nh].unsqueeze(2).to_broadcast([P, nh, dh])
                buf = qk[:, i % 2, 0:nh * dh].rearrange("p (h d) -> p h d", d=dh)
                ha = na // dh
                if kind == "B":
                    dve.wait_ge(v_done, count(V_KINDS, j + 1))
                    link(dve.tensor_tensor(buf[:, 0:ha, :].rearrange("p (u e) d -> p e u d", e=2),
                                           proj_a(j).rearrange("p (e u d) -> p e u d", e=2, d=dh),
                                           head_rstd[:, i % 2, 0:ha].rearrange("p (e u) -> p e u", e=2).unsqueeze(3)
                                           .to_broadcast([P, 2, 4, dh]), ALU.mult))
                else:
                    ins = dve.tensor_tensor(buf[:, 0:ha, :], proj_a(j).rearrange("p (h d) -> p h d", d=dh), rstd[:, 0:ha, :], ALU.mult)
                if kind == "B":
                    ins = dve.tensor_tensor(buf[:, ha:nh, :], proj_b(j)[:, 0:P].rearrange("p (h d) -> p h d", d=dh),
                                            rstd[:, ha:nh, :], ALU.mult)
                ins.then_inc(normed, 1)

            def qk_job(i):
                return [j for j in range(NJ) if KIND[j] in QK_KINDS][i]

            def copy_k(j):
                kind, t = KIND[j], JOBS[j][1]
                if kind not in HAS_K:
                    return
                dve.wait_ge(turned, batches(j + 1))
                if kind in HAS_Q:
                    dve.wait_ge(q_done, count(HAS_Q, j + 1))
                bank = ps[:, TQ, :].rearrange("p (b n) -> p b n", n=P)
                if kind == "memk":
                    ins = dve.tensor_copy(k_mem[:, :, t * P:(t + 1) * P], bank)
                else:
                    v_wait(dve, j)
                    if kind == "A":
                        ins = dve.tensor_copy(k_ring[:, j % RK, :, :], bank[:, 2:4, :])
                    else:
                        ins = dve.tensor_copy(k_ring[:, j % RK, 0, :], bank[:, 0, :])
                ins.then_inc(k_done, 1)

            def minima(n):
                j, u = UNITS[n]
                kind, (s, t) = KIND[j], JOBS[j]
                order = STAGES[s][1]
                dve.wait_ge(scored, n + 1)
                if n >= 2:
                    dve.wait_ge(prob_turned, n - 1)
                if kind == "M":
                    dve.tensor_reduce(small[:, n % 2, 0:2], scores, AX.X, ALU.min).then_inc(min_done, 1)
                    return
                c0 = 0 if has_prev(j) else P
                mask = (masks[:, 3:4, :] if order == 2 else masks[:, 2:3, :] if c0 else
                        masks[:, 1:3, :] if kind == "A" else masks[:, 0:3:2, :])
                for e in range(2):
                    low, _ = unit_stats(n, e)
                    start = START_MIN if kind == "A" else neg_sink[:, u + 4 * e:u + 4 * e + 1]
                    ins = dve.tensor_tensor_reduce(prob[:, n % 2, e, c0:256].rearrange("p (b n) -> p b n", n=P),
                                                   scores[:, e, c0:256].rearrange("p (b n) -> p b n", n=P), mask, 1.0, start,
                                                   ALU.add, ALU.min, low)
                    if e == 0:
                        link(ins)
                ins.then_inc(min_done, 1)
                if kind == "B":
                    dve.wait_ge(min_done, n + 1)
                    dve.tensor_tensor(small[:, n % 2, 4:6], small[:, n % 2, 0:2], neg_sink[:, u:u + 5:4],
                                      ALU.subtract).then_inc(sink_gap, 1)

            def divide(n):
                j, u = UNITS[n]
                kind = KIND[j]
                if kind == "A":
                    return
                dve.wait_ge(exp_done, n + 1)
                total = small[:, n % 2, 2:4]
                if kind == "B":
                    dve.wait_ge(sink_exp, count_b(n) + 1)
                    link(dve.tensor_tensor(small[:, n % 2, 6:8], total, small[:, n % 2, 4:6], ALU.add))
                    total = small[:, n % 2, 6:8]
                link(dve.reciprocal(small[:, n % 2, 8:10], total))
                c0 = 0 if has_prev(j) else P
                for e in range(2):
                    ins = dve.tensor_scalar(prob[:, n % 2, e, c0:256], prob[:, n % 2, e, c0:256],
                                            small[:, n % 2, 8 + e:9 + e], None, ALU.mult)
                    if e == 0:
                        link(ins)
                ins.then_inc(prob_done, 1)

            def copy_out(n):
                j, u = UNITS[n]
                kind, (s, t) = KIND[j], JOBS[j]
                dve.wait_ge(pv_done, n + 1)
                if kind == "M":
                    dst = attn_out[:, 2 + 2 * u:4 + 2 * u, t * P:(t + 1) * P]
                    src = ps[:, OB, 0:256].rearrange("p (e n) -> p e n", e=2)
                else:
                    base = 2 * STAGES[s][2] if kind == "A" else 6
                    dst = attn_out[:, base + u, t * P:(t + 1) * P]
                    src = ps[:, OB, 0:P]
                dve.tensor_copy(dst, src).then_inc(o_done, 1)

            def merge_factors():
                dve.wait_ge(stats_in, 32)
                lows = [stats[:, g, :, 0:4] for g in range(3)]
                sums = [stats[:, g, :, 4:8] for g in range(3)]
                mx = merge["max"][:].rearrange("p (t h) -> p t h", h=4)
                e = merge["e"][:].rearrange("p (g t h) -> p g t h", g=3, h=4)
                f = merge["f"][:].rearrange("p (g t h) -> p g t h", g=3, h=4)
                total = merge["total"][:].rearrange("p (t h) -> p t h", h=4)
                link(dve.tensor_tensor(mx, lows[0], lows[1], ALU.min))
                link(dve.tensor_tensor(mx, mx, lows[2], ALU.min))
                for g in range(3):
                    ins = dve.tensor_tensor(e[:, g], mx, lows[g], ALU.subtract)
                    if g < 2:
                        link(ins)
                ins.then_inc(shift_ready, 1)
                dve.wait_ge(shift_exp, 1)
                for g in range(3):
                    link(dve.tensor_tensor(f[:, g], e[:, g], sums[g], ALU.mult))
                link(dve.tensor_tensor(total, f[:, 0], f[:, 1], ALU.add))
                link(dve.tensor_tensor(total, total, f[:, 2], ALU.add))
                link(dve.reciprocal(total, total))
                for g in range(3):
                    ins = dve.tensor_tensor(f[:, g], e[:, g], total, ALU.mult)
                    if g < 2:
                        link(ins)
                ins.then_inc(factors_ready, 1)

            def merge_use(m):
                pair, half, g = merge_batch(m)
                dve.wait_ge(factor_turned, m + 1)
                dst = attn_out[:, pair, half * 512:(half + 1) * 512]
                bank = ps[:, OB, :]
                if g == 0:
                    dve.tensor_tensor(dst, bank, dst, ALU.mult).then_inc(factor_used, 1)
                    dve.wait_ge(factor_used, m + 1)
                    return
                src = attn_out[:, 2 * g + pair, :]
                if g == 1:
                    src = src.rearrange("p (r b i) -> p b i r", r=4, b=2)[:, half]
                    bank, dst = (a.rearrange("p (i r) -> p i r", r=4) for a in (bank, dst))
                else:
                    src = src.rearrange("p (t i) -> p i t", t=8)[:, half * 64:(half + 1) * 64]
                    bank, dst = (a.rearrange("p (i t) -> p i t", t=8) for a in (bank, dst))
                dve.tensor_tensor(src, bank, src, ALU.mult).then_inc(factor_used, 1)
                dve.wait_ge(factor_used, m + 1)
                dve.tensor_tensor(dst, dst, src, ALU.add).then_inc(group_added, 1)
                dve.wait_ge(group_added, 2 * (m // 3) + g)

            for n in (0, 1):
                x_scale(n)
            for n in (0, 1):
                x_gain(n)
            x_low(dve, 1)
            for k in range(1, 8, 2):
                w_low(dve, k)
            for n in pair_of(0):
                x_scale(n)
            n = 0
            for j in range(NJ + LAG + 1):
                if 0 <= j - 1 < NJ:
                    sum_squares(j - 1)
                    if 0 not in step_slices(j):
                        normalise(j - 1)
                for m in pair_of(j + 1):
                    x_scale(m)
                for m in pair_of(j):
                    x_gain(m)
                for m in pair_of(j)[1:]:
                    x_low(dve, m)
                if j == 4:
                    tables()
                for k in range(8):
                    if k in step_slices(j):
                        minima(n)
                        divide(n)
                        if n >= 2:
                            copy_out(n - 2)
                        n += 1
                    if k == 0 and 0 in step_slices(j) and 0 <= j - 1 < NJ:
                        normalise(j - 1)
                    if 0 <= j - 1 < NJ and k == turn_slices(j)[KIND[j - 1] == "B"]:
                        copy_k(j - 1)
                    if k % 2 and j in last_job_of.values() and JOBS[j][0] + 1 < len(STAGES):
                        w_low(dve, 8 * (JOBS[j][0] + 1) + k)
                    if (j, k) in MERGE_AT:
                        merge_use(MERGE_AT.index((j, k)))
                if j == merge_from:
                    merge_factors()
            copy_out(NU - 2)
            copy_out(NU - 1)

        @block.tensor
        def _(pe):
            pe.wait_ge(ident_ready, 1)
            pe.wait_ge(gain_in, 32)
            pe.transpose(ps[:, OB, 0:2 * NK], gain_rows, ident[0:2 * NK, 0:2 * NK]).then_inc(gain_turned, 1)

            def turn_x(n):
                pe.wait_ge(x_scaled, n + 1)
                if n >= 2:
                    pe.wait_ge(x_gained, n - 1)
                    keys = count(HAS_K, (n - 2) // 2 - 1)
                    if keys:
                        pe.wait_ge(k_done, keys)
                elif n == 1:
                    pe.wait_ge(gain_ready, 1)
                for k in range(NK):
                    ins = pe.transpose(wide(n)[:, k * P:(k + 1) * P], x_slot[n][:, k * P:(k + 1) * P], ident[:])
                ins.then_inc(x_turned, 1)

            for n in (0, 1):
                turn_x(n)

            def project(j, k):
                s, t = JOBS[j]
                kind, order, _, _, na, nb, tiles = STAGES[s]
                n = 8 * s + k
                if k == 0:
                    if kind in ("memk", "memv"):
                        x_split(pe, 2)
                    elif s == 2:
                        x_split(pe, 3 + t)
                    if j >= 2:
                        if count(QK_KINDS, j - 1):
                            pe.wait_ge(sq_done, count(QK_KINDS, j - 1))
                            pe.wait_ge(normed, count(QK_KINDS, j - 1))
                        if count(V_KINDS, j - 1):
                            pe.wait_ge(v_done, count(V_KINDS, j - 1))
                if t == 0:
                    w_split(pe, n)
                if kind in ("memk", "memv"):
                    hi, lo = (m[:, k, t * P:(t + 1) * P] for m in (mem_hi, mem_lo))
                else:
                    hi, lo = (token_tile(m[:, k, :], order, t) for m in (act_hi, act_lo))
                for i, (lhs, w) in enumerate(((hi, w_hi), (hi, w_lo), (lo, w_hi))):
                    ins = pe.matmul(proj_a(j)[:, 0:na], lhs, w[:, k, 0:na], start=(k == 0 and i == 0), stop=(k == 7 and i == 2))
                    if nb:
                        ins = pe.matmul(proj_b(j), lhs, w[:, k, na:na + nb], start=(k == 0 and i == 0), stop=(k == 7 and i == 2))
                if t == tiles - 1:
                    ins.then_inc(w_used, 1)
                    if k == 7:
                        pe.wait_ge(w_used, n + 1)
                        pe.nop().then_inc(proj_done, 1)
                elif k == 7:
                    ins.then_inc(proj_done, 1)

            def turn(j, batch):
                kind = KIND[j]
                if batch >= BATCHES[kind]:
                    return
                i = count(QK_KINDS, j)
                pe.wait_ge(roped, i + 1)
                bank_free(j, batch)
                bank = ps[:, TQ, :].rearrange("p (b n) -> p b n", n=P)
                buf = qk[:, i % 2, :]
                if kind == "B" and batch == 1:
                    ins = pe.transpose(bank[:, 0, :], buf[:, 512:640], ident[:])
                else:
                    for b in range(4):
                        ins = pe.transpose(bank[:, b, :], buf[:, b * P:(b + 1) * P], ident[:])
                ins.then_inc(turned, 1)

            def scores_read(n):
                if n >= 1:
                    pe.wait_ge(exp_done if KIND[UNITS[n - 1][0]] == "M" else min_done, n)

            def bank_free(j, batch):
                scores_read(units_scored(j + 1, turn_slices(j + 1)[batch]))
                q = count(HAS_Q, j + (1 if batch else 0))
                k = count(HAS_K, j)
                if q:
                    pe.wait_ge(q_done, q)
                if k:
                    pe.wait_ge(k_done, k)

            def score(n):
                j, u = UNITS[n]
                kind = KIND[j]
                if kind != "M" or u == 0:
                    pe.wait_ge(q_done, count(HAS_Q, j) + 1)
                    pe.wait_ge(k_done, count(HAS_K, j) + (kind != "M"))
                scores_read(n)
                slot, k = slot_of(n)
                two = slot <= NJ and KIND[slot - 1] == "B"
                pe.wait_ge(q_done, count(HAS_Q, slot if k > turn_slices(slot)[0] else slot - 1))
                pe.wait_ge(k_done, count(HAS_K, slot if k > turn_slices(slot)[two] else slot - 1))
                for e in range(2):
                    if kind == "M":
                        h = 2 * u + e
                        ins = pe.matmul(scores[:, e, :], q_ring[:, j % RQ, h, :], k_mem[:, h, :], start=True, stop=True)
                        continue
                    rows = slice(64 * e, 64 * e + 64)
                    q = q_ring[rows, j % RQ, u, :]
                    kk = u if kind == "A" else 0
                    if has_prev(j):
                        pe.matmul(scores[:, e, 0:P], q, k_ring[rows, (j - 1) % RK, kk, :], start=True, stop=True)
                    ins = pe.matmul(scores[:, e, P:256], q, k_ring[rows, j % RK, kk, :], start=True, stop=True)
                ins.then_inc(scored, 1)

            def turn_probs(n):
                j = UNITS[n][0]
                if KIND[j] == "A":
                    pe.wait_ge(exp_done, n + 1)
                else:
                    pe.wait_ge(prob_done, count_bm(n) + 1)
                if n >= 1:
                    pe.wait_ge(prob_copied, n)
                for e in range(2):
                    for b in range(0 if has_prev(j) else 1, 2):
                        ins = pe.transpose(prob_turn[:, e, b, :], prob[:, n % 2, e, b * P:(b + 1) * P], ident[:])
                ins.then_inc(prob_turned, 1)

            def weigh_values(n):
                j, u = UNITS[n]
                kind = KIND[j]
                pe.wait_ge(prob_copied, n + 1)
                if n >= 1:
                    pe.wait_ge(o_done, n)
                used = merges_before(*slot_of(min(n + 2, NU - 1)))
                if used:
                    pe.wait_ge(factor_used, used)
                if kind != "M":
                    pe.wait_ge(v_done, count(V_KINDS, j + 1))
                first = 0 if has_prev(j) else 1
                for e in range(2):
                    for b in range(first, 2):
                        if kind == "M":
                            h = 2 * u + e
                            v = v_mem[:, b, h * P:(h + 1) * P]
                            dst = ps[:, OB, e * P:(e + 1) * P]
                        else:
                            c = 64 * (2 * u + e if kind == "A" else e)
                            v = v_ring[:, (j - 1 + b) % RK, c:c + 64]
                            dst = ps[64 * e:64 * e + 64, OB, 0:P]
                        ins = pe.matmul(dst, v, prob_t[:, n % 2, e, b, :], start=(b == first), stop=(b == 1))
                ins.then_inc(pv_done, 1)

            def turn_factors(m, j):
                pair, half, g = merge_batch(m)
                pe.wait_ge(o_done, units_scored(*MERGE_AT[m]) - 2)
                if m:
                    pe.wait_ge(factor_used, m)
                pe.wait_ge(spread_done, m + 1)
                for i in range(4):
                    ins = pe.transpose(ps[:, OB, i * P:(i + 1) * P], square[:, i * P:(i + 1) * P], ident[:])
                ins.then_inc(factor_turned, 1)

            n = 0
            for j in range(NJ + LAG + 1):
                for k in range(8):
                    if j < NJ:
                        project(j, k)
                    if k in step_slices(j):
                        score(n)
                        if n >= 1:
                            turn_probs(n - 1)
                        if n >= 2:
                            weigh_values(n - 2)
                        n += 1
                    if k in (3, 4) and pair_of(j):
                        turn_x(pair_of(j)[k - 3])
                    if k == turn_slices(j)[0] and 0 <= j - 1 < NJ:
                        if j <= 4:
                            pe.wait_ge(x_gained, min(2 * j + 3, NX))
                        turn(j - 1, 0)
                    if k == turn_slices(j)[1] and 0 <= j - 1 < NJ:
                        turn(j - 1, 1)
                    if (j, k) in MERGE_AT:
                        turn_factors(MERGE_AT.index((j, k)), j)
            turn_probs(NU - 1)
            weigh_values(NU - 2)
            weigh_values(NU - 1)


def gated_outputs(nc, w_gate, b_gate, w_o_a, w_o_b, w_o_m, ps, act_hi, act_lo, attn_out, merged):
    NK = act_hi.shape[1]
    BR = 3
    BRANCH_TILES = [(0, 2), (6, 4), (2, 4)]
    O_SLOT = [0, 2, 6]
    UN = 2 * BR
    with ExitStack() as ctx:
        def sb(name, shape, dt=F32):
            return ctx.enter_context(nc.sbuf_tensor(name, shape, dt))

        def sem(name):
            return ctx.enter_context(nc.semaphore(name))

        g_raw = sb("g_raw", [P, BR, NK, P])
        g_hi = sb("g_hi", [P, BR, NK, P], F32R)
        g_lo = sb("g_lo", [P, BR, NK, P], F32R)
        o_raw = sb("o_raw", [P, 10, P])
        o_w = sb("o_w", [P, 10, P])
        bias = sb("gate_bias", [P, 2 * BR * NK])
        gate = sb("gate", [P, 2, 512])
        g_in = [sem(f"g_in{b}") for b in range(BR)]
        g_hi_done = [sem(f"g_hi_done{b}") for b in range(BR)]
        g_lo_done = [sem(f"g_lo_done{b}") for b in range(BR)]
        g_used = [sem(f"g_used{b}") for b in range(BR)]
        o_in, o_copied, bias_in = sem("o_in"), sem("o_copied"), sem("bias_in")
        gate_summed, out_summed, gate_done, weighed, added = (
            sem(n) for n in ("gate_summed", "out_summed", "gate_done", "weighed", "added"))
        block = ctx.enter_context(nc.Block())

        @block.sync
        def _(sp):
            with nc.allow_non_contiguous_dma(reason="one bias per partition"):
                for half in range(2):
                    sp.dma_start(bias[:, half * BR * NK:(half + 1) * BR * NK], b_gate[0].rearrange("(k p) -> p k", p=P)
                                 ).then_inc(bias_in, 16)

            def load_tile(f):
                cols = bass.ds(f * P, P)
                for b in range(BR):
                    sp.wait_ge(g_lo_done[b], f)
                    sp.dma_start(g_raw[:, b], w_gate[0].rearrange("(k p) n -> p k n", p=P)[:, :, bass.ds(f * P + b * NK * P, P)]
                                 ).then_inc(g_in[b], 16)
                sp.wait_ge(o_copied, f)
                sp.dma_start(o_raw[:, 0:2], w_o_a[0].rearrange("(k p) n -> p k n", p=P)[:, :, cols]).then_inc(o_in, 16)
                for e in range(2):
                    sp.dma_start(o_raw[64 * e:64 * e + 64, 2:6],
                                 w_o_b[0].rearrange("(e j d) n -> e d j n", e=2, d=64)[e][:, :, cols]).then_inc(o_in, 16)
                sp.dma_start(o_raw[:, 6:10], w_o_m[0].rearrange("(k p) n -> p k n", p=P)[:, :, cols]).then_inc(o_in, 16)

            load_tile(0)
            with sp.Fori(1, NK) as f:
                load_tile(f)

        @block.scalar
        def _(act):
            def cast(f, b):
                act.wait_ge(g_in[b], 16 * (f + 1))
                act.wait_ge(g_used[b], f)
                act.activation(g_hi[:, b], g_raw[:, b], ACT.Copy).then_inc(g_hi_done[b], 1)

            def copy_weights(f):
                act.wait_ge(o_in, 64 * (f + 1))
                act.wait_ge(out_summed, UN * f)
                act.activation(o_w[:], o_raw[:], ACT.Copy).then_inc(o_copied, 1)

            def tile(f, first, last):
                for b in range(BR):
                    for half in range(2):
                        u = 2 * b + half
                        act.wait_ge(gate_summed, UN * f + u + 1)
                        if not first or u >= 2:
                            act.wait_ge(added, UN * f + u - 1)
                        column = f + (half * BR + b) * NK
                        column = column if isinstance(f, int) else act.snap(column)
                        act.activation(gate[:, u % 2, :], ps[:, 2 * (u % 3), :], ACT.Sigmoid,
                                       bias=bias[:, bass.ds(column, 1)]).then_inc(gate_done, 1)
                    if not last:
                        cast(f + 1, b)
                if not last:
                    copy_weights(f + 1)

            for b in range(BR):
                cast(0, b)
            copy_weights(0)
            act.wait_ge(bias_in, 32)
            tile(0, True, False)
            with act.Fori(1, NK - 1) as f:
                tile(f, False, False)
            tile(NK - 1, False, True)

        @block.gpsimd
        def _(pool):
            with pool.Fori(0, NK) as f:
                for b in range(BR):
                    pool.wait_ge(g_hi_done[b], f + 1)
                    pool.tensor_tensor(g_lo[:, b], g_raw[:, b], g_hi[:, b].bitcast(F32), ALU.subtract).then_inc(g_lo_done[b], 1)

        @block.vector
        def _(dve):
            def tile(f, first):
                for u in range(UN):
                    b, half = u // 2, u % 2
                    at = UN * f + u
                    dve.wait_ge(gate_done, at + 1)
                    dve.wait_ge(out_summed, at + 1)
                    dve.tensor_tensor(gate[:, u % 2, :], ps[:, 2 * (u % 3) + 1, :], gate[:, u % 2, :], ALU.mult).then_inc(weighed, 1)
                    dve.wait_ge(weighed, at + 1)
                    dst = merged[:, bass.ds(f, 1), half * 512:(half + 1) * 512]
                    src = gate[:, u % 2:u % 2 + 1, :]
                    if b == 0:
                        dve.tensor_copy(dst, src).then_inc(added, 1)
                    else:
                        dve.wait_ge(added, at - 1)
                        dve.tensor_tensor(dst, dst, src, ALU.add).then_inc(added, 1)

            with dve.Fori(0, NK) as f:
                tile(f, False)

        @block.tensor
        def _(pe):
            def tile(f, first):
                for u in range(UN):
                    b, half = u // 2, u % 2
                    at = UN * f + u
                    cols = slice(half * 512, (half + 1) * 512)
                    if half == 0:
                        pe.wait_ge(g_lo_done[b], f + 1)
                    if not first or u >= 3:
                        pe.wait_ge(weighed, at - 2)
                    for k in range(NK):
                        for i, (w, a) in enumerate(((g_hi, act_hi), (g_hi, act_lo), (g_lo, act_hi))):
                            ins = pe.matmul(ps[:, 2 * (u % 3), :], w[:, b, k, :], a[:, k, cols],
                                            start=(k == 0 and i == 0), stop=(k == NK - 1 and i == 2))
                    ins.then_inc(gate_summed, 1)
                    if half == 1:
                        pe.wait_ge(gate_summed, at + 1)
                        pe.nop().then_inc(g_used[b], 1)
                    if u == 0:
                        pe.wait_ge(o_copied, f + 1)
                    t0, tiles = BRANCH_TILES[b]
                    for i in range(tiles):
                        ins = pe.matmul(ps[:, 2 * (u % 3) + 1, :], o_w[:, O_SLOT[b] + i, :], attn_out[:, t0 + i, cols],
                                        start=(i == 0), stop=(i == tiles - 1))
                    ins.then_inc(out_summed, 1)

            tile(0, True)
            with pe.Fori(1, NK) as f:
                tile(f, False)


def output_projection(nc, x_t, w_out, ffn_norm, ps, act_hi, act_lo, ident, half_power, merged, x1):
    NT, NK, D = x1.shape[1], act_hi.shape[1], x1.shape[2]
    NRAW_O = 3
    with ExitStack() as ctx:
        def sb(name, shape, dt=F32):
            return ctx.enter_context(nc.sbuf_tensor(name, shape, dt))

        def sem(name):
            return ctx.enter_context(nc.semaphore(name))

        wo_hi = sb("wo_hi", [P, 2, NK, 512], F32R)
        wo_lo = sb("wo_lo", [P, 2, NK, 512], F32R)
        wo_raw = sb("wo_raw", [P, NRAW_O, 512])
        gain = sb("ffn_gain", [P, NK])
        sums = sb("x1_sums", [P, NT])
        rstd = sb("x1_rstd", [P, NT])
        wo_in = [sem(f"wo_in{n}") for n in range(NRAW_O)]
        res_in = [sem(f"res_in{t}") for t in range(NT // 2)]
        gain_in, wo_hi_done, wo_lo_done, m_hi, m_lo = (sem(n) for n in ("gain_in", "wo_hi_done", "wo_lo_done", "m_hi", "m_lo"))
        out_done, x1_done, x1_sq, x1_ms, x1_rs, x1_scaled, x1_turned, x1_gained, h_hi, h_lo = (
            sem(n) for n in ("out_done", "x1_done", "x1_sq", "x1_ms", "x1_rs", "x1_scaled", "x1_turned", "x1_gained", "h_hi", "h_lo"))
        NS = 2 * NK

        def turned(t):
            return ps[:, 4 + 2 * (t % 2):6 + 2 * (t % 2), :].rearrange("p b n -> p (b n)")

        block = ctx.enter_context(nc.Block())

        @block.sync
        def _(sp):
            for n in range(NS):
                half, k = n // NK, n % NK
                if n >= NRAW_O:
                    sp.wait_ge(wo_lo_done, n - NRAW_O + 1)
                sp.dma_start(wo_raw[:, n % NRAW_O, :], w_out[0, k * P:(k + 1) * P, half * 512:(half + 1) * 512]
                             ).then_inc(wo_in[n % NRAW_O], 16)
                if half:
                    sp.dma_start(x1[:, k, :], x_t[k]).then_inc(res_in[k // 2], 16)
            with nc.allow_non_contiguous_dma(reason="one gain per partition"):
                sp.dma_start(gain[:, :], ffn_norm[0].rearrange("(k p) -> p k", p=P)).then_inc(gain_in, 16)

        @block.scalar
        def _(act):
            for n in range(NS):
                if n < NK:
                    act.activation(act_hi[:, n, :], merged[:, n, :], ACT.Copy).then_inc(m_hi, 1)
                act.wait_ge(wo_in[n % NRAW_O], 16 * (n // NRAW_O + 1))
                act.activation(wo_hi[:, n // NK, n % NK, :], wo_raw[:, n % NRAW_O, :], ACT.Copy).then_inc(wo_hi_done, 1)

            def high(t):
                act.wait_ge(x1_gained, t + 1)
                act.activation(act_hi[:, :, t * P:(t + 1) * P], merged[:, t, :].rearrange("p (k n) -> p k n", n=P),
                               ACT.Copy).then_inc(h_hi, 1)

            for t in range(NT):
                if t == 0:
                    act.wait_ge(m_lo, NK)
                act.wait_ge(x1_done, 2 * (t + 1))
                act.activation(merged[:, t, :], x1[:, t, :], ACT.Square, accum_out=sums[:, t:t + 1]).then_inc(x1_sq, 1)
                if t >= 1:
                    high(t - 1)
            high(NT - 1)

        @block.gpsimd
        def _(pool):
            for n in range(NS):
                pool.wait_ge(wo_hi_done, n + 1)
                pool.tensor_tensor(wo_lo[:, n // NK, n % NK, :], wo_raw[:, n % NRAW_O, :],
                                   wo_hi[:, n // NK, n % NK, :].bitcast(F32), ALU.subtract).then_inc(wo_lo_done, 1)

            def low(t):
                pool.wait_ge(h_hi, t + 1)
                pool.tensor_tensor(act_lo[:, :, t * P:(t + 1) * P], merged[:, t, :].rearrange("p (k n) -> p k n", n=P),
                                   act_hi[:, :, t * P:(t + 1) * P].bitcast(F32), ALU.subtract).then_inc(h_lo, 1)

            for t in range(NT):
                pool.wait_ge(x1_sq, t + 1)
                pool.tensor_scalar(rstd[:, t:t + 1], sums[:, t:t + 1], 1.0 / D, EPS, ALU.mult, ALU.add).then_inc(x1_ms, 1)
                pool.wait_ge(x1_ms, t + 1)
                pool.tensor_tensor(rstd[:, t:t + 1], rstd[:, t:t + 1], half_power[:, 0:1], ALU.pow).then_inc(x1_rs, 1)
                if t >= 1:
                    low(t - 1)
            low(NT - 1)

        @block.vector
        def _(dve):
            def gained(t):
                dve.wait_ge(x1_turned, t + 1)
                dve.tensor_tensor(merged[:, t, :].rearrange("p (k n) -> p k n", n=P),
                                  turned(t).rearrange("p (k n) -> p k n", n=P),
                                  gain[:].unsqueeze(2).to_broadcast([P, NK, P]), ALU.mult).then_inc(x1_gained, 1)

            for k in range(NK):
                dve.wait_ge(m_hi, k + 1)
                dve.tensor_tensor(act_lo[:, k, :], merged[:, k, :], act_hi[:, k, :].bitcast(F32), ALU.subtract).then_inc(m_lo, 1)
            dve.wait_ge(gain_in, 16)
            for t in range(NT):
                dve.wait_ge(res_in[t // 2], 32)
                for half in range(2):
                    n = 2 * t + half
                    dve.wait_ge(out_done, n + 1)
                    dst = x1[:, t, half * 512:(half + 1) * 512]
                    dve.tensor_tensor(dst, ps[:, n % 4, :], dst, ALU.add).then_inc(x1_done, 1)
                if t >= 1:
                    gained(t - 1)
                dve.wait_ge(x1_rs, t + 1)
                dve.tensor_scalar(merged[:, t, :], x1[:, t, :], rstd[:, t:t + 1], None, ALU.mult).then_inc(x1_scaled, 1)
            gained(NT - 1)

        @block.tensor
        def _(pe):
            def turn(t):
                pe.wait_ge(x1_scaled, t + 1)
                if t >= 2:
                    pe.wait_ge(x1_gained, t - 1)
                for k in range(NK):
                    ins = pe.transpose(turned(t)[:, k * P:(k + 1) * P], merged[:, t, k * P:(k + 1) * P], ident[:])
                ins.then_inc(x1_turned, 1)

            for t in range(NT):
                for half in range(2):
                    n = 2 * t + half
                    if n >= 4:
                        pe.wait_ge(x1_done, n - 3)
                    for k in range(NK):
                        if t == 0:
                            if half == 0:
                                pe.wait_ge(m_lo, k + 1)
                            pe.wait_ge(wo_lo_done, NK * half + k + 1)
                        for i, (a, w) in enumerate(((act_hi, wo_hi), (act_hi, wo_lo), (act_lo, wo_hi))):
                            ins = pe.matmul(ps[:, n % 4, :], a[:, k, t * P:(t + 1) * P], w[:, half, k, :],
                                            start=(k == 0 and i == 0), stop=(k == NK - 1 and i == 2))
                    ins.then_inc(out_done, 1)
                if t >= 1:
                    turn(t - 1)
            turn(NT - 1)


def feed_forward(nc, w_up, conv_w, conv_b, w_down, out_t, ps, act_hi, act_lo, ident, x1, spare):
    NK, S, NT = act_hi.shape[1], act_hi.shape[2], x1.shape[1]
    FF = w_down.shape[1]
    FT = FF // P
    NC = FT // 2
    YN = 2 * NT
    with ExitStack() as ctx:
        def sb(name, shape, dt=F32):
            return ctx.enter_context(nc.sbuf_tensor(name, shape, dt))

        def sem(name):
            return ctx.enter_context(nc.semaphore(name))

        f_raw = sb("f_raw", [P, 6, 1024])
        f_hi = sb("f_hi", [P, 6, 1024], F32R)
        f_lo = sb("f_lo", [P, 6, 1024], F32R)
        z_hi = sb("z_hi", [P, 2, S], F32R)
        z_lo = sb("z_lo", [P, 2, S], F32R)
        conv0 = sb("conv0", [P, 2, S])
        conv = [conv0[:, :, :], spare]
        taps = sb("taps", [P, 4, 2 * FT])
        taps_raw = conv0[0:2 * FT, 0, 0:4 * P].rearrange("p (j n) -> p j n", j=4)

        taps_in, taps_turned, taps_ready = sem("taps_in"), sem("taps_turned"), sem("taps_ready")
        f_in = [sem(f"f_in{b}") for b in range(6)]
        f_hi_done = [sem(f"f_hi_done{b}") for b in range(6)]
        f_lo_done = [sem(f"f_lo_done{b}") for b in range(6)]
        u_done = [sem(f"u_done{q}") for q in range(4)]
        tap2_done = [sem(f"tap2_done{q}") for q in range(4)]
        tap1_done = [sem(f"tap1_done{q}") for q in range(4)]
        tap0_done = [sem(f"tap0_done{q}") for q in range(4)]
        silu_done = [sem(f"silu_done{p}") for p in range(2)]
        z_done = [sem(f"z_done{p}") for p in range(2)]
        z_hi_done = [sem(f"z_hi_done{p}") for p in range(2)]
        z_lo_done = [sem(f"z_lo_done{p}") for p in range(2)]
        y_done, y_added, stored = sem("y_done"), sem("y_added"), sem("stored")

        def up_psum(q):
            return ps[:, 2 * q:2 * q + 2, :].rearrange("p b n -> p (b n)")

        block = ctx.enter_context(nc.Block())

        @block.sync
        def _(sp):
            for j in range(3):
                sp.dma_start(taps_raw[:, j, :], conv_w[0, j].rearrange("(t n) -> t n", n=P)).then_inc(taps_in, 16)
            sp.dma_start(taps_raw[:, 3, :], conv_b[0].rearrange("(t n) -> t n", n=P)).then_inc(taps_in, 16)

            def load(b, c):
                sp.wait_ge(f_lo_done[b], c)
                if b < 4:
                    col = (2 * c + b // 2) * P + (b % 2) * FF
                    sp.dma_start(f_raw[:, b, :].rearrange("p (k n) -> p k n", n=P),
                                 w_up[0].rearrange("(k p) n -> p k n", p=P)[:, :, bass.ds(col, P)]).then_inc(f_in[b], 16)
                else:
                    sp.dma_start(f_raw[:, b, :], w_down[0, bass.ds((2 * c + b - 4) * P, P), :]).then_inc(f_in[b], 16)

            def chunk(c, down, more):
                if down:
                    load(4, c - 1)
                    load(5, c - 1)
                load(2, c)
                load(3, c)
                if more:
                    load(0, c + 1)
                    load(1, c + 1)

            load(0, 0)
            load(1, 0)
            chunk(0, False, True)
            chunk(1, True, True)
            with sp.Fori(2, NC - 1) as c:
                chunk(c, True, True)
            chunk(NC - 1, True, False)
            load(4, NC - 1)
            load(5, NC - 1)
            for t in range(NT):
                sp.wait_ge(y_added, YN * (NC - 1) + 2 * t + 2)
                sp.dma_start(out_t[t], x1[:, t, :]).then_inc(stored, 16)
            sp.wait_ge(stored, 16 * NT)

        @block.gpsimd
        def _(pool):
            def low(b, c):
                pool.wait_ge(f_hi_done[b], c + 1)
                pool.tensor_tensor(f_lo[:, b, :], f_raw[:, b, :], f_hi[:, b, :].bitcast(F32), ALU.subtract).then_inc(f_lo_done[b], 1)

            def z_low(p, c):
                pool.wait_ge(z_hi_done[p], c + 1)
                pool.tensor_tensor(z_lo[:, p, :], conv[p][:, 0, :], z_hi[:, p, :].bitcast(F32), ALU.subtract).then_inc(z_lo_done[p], 1)

            def chunk(c, down, more):
                if down:
                    z_low(1, c - 1)
                    low(4, c - 1)
                    low(5, c - 1)
                low(2, c)
                low(3, c)
                if more:
                    low(0, c + 1)
                    low(1, c + 1)
                z_low(0, c)

            low(0, 0)
            low(1, 0)
            chunk(0, False, True)
            with pool.Fori(1, NC - 1) as c:
                chunk(c, True, True)
            chunk(NC - 1, True, False)
            z_low(1, NC - 1)
            low(4, NC - 1)
            low(5, NC - 1)

        @block.scalar
        def _(act):
            def high(b, c):
                act.wait_ge(f_in[b], 16 * (c + 1))
                if b < 4:
                    act.wait_ge(u_done[b], c)
                else:
                    act.wait_ge(y_done, YN * c)
                act.activation(f_hi[:, b, :], f_raw[:, b, :], ACT.Copy).then_inc(f_hi_done[b], 1)

            def own_tap(p, c):
                for e in range(2):
                    q = 2 * p + e
                    act.wait_ge(u_done[q], c + 1)
                    if e == 0:
                        act.wait_ge(z_lo_done[p], c)
                    feature = 2 * c + p + e * FT if isinstance(c, int) else act.snap(2 * c + p + e * FT)
                    act.activation(conv[p][:, e, :], up_psum(q), ACT.Identity, scale=taps[:, 2, bass.ds(feature, 1)],
                                   bias=taps[:, 3, bass.ds(feature, 1)]).then_inc(tap2_done[q], 1)
                act.wait_ge(tap0_done[2 * p], c + 1)
                act.activation(conv[p][:, 0, :], conv[p][:, 0, :], ACT.Silu).then_inc(silu_done[p], 1)

            def z_high(p, c):
                act.wait_ge(z_done[p], c + 1)
                act.wait_ge(y_done, YN * c)
                act.activation(z_hi[:, p, :], conv[p][:, 0, :], ACT.Copy).then_inc(z_hi_done[p], 1)

            def chunk(c, down, more):
                if down:
                    own_tap(1, c - 1)
                    z_high(1, c - 1)
                    high(4, c - 1)
                    high(5, c - 1)
                high(2, c)
                high(3, c)
                own_tap(0, c)
                if more:
                    high(0, c + 1)
                    high(1, c + 1)
                z_high(0, c)

            high(0, 0)
            high(1, 0)
            act.wait_ge(taps_turned, 1)
            act.activation(taps[:].rearrange("p j n -> p (j n)"), ps[:, 7, 0:8 * FT], ACT.Copy).then_inc(taps_ready, 1)
            act.wait_ge(taps_ready, 1)
            chunk(0, False, True)
            chunk(1, True, True)
            with act.Fori(2, NC - 1) as c:
                chunk(c, True, True)
            chunk(NC - 1, True, False)
            own_tap(1, NC - 1)
            z_high(1, NC - 1)
            high(4, NC - 1)
            high(5, NC - 1)

        @block.vector
        def _(dve):
            def other_taps(q, c):
                p, e = q // 2, q % 2
                dst = conv[p][:, e, :]
                feature = 2 * c + p + e * FT
                dve.wait_ge(tap2_done[q], c + 1)
                dve.scalar_tensor_tensor(out=dst[:, 1:S], in0=up_psum(q)[:, 0:S - 1], scalar=taps[:, 1, bass.ds(feature, 1)],
                                         in1=dst[:, 1:S], op0=ALU.mult, op1=ALU.add).then_inc(tap1_done[q], 1)
                dve.wait_ge(tap1_done[q], c + 1)
                dve.scalar_tensor_tensor(out=dst[:, 2:S], in0=up_psum(q)[:, 0:S - 2], scalar=taps[:, 0, bass.ds(feature, 1)],
                                         in1=dst[:, 2:S], op0=ALU.mult, op1=ALU.add).then_inc(tap0_done[q], 1)

            def product(p, c):
                dve.wait_ge(silu_done[p], c + 1)
                dve.wait_ge(tap0_done[2 * p + 1], c + 1)
                dve.tensor_tensor(conv[p][:, 0, :], conv[p][:, 0, :], conv[p][:, 1, :], ALU.mult).then_inc(z_done[p], 1)

            def add(i, c):
                dst = x1[:, i // 2, (i % 2) * 512:(i % 2 + 1) * 512]
                dve.wait_ge(y_done, YN * c + i + 1)
                dve.tensor_tensor(dst, ps[:, 4 + i % 4, :], dst, ALU.add).then_inc(y_added, 1)

            def chunk(c, down):
                if down:
                    other_taps(2, c - 1)
                    other_taps(3, c - 1)
                    product(1, c - 1)
                other_taps(0, c)
                if down:
                    add(0, c - 1)
                other_taps(1, c)
                if down:
                    for i in range(1, 4):
                        add(i, c - 1)
                product(0, c)
                if down:
                    for i in range(4, YN):
                        add(i, c - 1)
                    dve.wait_ge(y_added, YN * c)

            chunk(0, False)
            chunk(1, True)
            with dve.Fori(2, NC) as c:
                chunk(c, True)
            other_taps(2, NC - 1)
            other_taps(3, NC - 1)
            product(1, NC - 1)
            for i in range(YN):
                add(i, NC - 1)

        @block.tensor
        def _(pe):
            def up(q, c, first):
                pe.wait_ge(f_lo_done[q], c + 1)
                if q < 2:
                    pe.wait_ge(tap0_done[q], c)
                elif not first and q == 2:
                    pe.wait_ge(y_added, YN * c)
                for half in range(2):
                    for k in range(NK):
                        for i, (w, a) in enumerate(((f_hi, act_hi), (f_hi, act_lo), (f_lo, act_hi))):
                            ins = pe.matmul(ps[:, 2 * q + half, :], w[:, q, k * P:(k + 1) * P],
                                            a[:, k, half * 512:(half + 1) * 512],
                                            start=(k == 0 and i == 0), stop=(k == NK - 1 and i == 2))
                ins.then_inc(u_done[q], 1)

            def down(c):
                for p in range(2):
                    pe.wait_ge(z_lo_done[p], c + 1)
                    pe.wait_ge(f_lo_done[4 + p], c + 1)
                    pe.wait_ge(tap0_done[2 + p], c + 1)
                for i in range(YN):
                    t, half = i // 2, i % 2
                    if i >= 4:
                        pe.wait_ge(y_added, YN * c + i - 3)
                    for p in range(2):
                        for m, (z, w) in enumerate(((z_hi, f_hi), (z_hi, f_lo), (z_lo, f_hi))):
                            ins = pe.matmul(ps[:, 4 + i % 4, :], z[:, p, t * P:(t + 1) * P],
                                            w[:, 4 + p, half * 512:(half + 1) * 512],
                                            start=(p == 0 and m == 0), stop=(p == 1 and m == 2))
                    ins.then_inc(y_done, 1)

            pe.wait_ge(taps_in, 64)
            for j in range(4):
                ins = pe.transpose(ps[:, 7, j * 2 * FT:(j + 1) * 2 * FT], taps_raw[:, j, :], ident[0:2 * FT, 0:2 * FT])
            ins.then_inc(taps_turned, 1)
            up(0, 0, True)
            up(1, 0, True)
            pe.wait_ge(taps_ready, 1)
            up(2, 0, True)
            up(3, 0, True)
            with pe.Fori(1, NC) as c:
                up(0, c, False)
                up(1, c, False)
                down(c - 1)
                up(2, c, False)
                up(3, c, False)
            down(NC - 1)


_INS = ['x', 'mem', 'positions', 'attn_norm', 'w_in', 'a_q_norm', 'a_k_norm', 'b_q_norm', 'b_k_norm', 'b_sinks',
        'mem_norm', 'w_mem_kv', 'm_q_norm', 'm_k_norm', 'w_o_a', 'w_o_b', 'w_o_m', 'w_gate', 'b_gate', 'w_out',
        'ffn_norm', 'w_up', 'conv_w', 'conv_b', 'w_down']
_OUTS = [((1, 1024, 1024), 'float32')]


def kernel(**inputs):
    import numpy as _np
    import concourse.bacc as _bacc
    from concourse import mybir as _mybir
    from concourse.bass_utils import run_bass_kernel_spmd as _run

    nc = _bacc.Bacc("TRN2", target_bir_lowering=False, num_devices=1)
    arrays, args = {}, []
    for name in _INS:
        a = _np.ascontiguousarray(inputs[name])
        arrays[f"in_{name}_dram"] = a
        args.append(nc.dram_tensor(f"in_{name}_dram", a.shape, _mybir.dt.from_np(a.dtype), kind="ExternalInput").ap())
    for i, (shape, dtype) in enumerate(_OUTS):
        dt = _mybir.dt.from_np(_np.dtype(dtype))
        args.append(nc.dram_tensor(f"out_{i}_dram", shape, dt, kind="ExternalOutput").ap())
    layer(nc, *args)
    r = _run(nc, [arrays], core_ids=[0])
    return r.results[0]["out_0_dram"]
```

```python
import math
from contextlib import ExitStack

import concourse.bass as bass
import numpy as np
from concourse import mybir

F32 = mybir.dt.float32
F32R = mybir.dt.float32r
I32 = mybir.dt.int32
ALU = mybir.AluOpType
ACT = mybir.ActivationFunctionType
AX = mybir.AxisListType

P = 128
EPS = 1e-6
MASKED = 1e30
START_MIN = 3e38
ROPE_THETA = 500000.0
ROT = 16
HALF = ROT // 2

STAGES = [
    ("memk", 0, 0, 0, 512, 0, 2),
    ("memv", 0, 0, 512, 512, 0, 2),
    ("A", 0, 0, 0, 512, 256, 8),
    ("A", 1, 1, 768, 512, 256, 8),
    ("A", 2, 2, 1536, 512, 256, 8),
    ("B", 0, 0, 2304, 512, 256, 8),
    ("M", 0, 0, 3072, 512, 0, 8),
]
JOBS = [(s, t) for s, st in enumerate(STAGES) for t in range(st[6])]
KIND = [STAGES[s][0] for s, _ in JOBS]
NJ = len(JOBS)
UNITS_OF = {"memk": 0, "memv": 0, "A": 2, "B": 4, "M": 2}
UNITS = [(j, u) for j in range(NJ) for u in range(UNITS_OF[KIND[j]])]
NU = len(UNITS)
LAG = 2
RQ, RK = 3, 4
BATCHES = {"memk": 1, "memv": 0, "A": 1, "B": 2, "M": 1}


def count(kinds, upto):
    return sum(k in kinds for k in KIND[:max(upto, 0)])


QK_KINDS = ("memk", "A", "B", "M")
V_KINDS = ("memv", "A", "B")
HAS_Q = ("A", "B", "M")
HAS_K = ("memk", "A", "B")


def batches(upto):
    return sum(BATCHES[k] for k in KIND[:max(upto, 0)])


def units_before(j):
    return sum(UNITS_OF[k] for k in KIND[:max(j, 0)])


def raw_slot(n):
    if n < 8:
        first, places = 0, (0, 1, 6, 7, 8, 9, 10, 11)
    elif n < 24:
        first, places = 8, (0, 1, 2, 3)
    elif n < 48:
        first, places = 24, (0, 1, 8, 9, 10, 11)
    else:
        first, places = 48, (0, 1, 4, 6)
    return places[(n - first) % len(places)]


def raw_group(n):
    place = raw_slot(n)
    if n < 8:
        return n
    return place if place < 4 else 2 + place % 4


def raw_before(n):
    return next((m for m in range(n - 1, -1, -1) if raw_group(m) == raw_group(n)), None)


def raw_uses(n):
    return sum(raw_group(m) == raw_group(n) for m in range(n + 1))


def has_prev(j):
    s, t = JOBS[j]
    kind, order = STAGES[s][:2]
    if kind == "M":
        return True
    return t > 0 if order == 0 else (t % 2 == 1 if order == 1 else False)


def step_slices(j):
    n = UNITS_OF[KIND[j - LAG]] if 0 <= j - LAG < NJ else 0
    return {0: [], 2: [1, 4], 4: [0, 2, 4, 6]}[n]


TURN_AT = (5, 7)


def slot_of(n):
    j, u = UNITS[n]
    return j + LAG, step_slices(j + LAG)[u]


def units_scored(slot, k):
    return sum(slot_of(n) <= (slot, k) for n in range(NU))


def token_tile(ap, order, tile):
    if order == 0:
        return ap[:, tile * P:(tile + 1) * P]
    if order == 1:
        return ap.rearrange("p (b i r) -> p r b i", b=2, r=4)[:, tile // 2, tile % 2, :]
    return ap.rearrange("p (i t) -> p t i", t=8)[:, tile]


def layer(nc, x, mem, positions, attn_norm, w_in, a_q_norm, a_k_norm, b_q_norm, b_k_norm, b_sinks,
          mem_norm, w_mem_kv, m_q_norm, m_k_norm, w_o_a, w_o_b, w_o_m, w_gate, b_gate, w_out,
          ffn_norm, w_up, conv_w, conv_b, w_down, out):
    S, D = x.shape[1], x.shape[2]
    NT, NK = S // P, D // P
    FF = w_down.shape[1]
    x_t = x[0].rearrange("(t p) d -> t p d", p=P)
    mem_t = mem[0].rearrange("(t p) d -> t p d", p=P)
    out_t = out[0].rearrange("(t p) d -> t p d", p=P)

    stats_dram = [nc.dram_tensor(f"stats_{g}", (S, 8), F32, kind="Internal").ap() for g in (1, 2)]

    with ExitStack() as whole:
        def sb(name, shape, dt=F32, ctx=whole):
            return ctx.enter_context(nc.sbuf_tensor(name, shape, dt))

        def sem(name):
            return whole.enter_context(nc.semaphore(name))

        ps = whole.enter_context(nc.psum_tensor("ps", [P, 8, 512], F32))
        act_hi = sb("act_hi", [P, NK, S], F32R)
        act_lo = sb("act_lo", [P, NK, S], F32R)
        ident = sb("ident", [P, P])
        ident_ready = sem("ident_ready")
        half_power = sb("half_power", [P, 16])

        attn_out = sb("attn_out", [P, 10, S])
        w_raw = sb("w_raw", [P, 2, 768])
        first_gate = w_raw[:].rearrange("p a n -> p (a n)")[:, 0:NK * P].rearrange("p (k n) -> p k n", n=P)
        wo_raw = w_raw[:].rearrange("p a n -> p (a n)").rearrange("p (a n) -> p a n", n=512)
        first_gate_in = sem("g_in0")
        x1, spare = attn_out[:, 0:NT, :], attn_out[:, NT:NT + 2, :]

        input_projections(nc, x_t, mem_t, positions, attn_norm, w_in, a_q_norm, a_k_norm, b_q_norm,
                          b_k_norm, b_sinks, mem_norm, w_mem_kv, m_q_norm, m_k_norm, w_gate, w_raw, first_gate,
                          first_gate_in, stats_dram, ps, act_hi, act_lo, ident, ident_ready, half_power, attn_out)
        with ExitStack() as middle:
            merged = sb("merged", [P, NK, S], ctx=middle)
            taps = sb("taps", [P, 4, 2 * FF // P], ctx=middle)
            conv0, f_raw = merged[:, 0:2, :], [merged[:, 2 + b, :] for b in range(6)]
            f_in = [sem(f"f_in{b}") for b in range(6)]
            wo_in = [sem(f"wo_in{n}") for n in range(NRAW_O)]
            gated_outputs(nc, w_gate, b_gate, w_o_a, w_o_b, w_o_m, w_out, ps, act_hi, act_lo, attn_out, merged,
                          first_gate, first_gate_in, wo_raw, wo_in)
            output_projection(nc, x_t, w_out, ffn_norm, conv_w, conv_b, w_up, ps, act_hi, act_lo, ident, half_power,
                              merged, x1, spare, wo_raw, wo_in, taps, f_raw, f_in)
            feed_forward(nc, w_up, w_down, out_t, ps, act_hi, act_lo, x1, [conv0, spare], taps, f_raw, f_in)


NRAW_O = 3


def load_w_out(sp, w_out, wo_raw, wo_in, n):
    NK = w_out.shape[1] // P
    half, k = n // NK, n % NK
    sp.dma_start(wo_raw[:, n % NRAW_O, :], w_out[0, k * P:(k + 1) * P, half * 512:(half + 1) * 512]
                 ).then_inc(wo_in[n % NRAW_O], 16)


def load_w_up(sp, w_up, dst, b, c, f_in):
    col = (2 * c + b // 2) * P + (b % 2) * w_up.shape[2] // 2
    sp.dma_start(dst.rearrange("p (k n) -> p k n", n=P),
                 w_up[0].rearrange("(k p) n -> p k n", p=P)[:, :, bass.ds(col, P)]).then_inc(f_in[b], 16)


def input_projections(nc, x_t, mem_t, positions, attn_norm, w_in, a_q_norm, a_k_norm, b_q_norm, b_k_norm,
                      b_sinks, mem_norm, w_mem_kv, m_q_norm, m_k_norm, w_gate, w_raw, first_gate, first_gate_in, stats_dram, ps, act_hi, act_lo,
                      ident, ident_ready, half_power, attn_out):
    NK, S = act_hi.shape[1], act_hi.shape[2]
    NX = 10
    inv_d = 1.0 / (NK * P)
    with ExitStack() as ctx:
        def sb(name, shape, dt=F32):
            return ctx.enter_context(nc.sbuf_tensor(name, shape, dt))

        def sem(name):
            return ctx.enter_context(nc.semaphore(name))

        w_hi = sb("w_hi", [P, NK, 768], F32R)
        w_lo = sb("w_lo", [P, NK, 768], F32R)
        k_mem = sb("k_mem", [P, 4, 256])
        v_mem = sb("v_mem", [P, 2, 512])
        masks = sb("masks", [P, 4, P])
        rope_cos = sb("rope_cos", [P, 3, 8, ROT])
        rope_sin = sb("rope_sin", [P, 3, 8, ROT])
        gains = sb("gains", [P, 768])
        norm_gain = sb("norm_gain", [P, 2, NK])
        neg_sink = sb("neg_sink", [P, 8])
        row_sums = sb("row_sums", [P, 16])
        row_rstd = sb("row_rstd", [P, 16])
        stats = sb("stats", [P, 3, 8, 8])
        with ExitStack() as early:
            mem_hi = early.enter_context(nc.sbuf_tensor("mem_hi", [P, NK, 256], F32R))
            mem_lo = early.enter_context(nc.sbuf_tensor("mem_lo", [P, NK, 256], F32R))
        q_ring = sb("q_ring", [P, RQ, 4, P])
        k_ring = sb("k_ring", [P, RK, 2, P])
        v_ring = sb("v_ring", [P, RK, 256])
        prob = sb("prob", [P, 2, 2, 256])
        prob_t = sb("prob_t", [P, 2, 2, 2, P])
        square = sb("square", [P, 640])
        qk = sb("qk", [P, 2, 640])
        rope_a = sb("rope_a", [P, 10, ROT])
        rope_b = sb("rope_b", [P, 10, ROT])
        head_ss = sb("head_ss", [P, 2, 10])
        head_rstd = sb("head_rstd", [P, 2, 10])
        small = sb("small", [P, 2, 12])
        parity = sb("parity", [P, 2])
        pos_i = sb("pos_i", [P, 3, 8], I32)
        pos_f = sb("pos_f", [P, 3, 8])
        angle = prob[:, 1, :, :].rearrange("p a b -> p (a b)")[:, 0:384].rearrange("p (s n) -> p s n", s=2)
        turns = prob_t[:, 0, :, :, :].rearrange("p e b n -> p (e b n)")[:, 0:384].rearrange("p (s n) -> p s n", s=2)
        merge = {n: sb(f"merge_{n}", [P, w]) for n, w in
                 (("max", 32), ("e", 96), ("total", 32), ("f", 96))}

        mem_in = [sem(f"mem_in{n}") for n in range(2)]
        x_in = [sem(f"x_in{n}") for n in range(4)]
        const_in = sem("const_in")
        masks_built = sem("masks_built")
        gain_in, gain_turned, gain_ready = sem("gain_in"), sem("gain_turned"), sem("gain_ready")
        x_sq, x_rstd, x_scaled, x_turned, x_gained, x_hi, x_lo_even, x_lo_odd = (
            sem(n) for n in ("x_sq", "x_rstd", "x_scaled", "x_turned", "x_gained", "x_hi", "x_lo_even", "x_lo_odd"))
        angles_ready, sines_ready, rope_ready = sem("angles_ready"), sem("sines_ready"), sem("rope_ready")
        sink_ready = sem("sink_ready")
        raw_in = [sem(f"raw_in{n}") for n in range(8)]
        w_hi_done, w_lo_even, w_lo_odd, w_used = (sem(n) for n in ("w_hi_done", "w_lo_even", "w_lo_odd", "w_used"))
        proj_done, sq_done, ss_done, rstd_done, normed, roped = (
            sem(n) for n in ("proj_done", "sq_done", "ss_done", "rstd_done", "normed", "roped"))
        v_done, turned, q_done, k_done = (sem(n) for n in ("v_done", "turned", "q_done", "k_done"))
        scored, min_done, exp_done, prob_done, prob_turned, prob_copied, pv_done, o_done, sink_gap, sink_exp = (
            sem(n) for n in ("scored", "min_done", "exp_done", "prob_done", "prob_turned", "prob_copied",
                             "pv_done", "o_done", "sink_gap", "sink_exp"))
        spread_done = sem("spread_done")
        stats_out, stats_in, shift_ready, shift_exp, factors_ready, factor_turned, factor_used = (
            sem(n) for n in ("stats_out", "stats_in", "shift_ready", "shift_exp", "factors_ready",
                             "factor_turned", "factor_used"))
        group_added = sem("group_added")
        dve_chain, act_chain, pool_chain = sem("dve_chain"), sem("act_chain"), sem("pool_chain")

        TQ, SC, PT, OB = 4, 5, 6, 7

        def proj_a(j):
            return ps[:, 2 * (j % 2), :]

        def proj_b(j):
            return ps[:, 2 * (j % 2) + 1, 0:256]

        def wide(n):
            return ps[:, 4 + 2 * (n % 2):6 + 2 * (n % 2), :].rearrange("p b n -> p (b n)")

        scores = ps[:, TQ:SC + 1, 0:256]
        prob_turn = ps[:, PT, :].rearrange("p (e b n) -> p e b n", e=2, b=2)

        last_job_of = {s: max(j for j in range(NJ) if JOBS[j][0] == s) for s in range(len(STAGES))}
        merge_from = next(j for j in range(NJ) if KIND[j] == "B") + 2
        MERGE_AT = [(merge_from + 1 + m // 2, (3, 5)[m % 2]) for m in range(12)]

        def merges_before(slot, k):
            return sum(at < (slot, k) for at in MERGE_AT)

        def merge_batch(m):
            return m // 6, (m // 3) % 2, m % 3

        x_slot = [attn_out[:, n, :] for n in range(NX)]
        gain_rows = square[0:2 * NK, 0:P]
        squares_junk = square[:, :].bitcast(mybir.dt.bfloat16)[:, 0:NK * P]

        def raw(n):
            return w_raw[:, raw_slot(n), :] if raw_slot(n) < 2 else attn_out[:, raw_slot(n) - 2, :]

        def x_split(eng, n):
            eng.wait_ge(x_lo_even, (n + 1) // 2)
            eng.wait_ge(x_lo_odd, n // 2)

        X_SLOTS = (0, 2, 4, 5)

        def pair_of(slot):
            return (2 * X_SLOTS.index(slot) + 2, 2 * X_SLOTS.index(slot) + 3) if slot in X_SLOTS else ()

        def slot_of_x(n):
            return X_SLOTS[(n - 2) // 2] if n >= 2 else -1

        def x_low(eng, n):
            eng.wait_ge(x_hi, n + 1)
            hi, lo, c = (mem_hi, mem_lo, n) if n < 2 else (act_hi, act_lo, n - 2)
            eng.tensor_tensor(lo[:, :, c * P:(c + 1) * P], x_slot[n].rearrange("p (k n) -> p k n", n=P),
                              hi[:, :, c * P:(c + 1) * P].bitcast(F32), ALU.subtract
                              ).then_inc(x_lo_odd if n % 2 else x_lo_even, 1)

        def w_split(eng, n):
            eng.wait_ge(w_lo_odd if n % 2 else w_lo_even, n // 2 + 1)

        def w_low(eng, n):
            na, nb = STAGES[n // 8][4:6]
            eng.wait_ge(w_hi_done, n + 1)
            eng.tensor_tensor(w_lo[:, n % 8, 0:na + nb], raw(n)[:, 0:na + nb],
                              w_hi[:, n % 8, 0:na + nb].bitcast(F32), ALU.subtract
                              ).then_inc(w_lo_odd if n % 2 else w_lo_even, 1)

        def v_wait(eng, j):
            before = units_before(j - RK + 2)
            if before:
                eng.wait_ge(pv_done, before)

        def count_b(n):
            return sum(KIND[j] == "B" for j, _ in UNITS[:n])

        def count_bm(n):
            return sum(KIND[j] != "A" for j, _ in UNITS[:n])

        def unit_stats(n, e):
            j, u = UNITS[n]
            s, t = JOBS[j]
            if KIND[j] == "A":
                g = STAGES[s][2]
                h = 2 * u + e
                return stats[:, g, t, h:h + 1], stats[:, g, t, 4 + h:5 + h]
            return small[:, n % 2, e:e + 1], small[:, n % 2, 2 + e:3 + e]

        block = ctx.enter_context(nc.Block())

        @block.sync
        def _(sp):
            for n in range(2):
                sp.dma_start(x_slot[n], mem_t[n]).then_inc(mem_in[n], 16)
            sp.dma_start(gain_rows[0:NK, :], attn_norm[0].rearrange("(k p) -> k p", p=P)).then_inc(gain_in, 16)
            sp.dma_start(gain_rows[NK:2 * NK, :], mem_norm[0].rearrange("(k p) -> k p", p=P)).then_inc(gain_in, 16)

            def load_x(m):
                for n in (m, m + 1):
                    sp.dma_start(x_slot[n], x_t[n - 2]).then_inc(x_in[m // 2 - 1], 16)

            def load_constants():
                with nc.allow_non_contiguous_dma(reason="positions and gains, once"):
                    p0 = positions[0]
                    sp.dma_start(pos_i[:, 0, :], p0.rearrange("(t p) -> p t", p=P)).then_inc(const_in, 16)
                    for b in range(2):
                        sp.dma_start(pos_i[:, 1, :].rearrange("p (r b) -> p b r", b=2)[:, b],
                                      p0.rearrange("(b i r) -> b i r", b=2, r=4)[b]).then_inc(const_in, 16)
                    sp.dma_start(pos_i[:, 2, :], p0.rearrange("(i t) -> i t", t=8)).then_inc(const_in, 16)
                    for off, src in ((0, a_q_norm[0].rearrange("g d -> (g d)")), (192, a_k_norm[0].rearrange("g d -> (g d)")),
                                     (384, b_q_norm[0]), (448, b_k_norm[0]), (512, m_q_norm[0]), (640, m_k_norm[0])):
                        sp.dma_start(gains[:, off:off + src.shape[0]], src.partition_broadcast(P)).then_inc(const_in, 16)
                    sp.dma_start(neg_sink[:, :], b_sinks[0].partition_broadcast(P)).then_inc(const_in, 16)

            def reorder_stats():
                last_a1 = units_before(last_job_of[3] + 1)
                last_a2 = units_before(last_job_of[4] + 1)
                sp.wait_ge(exp_done, last_a1)
                for b in range(2):
                    sp.dma_start(stats_dram[0].rearrange("(b i r) c -> b i r c", b=2, r=4)[b],
                                 stats[:, 1].rearrange("p (r b) c -> p b r c", b=2)[:, b]).then_inc(stats_out, 16)
                sp.wait_ge(exp_done, last_a2)
                sp.dma_start(stats_dram[1].rearrange("(i t) c -> i t c", t=8), stats[:, 2]).then_inc(stats_out, 16)
                sp.wait_ge(stats_out, 48)
                for g in range(2):
                    sp.dma_start(stats[:, 1 + g], stats_dram[g].rearrange("(t p) c -> p t c", p=P)).then_inc(stats_in, 16)

            for n in range(8 * len(STAGES)):
                kind, _, _, col, na, nb, _ = STAGES[n // 8]
                src = w_mem_kv if kind in ("memk", "memv") else w_in
                k = n % 8
                if n == 8 * 6:
                    reorder_stats()
                if raw_before(n) is not None:
                    w_split(sp, raw_before(n))
                if n == 8 + 2:
                    x_split(sp, 2)
                if n == 4:
                    load_x(2)
                if n == 8:
                    for m in (4, 6, 8):
                        w_split(sp, m - 2)
                        w_split(sp, m - 1)
                        load_x(m)
                    load_constants()
                if n == 24 + 2:
                    x_split(sp, NX)
                if n == 48 + 2:
                    sp.wait_ge(group_added, 4)
                sp.dma_start(raw(n)[:, 0:na + nb],
                             src[0, k * P:(k + 1) * P, col:col + na + nb]).then_inc(raw_in[raw_group(n)], 16)
            for place in range(2):
                w_split(sp, max(n for n in range(8 * len(STAGES)) if raw_slot(n) == place))
            sp.dma_start(first_gate, w_gate[0].rearrange("(k p) n -> p k n", p=P)[:, :, 0:P]).then_inc(first_gate_in, 16)

        @block.gpsimd
        def _(pool):
            chain = [0]

            def link(ins):
                chain[0] += 1
                ins.then_inc(pool_chain, 1)
                pool.wait_ge(pool_chain, chain[0])

            link(pool.memset(ident[:], 0.0))
            pool.affine_select(out=ident[:], in_=ident[:], compare_op=ALU.not_equal, fill=1.0, base=0,
                               pattern=[[-1, P]], channel_multiplier=1).then_inc(ident_ready, 1)
            link(pool.memset(half_power[:], -0.5))
            link(pool.memset(masks[:], 0.0))
            for m, sign, base in ((0, 1, -1), (1, 1, 0), (2, -1, 0), (3, -1, 0)):
                link(pool.affine_select(out=masks[:, m, :], in_=masks[:, m, :], compare_op=ALU.is_ge, fill=MASKED,
                                        base=base, pattern=[[sign, P]], channel_multiplier=-sign))
            link(pool.memset(prob[:, 1, 1, 0:64], 0.0))
            pool.affine_select(out=prob[:, 1, 1, 0:64], in_=prob[:, 1, 1, 0:64], compare_op=ALU.not_equal, fill=MASKED,
                               base=0, pattern=[[-2, 64]], channel_multiplier=1).then_inc(masks_built, 1)

            def x_rms(n):
                pool.wait_ge(x_sq, n + 1)
                link(pool.tensor_scalar(row_rstd[:, n:n + 1], row_sums[:, n:n + 1], inv_d, EPS, ALU.mult, ALU.add))
                pool.tensor_tensor(row_rstd[:, n:n + 1], row_rstd[:, n:n + 1], half_power[:, 0:1],
                                   ALU.pow).then_inc(x_rstd, 1)

            for n in (0, 1):
                x_rms(n)
            x_low(pool, 0)

            def norm_and_rope(j):
                s, t = JOBS[j]
                kind, order, g = STAGES[s][:3]
                if kind not in QK_KINDS:
                    return
                i = count(QK_KINDS, j)
                nh, dh = {"memk": (4, 128), "A": (8, 64), "B": (10, 64), "M": (4, 128)}[kind]
                pool.wait_ge(ss_done, i + 1)
                link(pool.tensor_scalar(head_rstd[:, i % 2, 0:nh], head_ss[:, i % 2, 0:nh], 1.0 / dh, EPS,
                                        ALU.mult, ALU.add))
                pool.tensor_tensor(head_rstd[:, i % 2, 0:nh], head_rstd[:, i % 2, 0:nh], half_power[:, 0:nh],
                                   ALU.pow).then_inc(rstd_done, 1)
                buf = qk[:, i % 2, 0:nh * dh].rearrange("p (h d) -> p h d", d=dh)
                pool.wait_ge(normed, i + 1)
                if i == 0:
                    pool.wait_ge(const_in, 16 * 11)
                parts = {"memk": ((0, 4, 640),), "A": ((0, 4, 64 * g), (4, 8, 192 + 64 * g)),
                         "B": ((0, 8, 384), (8, 10, 448)), "M": ((0, 4, 512),)}[kind]
                for h0, h1, off in parts:
                    ins = pool.tensor_tensor(buf[:, h0:h1, :], buf[:, h0:h1, :],
                                             gains[:, off:off + dh].unsqueeze(1).to_broadcast([P, h1 - h0, dh]), ALU.mult)
                    if dh == 64 or (h0, h1, off) != parts[-1]:
                        link(ins)
                if dh == 128:
                    ins.then_inc(roped, 1)
                    return
                if kind == "A" and g == 0 and t == 0:
                    pool.wait_ge(rope_ready, 1)
                cos = rope_cos[:, order, t, :].unsqueeze(1).to_broadcast([P, nh, ROT])
                sin = rope_sin[:, order, t, :].unsqueeze(1)
                link(pool.tensor_tensor(rope_a[:, 0:nh, :], buf[:, :, 0:ROT], cos, ALU.mult))
                link(pool.tensor_tensor(rope_b[:, 0:nh, 0:HALF], buf[:, :, HALF:ROT],
                                        sin[:, :, 0:HALF].to_broadcast([P, nh, HALF]), ALU.mult))
                link(pool.tensor_tensor(rope_b[:, 0:nh, HALF:ROT], buf[:, :, 0:HALF],
                                        sin[:, :, HALF:ROT].to_broadcast([P, nh, HALF]), ALU.mult))
                pool.tensor_tensor(buf[:, :, 0:ROT], rope_a[:, 0:nh, :], rope_b[:, 0:nh, :],
                                   ALU.add).then_inc(roped, 1)

            for k in range(0, 8, 2):
                w_low(pool, k)
            for n in pair_of(0):
                x_rms(n)
            for j in range(NJ + LAG + 1):
                for n in pair_of(j + 1):
                    x_rms(n)
                if 0 <= j - 1 < NJ:
                    norm_and_rope(j - 1)
                for n in pair_of(j)[:1]:
                    x_low(pool, n)
                for s in last_job_of:
                    if last_job_of[s] == j and s + 1 < len(STAGES):
                        for k in range(0, 8, 2):
                            w_low(pool, 8 * (s + 1) + k)

        @block.scalar
        def _(act):
            def x_high(n):
                act.wait_ge(x_gained, n + 1)
                hi, c = (mem_hi, n) if n < 2 else (act_hi, n - 2)
                act.activation(hi[:, :, c * P:(c + 1) * P], x_slot[n].rearrange("p (k n) -> p k n", n=P),
                               ACT.Copy).then_inc(x_hi, 1)

            chain = [0]

            def link(ins):
                chain[0] += 1
                ins.then_inc(act_chain, 1)
                act.wait_ge(act_chain, chain[0])

            def x_square(n):
                if n < 2:
                    act.wait_ge(mem_in[n], 16)
                else:
                    act.wait_ge(x_in[n // 2 - 1], 32)
                if n >= 1:
                    act.wait_ge(x_sq, n)
                before = count(QK_KINDS, slot_of_x(n) - 1)
                if before:
                    act.wait_ge(ss_done, before)
                act.activation(squares_junk, x_slot[n], ACT.Square, accum_out=row_sums[:, n:n + 1]).then_inc(x_sq, 1)

            def sines():
                act.wait_ge(angles_ready, 1)
                act.activation(turns[:, :, :], angle[:, :, :], ACT.Sin).then_inc(sines_ready, 1)

            def cast_slice(n):
                _, _, _, col, na, nb, _ = STAGES[n // 8]
                act.wait_ge(raw_in[raw_group(n)], 16 * raw_uses(n))
                if n >= 8:
                    act.wait_ge(w_used, n - 7)
                act.activation(w_hi[:, n % 8, 0:na + nb], raw(n)[:, 0:na + nb], ACT.Copy).then_inc(w_hi_done, 1)

            def squares(j):
                kind = KIND[j]
                act.wait_ge(proj_done, j + 1)
                if kind in QK_KINDS:
                    i = count(QK_KINDS, j)
                    if i >= 1:
                        act.wait_ge(ss_done, i)
                    spreads = merges_before(j + 1, 0)
                    if spreads:
                        act.wait_ge(factor_turned, spreads)
                    if j <= X_SLOTS[-1]:
                        act.wait_ge(x_sq, 2 + 2 * sum(slot <= j + 1 for slot in X_SLOTS))
                    ins = act.activation(square[:, 0:512], proj_a(j), ACT.Square)
                    if kind == "B":
                        ins = act.activation(square[:, 512:640], proj_b(j)[:, 0:128], ACT.Square)
                    ins.then_inc(sq_done, 1)
                    if kind == "B":
                        act.wait_ge(sq_done, i + 1)
                if kind in V_KINDS:
                    t = JOBS[j][1]
                    if kind == "memv":
                        ins = act.activation(v_mem[:, t, :], proj_a(j), ACT.Copy)
                    else:
                        v_wait(act, j)
                        c0 = 0 if kind == "A" else 128
                        ins = act.activation(v_ring[:, j % RK, 0:256 - c0], proj_b(j)[:, c0:256], ACT.Copy)
                    ins.then_inc(v_done, 1)

            def copy_q(j):
                kind = KIND[j]
                if kind not in HAS_Q:
                    return
                act.wait_ge(turned, batches(j) + 1)
                before = units_before(j - RQ + 1)
                if before:
                    act.wait_ge(scored, before)
                nb = 2 if kind == "A" else 4
                scale = -(1.0 / math.sqrt(128 if kind == "M" else 64))
                act.activation(q_ring[:, j % RQ, 0:nb, :], ps[:, TQ, :].rearrange("p (b n) -> p b n", n=P)[:, 0:nb, :],
                               ACT.Copy, scale=scale).then_inc(q_done, 1)

            def exps(n):
                j, u = UNITS[n]
                kind, (s, t) = KIND[j], JOBS[j]
                act.wait_ge(min_done, n + 1)
                c0 = 0 if has_prev(j) else P
                for e in range(2):
                    low, total = unit_stats(n, e)
                    src = scores[:, e, :] if kind == "M" else prob[:, n % 2, e, c0:256]
                    if kind == "M" and n >= 2 and e == 0:
                        act.wait_ge(prob_turned, n - 1)
                    ins = act.activation(prob[:, n % 2, e, c0:256], src, ACT.Exp, bias=low, scale=-1.0, accum_out=total)
                    if e == 0:
                        link(ins)
                ins.then_inc(exp_done, 1)
                if kind == "B":
                    b = count_b(n)
                    act.wait_ge(sink_gap, b + 1)
                    act.activation(small[:, n % 2, 4:6], small[:, n % 2, 4:6], ACT.Exp).then_inc(sink_exp, 1)

            def copy_probs(n):
                c0 = 0 if has_prev(UNITS[n][0]) else 1
                act.wait_ge(prob_turned, n + 1)
                if n >= 2:
                    act.wait_ge(pv_done, n - 1)
                act.activation(prob_t[:, n % 2, :, c0:2, :], prob_turn[:, :, c0:2, :], ACT.Copy).then_inc(prob_copied, 1)

            def spread_factors(m, j):
                pair, half, g = merge_batch(m)
                if m == 0:
                    act.wait_ge(factors_ready, 1)
                else:
                    act.wait_ge(factor_turned, m)
                act.wait_ge(ss_done, count(QK_KINDS, j))
                f = merge["f"][:].rearrange("p (g t h) -> p g t h", g=3, h=4)
                act.activation(square[:, 0:512].rearrange("p (t e d) -> p t e d", t=4, e=2),
                               f[:, g, 4 * half:4 * half + 4, 2 * pair:2 * pair + 2].unsqueeze(3).to_broadcast([P, 4, 2, 64]),
                               ACT.Copy).then_inc(spread_done, 1)

            act.wait_ge(gain_turned, 1)
            act.activation(norm_gain[:].rearrange("p a k -> p (a k)"), ps[:, OB, 0:2 * NK], ACT.Copy).then_inc(gain_ready, 1)
            for n in (0, 1):
                x_square(n)
            for n in (0, 1):
                x_high(n)
            for k in range(8):
                cast_slice(k)
            for n in pair_of(0):
                x_square(n)
            n = 0
            for j in range(NJ + LAG + 1):
                if 0 <= j - 1 < NJ:
                    squares(j - 1)
                for m in pair_of(j + 1):
                    x_square(m)
                for k in range(8):
                    if k in step_slices(j):
                        exps(n)
                        if n >= 1:
                            copy_probs(n - 1)
                        n += 1
                    if k == 4:
                        for m in pair_of(j):
                            x_high(m)
                    if k == TURN_AT[0] and 0 <= j - 1 < NJ:
                        copy_q(j - 1)
                    if j in last_job_of.values() and JOBS[j][0] + 1 < len(STAGES):
                        cast_slice(8 * (JOBS[j][0] + 1) + k)
                    if (j, k) in MERGE_AT:
                        spread_factors(MERGE_AT.index((j, k)), j)
                if j == 4:
                    sines()
                if j == merge_from:
                    act.wait_ge(shift_ready, 1)
                    act.activation(merge["e"][:], merge["e"][:], ACT.Exp).then_inc(shift_exp, 1)
            copy_probs(NU - 1)

        @block.vector
        def _(dve):
            chain = [0]

            def link(ins):
                chain[0] += 1
                ins.then_inc(dve_chain, 1)
                dve.wait_ge(dve_chain, chain[0])

            def x_scale(n):
                dve.wait_ge(x_rstd, n + 1)
                dve.tensor_scalar(x_slot[n], x_slot[n], row_rstd[:, n:n + 1], None, ALU.mult).then_inc(x_scaled, 1)

            def x_gain(n):
                dve.wait_ge(x_turned, n + 1)
                if n == 0:
                    dve.wait_ge(gain_ready, 1)
                g = norm_gain[:, 1 if n < 2 else 0, :].unsqueeze(2).to_broadcast([P, NK, P])
                dve.tensor_tensor(x_slot[n].rearrange("p (k n) -> p k n", n=P),
                                  wide(n).rearrange("p (k n) -> p k n", n=P), g, ALU.mult).then_inc(x_gained, 1)

            def angles():
                dve.wait_ge(const_in, 16 * 11)
                link(dve.tensor_scalar(neg_sink[:, :], neg_sink[:, :], -1.0, None, ALU.mult))
                dve.wait_ge(masks_built, 1)
                link(dve.tensor_reduce(parity[:, 1:2], prob[:, 1, 1, 0:64], AX.X, ALU.add))
                link(dve.tensor_scalar(parity[:, 0:1], parity[:, 1:2], -1.0, MASKED, ALU.mult, ALU.add))
                own = masks[:, 3, :].rearrange("p (i h) -> p h i", h=2)
                for h in range(2):
                    ins = dve.tensor_scalar(own[:, h, :], own[:, h, :], parity[:, h:h + 1], None, ALU.max)
                    if h == 0:
                        link(ins)
                link(ins)

                link(dve.tensor_copy(pos_f[:], pos_i[:]))
                freqs = np.exp(np.arange(HALF, dtype=np.float32) * np.float32(-2.0 * math.log(ROPE_THETA) / ROT))
                cosine = angle[:, 0, :].rearrange("p (o f) -> p o f", f=HALF)
                sine = angle[:, 1, :].rearrange("p (o f) -> p o f", f=HALF)
                for f in range(HALF):
                    for part in (cosine, sine):
                        ins = dve.tensor_scalar(part[:, :, f], pos_f[:].rearrange("p o t -> p (o t)"), float(freqs[f]), None, ALU.mult)
                        link(ins)

            def reduce_angles():
                magic = 1.5 * 2.0 ** 23
                two_pi = 2.0 * math.pi
                part1 = 6.28125
                part2 = 507.0 / 262144.0
                part3 = two_pi - part1 - part2
                link(dve.tensor_scalar(turns[:, 0, :], angle[:, 0, :], 1.0 / two_pi, 0.25, ALU.mult, ALU.add))
                link(dve.tensor_scalar(turns[:, 0, :], turns[:, 0, :], magic, None, ALU.add))
                link(dve.tensor_scalar(turns[:, 1, :], angle[:, 1, :], 1.0 / two_pi, magic, ALU.mult, ALU.add))
                link(dve.tensor_scalar(turns[:, :, :], turns[:, :, :], -magic, None, ALU.add))
                for part in (part1, part2, part3):
                    link(dve.scalar_tensor_tensor(out=angle[:, :, :], in0=turns[:, :, :], scalar=-part, in1=angle[:, :, :],
                                                  op0=ALU.mult, op1=ALU.add))
                link(dve.tensor_scalar(angle[:, 0, :], angle[:, 0, :], math.pi / 2, None, ALU.add))
                dve.tensor_scalar(angle[:, :, :], angle[:, :, :], 3.1415925, -3.1415925, ALU.min, ALU.max).then_inc(angles_ready, 1)

            def rope_tables():
                dve.wait_ge(sines_ready, 1)
                cos_v = turns[:, 0, :].rearrange("p (o f) -> p o f", f=HALF)
                sin_v = turns[:, 1, :].rearrange("p (o f) -> p o f", f=HALF)
                rc = rope_cos[:].rearrange("p o t f -> p (o t) f")
                rs = rope_sin[:].rearrange("p o t f -> p (o t) f")
                link(dve.tensor_copy(rc[:, :, 0:HALF], cos_v))
                link(dve.tensor_copy(rc[:, :, HALF:ROT], cos_v))
                link(dve.tensor_scalar(rs[:, :, 0:HALF], sin_v, -1.0, None, ALU.mult))
                dve.tensor_copy(rs[:, :, HALF:ROT], sin_v).then_inc(rope_ready, 1)
                dve.wait_ge(rope_ready, 1)

            def sum_squares(j):
                kind = KIND[j]
                if kind not in QK_KINDS:
                    return
                i = count(QK_KINDS, j)
                nh, dh = {"memk": (4, 128), "A": (8, 64), "B": (10, 64), "M": (4, 128)}[kind]
                dve.wait_ge(sq_done, i + 1)
                if i >= 2:
                    dve.wait_ge(rstd_done, i - 1)
                dve.tensor_reduce(head_ss[:, i % 2, 0:nh], square[:, 0:nh * dh].rearrange("p (h d) -> p h d", d=dh),
                                  AX.X, ALU.add).then_inc(ss_done, 1)

            def normalise(j):
                kind = KIND[j]
                if kind not in QK_KINDS:
                    return
                i = count(QK_KINDS, j)
                nh, dh = {"memk": (4, 128), "A": (8, 64), "B": (10, 64), "M": (4, 128)}[kind]
                dve.wait_ge(rstd_done, i + 1)
                if i >= 2:
                    dve.wait_ge(turned, batches(qk_job(i - 1)))
                na = min(nh * dh, 512)
                rstd = head_rstd[:, i % 2, 0:nh].unsqueeze(2).to_broadcast([P, nh, dh])
                buf = qk[:, i % 2, 0:nh * dh].rearrange("p (h d) -> p h d", d=dh)
                ha = na // dh
                if kind == "B":
                    dve.wait_ge(v_done, count(V_KINDS, j + 1))
                    link(dve.tensor_tensor(buf[:, 0:ha, :].rearrange("p (u e) d -> p e u d", e=2),
                                           proj_a(j).rearrange("p (e u d) -> p e u d", e=2, d=dh),
                                           head_rstd[:, i % 2, 0:ha].rearrange("p (e u) -> p e u", e=2).unsqueeze(3)
                                           .to_broadcast([P, 2, 4, dh]), ALU.mult))
                else:
                    ins = dve.tensor_tensor(buf[:, 0:ha, :], proj_a(j).rearrange("p (h d) -> p h d", d=dh), rstd[:, 0:ha, :], ALU.mult)
                if kind == "B":
                    ins = dve.tensor_tensor(buf[:, ha:nh, :], proj_b(j)[:, 0:P].rearrange("p (h d) -> p h d", d=dh),
                                            rstd[:, ha:nh, :], ALU.mult)
                ins.then_inc(normed, 1)

            def qk_job(i):
                return [j for j in range(NJ) if KIND[j] in QK_KINDS][i]

            def copy_k(j):
                kind, t = KIND[j], JOBS[j][1]
                if kind not in HAS_K:
                    return
                dve.wait_ge(turned, batches(j + 1))
                if kind in HAS_Q:
                    dve.wait_ge(q_done, count(HAS_Q, j + 1))
                bank = ps[:, TQ, :].rearrange("p (b n) -> p b n", n=P)
                if kind == "memk":
                    ins = dve.tensor_copy(k_mem[:, :, t * P:(t + 1) * P], bank)
                else:
                    v_wait(dve, j)
                    if kind == "A":
                        ins = dve.tensor_copy(k_ring[:, j % RK, :, :], bank[:, 2:4, :])
                    else:
                        ins = dve.tensor_copy(k_ring[:, j % RK, 0, :], bank[:, 0, :])
                ins.then_inc(k_done, 1)

            def minima(n):
                j, u = UNITS[n]
                kind, (s, t) = KIND[j], JOBS[j]
                order = STAGES[s][1]
                dve.wait_ge(scored, n + 1)
                if n >= 2:
                    dve.wait_ge(prob_turned, n - 1)
                if kind == "M":
                    dve.tensor_reduce(small[:, n % 2, 0:2], scores, AX.X, ALU.min).then_inc(min_done, 1)
                    return
                c0 = 0 if has_prev(j) else P
                mask = (masks[:, 3:4, :] if order == 2 else masks[:, 2:3, :] if c0 else
                        masks[:, 1:3, :] if kind == "A" else masks[:, 0:3:2, :])
                for e in range(2):
                    low, _ = unit_stats(n, e)
                    start = START_MIN if kind == "A" else neg_sink[:, u + 4 * e:u + 4 * e + 1]
                    ins = dve.tensor_tensor_reduce(prob[:, n % 2, e, c0:256].rearrange("p (b n) -> p b n", n=P),
                                                   scores[:, e, c0:256].rearrange("p (b n) -> p b n", n=P), mask, 1.0, start,
                                                   ALU.add, ALU.min, low)
                    if e == 0:
                        link(ins)
                ins.then_inc(min_done, 1)
                if kind == "B":
                    dve.wait_ge(min_done, n + 1)
                    dve.tensor_tensor(small[:, n % 2, 4:6], small[:, n % 2, 0:2], neg_sink[:, u:u + 5:4],
                                      ALU.subtract).then_inc(sink_gap, 1)

            def divide(n):
                j, u = UNITS[n]
                kind = KIND[j]
                if kind == "A":
                    return
                dve.wait_ge(exp_done, n + 1)
                total = small[:, n % 2, 2:4]
                if kind == "B":
                    dve.wait_ge(sink_exp, count_b(n) + 1)
                    link(dve.tensor_tensor(small[:, n % 2, 6:8], total, small[:, n % 2, 4:6], ALU.add))
                    total = small[:, n % 2, 6:8]
                link(dve.reciprocal(small[:, n % 2, 8:10], total))
                c0 = 0 if has_prev(j) else P
                for e in range(2):
                    ins = dve.tensor_scalar(prob[:, n % 2, e, c0:256], prob[:, n % 2, e, c0:256],
                                            small[:, n % 2, 8 + e:9 + e], None, ALU.mult)
                    if e == 0:
                        link(ins)
                ins.then_inc(prob_done, 1)

            def copy_out(n):
                j, u = UNITS[n]
                kind, (s, t) = KIND[j], JOBS[j]
                dve.wait_ge(pv_done, n + 1)
                if kind == "M":
                    dst = attn_out[:, 2 + 2 * u:4 + 2 * u, t * P:(t + 1) * P]
                    src = ps[:, OB, 0:256].rearrange("p (e n) -> p e n", e=2)
                else:
                    base = 2 * STAGES[s][2] if kind == "A" else 6
                    dst = attn_out[:, base + u, t * P:(t + 1) * P]
                    src = ps[:, OB, 0:P]
                dve.tensor_copy(dst, src).then_inc(o_done, 1)

            def merge_factors():
                dve.wait_ge(stats_in, 32)
                lows = [stats[:, g, :, 0:4] for g in range(3)]
                sums = [stats[:, g, :, 4:8] for g in range(3)]
                mx = merge["max"][:].rearrange("p (t h) -> p t h", h=4)
                e = merge["e"][:].rearrange("p (g t h) -> p g t h", g=3, h=4)
                f = merge["f"][:].rearrange("p (g t h) -> p g t h", g=3, h=4)
                total = merge["total"][:].rearrange("p (t h) -> p t h", h=4)
                link(dve.tensor_tensor(mx, lows[0], lows[1], ALU.min))
                link(dve.tensor_tensor(mx, mx, lows[2], ALU.min))
                for g in range(3):
                    ins = dve.tensor_tensor(e[:, g], mx, lows[g], ALU.subtract)
                    if g < 2:
                        link(ins)
                ins.then_inc(shift_ready, 1)
                dve.wait_ge(shift_exp, 1)
                for g in range(3):
                    link(dve.tensor_tensor(f[:, g], e[:, g], sums[g], ALU.mult))
                link(dve.tensor_tensor(total, f[:, 0], f[:, 1], ALU.add))
                link(dve.tensor_tensor(total, total, f[:, 2], ALU.add))
                link(dve.reciprocal(total, total))
                for g in range(3):
                    ins = dve.tensor_tensor(f[:, g], e[:, g], total, ALU.mult)
                    if g < 2:
                        link(ins)
                ins.then_inc(factors_ready, 1)

            def merge_use(m):
                pair, half, g = merge_batch(m)
                dve.wait_ge(factor_turned, m + 1)
                dst = attn_out[:, pair, half * 512:(half + 1) * 512]
                bank = ps[:, OB, :]
                if g == 0:
                    dve.tensor_tensor(dst, bank, dst, ALU.mult).then_inc(factor_used, 1)
                    dve.wait_ge(factor_used, m + 1)
                    return
                src = attn_out[:, 2 * g + pair, :]
                if g == 1:
                    src = src.rearrange("p (r b i) -> p b i r", r=4, b=2)[:, half]
                    bank, dst = (a.rearrange("p (i r) -> p i r", r=4) for a in (bank, dst))
                else:
                    src = src.rearrange("p (t i) -> p i t", t=8)[:, half * 64:(half + 1) * 64]
                    bank, dst = (a.rearrange("p (i t) -> p i t", t=8) for a in (bank, dst))
                dve.tensor_tensor(src, bank, src, ALU.mult).then_inc(factor_used, 1)
                dve.wait_ge(factor_used, m + 1)
                dve.tensor_tensor(dst, dst, src, ALU.add).then_inc(group_added, 1)
                dve.wait_ge(group_added, 2 * (m // 3) + g)

            for n in (0, 1):
                x_scale(n)
            for n in (0, 1):
                x_gain(n)
            x_low(dve, 1)
            for k in range(1, 8, 2):
                w_low(dve, k)
            for n in pair_of(0):
                x_scale(n)
            n = 0
            for j in range(NJ + LAG + 1):
                if 0 <= j - 1 < NJ:
                    sum_squares(j - 1)
                    if 0 not in step_slices(j):
                        normalise(j - 1)
                for m in pair_of(j + 1):
                    x_scale(m)
                for m in pair_of(j):
                    x_gain(m)
                for m in pair_of(j)[1:]:
                    x_low(dve, m)
                for k in range(8):
                    if k in step_slices(j):
                        minima(n)
                        divide(n)
                        if n >= 2:
                            copy_out(n - 2)
                        n += 1
                    if k == 0 and 0 in step_slices(j) and 0 <= j - 1 < NJ:
                        normalise(j - 1)
                    if 0 <= j - 1 < NJ and k == TURN_AT[KIND[j - 1] == "B"]:
                        copy_k(j - 1)
                    if k % 2 and j in last_job_of.values() and JOBS[j][0] + 1 < len(STAGES):
                        w_low(dve, 8 * (JOBS[j][0] + 1) + k)
                    if (j, k) in MERGE_AT:
                        merge_use(MERGE_AT.index((j, k)))
                if j == 1:
                    angles()
                if j == 4:
                    reduce_angles()
                    rope_tables()
                if j == merge_from:
                    merge_factors()
            copy_out(NU - 2)
            copy_out(NU - 1)

        @block.tensor
        def _(pe):
            pe.wait_ge(ident_ready, 1)
            pe.wait_ge(gain_in, 32)
            pe.transpose(ps[:, OB, 0:2 * NK], gain_rows, ident[0:2 * NK, 0:2 * NK]).then_inc(gain_turned, 1)

            def turn_x(n):
                pe.wait_ge(x_scaled, n + 1)
                if n >= 2:
                    pe.wait_ge(x_gained, n - 1)
                    keys = count(HAS_K, slot_of_x(n) - 1)
                    if keys:
                        pe.wait_ge(k_done, keys)
                elif n == 1:
                    pe.wait_ge(gain_ready, 1)
                for k in range(NK):
                    ins = pe.transpose(wide(n)[:, k * P:(k + 1) * P], x_slot[n][:, k * P:(k + 1) * P], ident[:])
                ins.then_inc(x_turned, 1)

            for n in (0, 1):
                turn_x(n)

            def project(j, k):
                s, t = JOBS[j]
                kind, order, _, _, na, nb, tiles = STAGES[s]
                n = 8 * s + k
                if k == 0:
                    if kind in ("memk", "memv"):
                        x_split(pe, 2)
                    elif s == 2:
                        x_split(pe, 3 + t)
                    if j >= 2:
                        if count(QK_KINDS, j - 1):
                            pe.wait_ge(sq_done, count(QK_KINDS, j - 1))
                            pe.wait_ge(normed, count(QK_KINDS, j - 1))
                        if count(V_KINDS, j - 1):
                            pe.wait_ge(v_done, count(V_KINDS, j - 1))
                if t == 0:
                    w_split(pe, n)
                if kind in ("memk", "memv"):
                    hi, lo = (m[:, k, t * P:(t + 1) * P] for m in (mem_hi, mem_lo))
                else:
                    hi, lo = (token_tile(m[:, k, :], order, t) for m in (act_hi, act_lo))
                for i, (lhs, w) in enumerate(((hi, w_hi), (hi, w_lo), (lo, w_hi))):
                    ins = pe.matmul(proj_a(j)[:, 0:na], lhs, w[:, k, 0:na], start=(k == 0 and i == 0), stop=(k == 7 and i == 2))
                    if nb:
                        ins = pe.matmul(proj_b(j), lhs, w[:, k, na:na + nb], start=(k == 0 and i == 0), stop=(k == 7 and i == 2))
                if t == tiles - 1:
                    ins.then_inc(w_used, 1)
                    if k == 7:
                        pe.wait_ge(w_used, n + 1)
                        pe.nop().then_inc(proj_done, 1)
                elif k == 7:
                    ins.then_inc(proj_done, 1)

            def turn(j, batch):
                kind = KIND[j]
                if batch >= BATCHES[kind]:
                    return
                i = count(QK_KINDS, j)
                pe.wait_ge(roped, i + 1)
                bank_free(j, batch)
                bank = ps[:, TQ, :].rearrange("p (b n) -> p b n", n=P)
                buf = qk[:, i % 2, :]
                if kind == "B" and batch == 1:
                    ins = pe.transpose(bank[:, 0, :], buf[:, 512:640], ident[:])
                else:
                    for b in range(4):
                        ins = pe.transpose(bank[:, b, :], buf[:, b * P:(b + 1) * P], ident[:])
                ins.then_inc(turned, 1)

            def scores_read(n):
                if n >= 1:
                    pe.wait_ge(exp_done if KIND[UNITS[n - 1][0]] == "M" else min_done, n)

            def bank_free(j, batch):
                scores_read(units_scored(j + 1, TURN_AT[batch]))
                q = count(HAS_Q, j + (1 if batch else 0))
                k = count(HAS_K, j)
                if q:
                    pe.wait_ge(q_done, q)
                if k:
                    pe.wait_ge(k_done, k)

            def score(n):
                j, u = UNITS[n]
                kind = KIND[j]
                if kind != "M" or u == 0:
                    pe.wait_ge(q_done, count(HAS_Q, j) + 1)
                    pe.wait_ge(k_done, count(HAS_K, j) + (kind != "M"))
                scores_read(n)
                slot, k = slot_of(n)
                two = slot <= NJ and KIND[slot - 1] == "B"
                pe.wait_ge(q_done, count(HAS_Q, slot if k > TURN_AT[0] else slot - 1))
                pe.wait_ge(k_done, count(HAS_K, slot if k > TURN_AT[two] else slot - 1))
                for e in range(2):
                    if kind == "M":
                        h = 2 * u + e
                        ins = pe.matmul(scores[:, e, :], q_ring[:, j % RQ, h, :], k_mem[:, h, :], start=True, stop=True)
                        continue
                    rows = slice(64 * e, 64 * e + 64)
                    q = q_ring[rows, j % RQ, u, :]
                    kk = u if kind == "A" else 0
                    if has_prev(j):
                        pe.matmul(scores[:, e, 0:P], q, k_ring[rows, (j - 1) % RK, kk, :], start=True, stop=True)
                    ins = pe.matmul(scores[:, e, P:256], q, k_ring[rows, j % RK, kk, :], start=True, stop=True)
                ins.then_inc(scored, 1)

            def turn_probs(n):
                j = UNITS[n][0]
                if KIND[j] == "A":
                    pe.wait_ge(exp_done, n + 1)
                else:
                    pe.wait_ge(prob_done, count_bm(n) + 1)
                if n >= 1:
                    pe.wait_ge(prob_copied, n)
                for e in range(2):
                    for b in range(0 if has_prev(j) else 1, 2):
                        ins = pe.transpose(prob_turn[:, e, b, :], prob[:, n % 2, e, b * P:(b + 1) * P], ident[:])
                ins.then_inc(prob_turned, 1)

            def weigh_values(n):
                j, u = UNITS[n]
                kind = KIND[j]
                pe.wait_ge(prob_copied, n + 1)
                if n >= 1:
                    pe.wait_ge(o_done, n)
                used = merges_before(*slot_of(min(n + 2, NU - 1)))
                if used:
                    pe.wait_ge(factor_used, used)
                if kind != "M":
                    pe.wait_ge(v_done, count(V_KINDS, j + 1))
                first = 0 if has_prev(j) else 1
                for e in range(2):
                    for b in range(first, 2):
                        if kind == "M":
                            h = 2 * u + e
                            v = v_mem[:, b, h * P:(h + 1) * P]
                            dst = ps[:, OB, e * P:(e + 1) * P]
                        else:
                            c = 64 * (2 * u + e if kind == "A" else e)
                            v = v_ring[:, (j - 1 + b) % RK, c:c + 64]
                            dst = ps[64 * e:64 * e + 64, OB, 0:P]
                        ins = pe.matmul(dst, v, prob_t[:, n % 2, e, b, :], start=(b == first), stop=(b == 1))
                ins.then_inc(pv_done, 1)

            def turn_factors(m, j):
                pair, half, g = merge_batch(m)
                pe.wait_ge(o_done, units_scored(*MERGE_AT[m]) - 2)
                if m:
                    pe.wait_ge(factor_used, m)
                pe.wait_ge(spread_done, m + 1)
                for i in range(4):
                    ins = pe.transpose(ps[:, OB, i * P:(i + 1) * P], square[:, i * P:(i + 1) * P], ident[:])
                ins.then_inc(factor_turned, 1)

            n = 0
            for j in range(NJ + LAG + 1):
                if j == X_SLOTS[-1] + 1:
                    pe.wait_ge(x_gained, NX)
                for k in range(8):
                    if j < NJ:
                        project(j, k)
                    if k in step_slices(j):
                        score(n)
                        if n >= 1:
                            turn_probs(n - 1)
                        if n >= 2:
                            weigh_values(n - 2)
                        n += 1
                    if k in (3, 4) and pair_of(j):
                        turn_x(pair_of(j)[k - 3])
                    if k == TURN_AT[0] and 0 <= j - 1 < NJ:
                        if j <= X_SLOTS[-1]:
                            pe.wait_ge(x_gained, 1 + 2 * sum(slot <= j for slot in X_SLOTS) + (j not in X_SLOTS))
                        turn(j - 1, 0)
                    if k == TURN_AT[1] and 0 <= j - 1 < NJ:
                        turn(j - 1, 1)
                    if (j, k) in MERGE_AT:
                        turn_factors(MERGE_AT.index((j, k)), j)
            turn_probs(NU - 1)
            weigh_values(NU - 2)
            weigh_values(NU - 1)


def gated_outputs(nc, w_gate, b_gate, w_o_a, w_o_b, w_o_m, w_out, ps, act_hi, act_lo, attn_out, merged,
                  first_gate, first_gate_in, wo_raw, wo_in):
    NK = act_hi.shape[1]
    BR = 3
    BRANCH_TILES = [(0, 2), (6, 4), (2, 4)]
    O_SLOT = [0, 2, 6]
    UN = 2 * BR
    with ExitStack() as ctx:
        def sb(name, shape, dt=F32):
            return ctx.enter_context(nc.sbuf_tensor(name, shape, dt))

        def sem(name):
            return ctx.enter_context(nc.semaphore(name))

        g_raw = sb("g_raw", [P, BR, NK, P])
        g_hi = sb("g_hi", [P, BR, NK, P], F32R)
        g_lo = sb("g_lo", [P, BR, NK, P], F32R)
        o_raw = sb("o_raw", [P, 10, P])
        o_w = sb("o_w", [P, 10, P])
        bias = sb("gate_bias", [P, 2 * BR * NK])
        gate = sb("gate", [P, 2, 512])
        g_in = [first_gate_in] + [sem(f"g_in{b}") for b in range(1, BR)]
        g_hi_done = [sem(f"g_hi_done{b}") for b in range(BR)]
        g_lo_done = [sem(f"g_lo_done{b}") for b in range(BR)]
        g_used = [sem(f"g_used{b}") for b in range(BR)]
        o_in, o_copied, bias_in = sem("o_in"), sem("o_copied"), sem("bias_in")
        gate_summed, out_summed, gate_done, weighed, added = (
            sem(n) for n in ("gate_summed", "out_summed", "gate_done", "weighed", "added"))
        block = ctx.enter_context(nc.Block())

        @block.sync
        def _(sp):
            with nc.allow_non_contiguous_dma(reason="one bias per partition"):
                for half in range(2):
                    sp.dma_start(bias[:, half * BR * NK:(half + 1) * BR * NK], b_gate[0].rearrange("(k p) -> p k", p=P)
                                 ).then_inc(bias_in, 16)

            def load_tile(f, first=False):
                cols = bass.ds(f * P, P)
                for b in range(1 if first else 0, BR):
                    sp.wait_ge(g_lo_done[b], f)
                    sp.dma_start(g_raw[:, b], w_gate[0].rearrange("(k p) n -> p k n", p=P)[:, :, bass.ds(f * P + b * NK * P, P)]
                                 ).then_inc(g_in[b], 16)
                sp.wait_ge(o_copied, f)
                sp.dma_start(o_raw[:, 0:2], w_o_a[0].rearrange("(k p) n -> p k n", p=P)[:, :, cols]).then_inc(o_in, 16)
                for e in range(2):
                    sp.dma_start(o_raw[64 * e:64 * e + 64, 2:6],
                                 w_o_b[0].rearrange("(e j d) n -> e d j n", e=2, d=64)[e][:, :, cols]).then_inc(o_in, 16)
                sp.dma_start(o_raw[:, 6:10], w_o_m[0].rearrange("(k p) n -> p k n", p=P)[:, :, cols]).then_inc(o_in, 16)

            load_tile(0, True)
            sp.wait_ge(g_lo_done[0], 1)
            for n in range(NRAW_O):
                load_w_out(sp, w_out, wo_raw, wo_in, n)
            with sp.Fori(1, NK) as f:
                load_tile(f)

        @block.scalar
        def _(act):
            def cast(f, b, first=False):
                act.wait_ge(g_in[b], 16 * (f + 1))
                act.wait_ge(g_used[b], f)
                act.activation(g_hi[:, b], first_gate if first and b == 0 else g_raw[:, b], ACT.Copy).then_inc(g_hi_done[b], 1)

            def copy_weights(f):
                act.wait_ge(o_in, 64 * (f + 1))
                act.wait_ge(out_summed, UN * f)
                act.activation(o_w[:], o_raw[:], ACT.Copy).then_inc(o_copied, 1)

            def tile(f, first, last):
                for b in range(BR):
                    for half in range(2):
                        u = 2 * b + half
                        act.wait_ge(gate_summed, UN * f + u + 1)
                        if not first or u >= 2:
                            act.wait_ge(added, UN * f + u - 1)
                        column = f + (half * BR + b) * NK
                        column = column if isinstance(f, int) else act.snap(column)
                        act.activation(gate[:, u % 2, :], ps[:, 2 * (u % 3), :], ACT.Sigmoid,
                                       bias=bias[:, bass.ds(column, 1)]).then_inc(gate_done, 1)
                    if not last:
                        cast(f + 1, b)
                if not last:
                    copy_weights(f + 1)

            for b in range(BR):
                cast(0, b, True)
            copy_weights(0)
            act.wait_ge(bias_in, 32)
            tile(0, True, False)
            with act.Fori(1, NK - 1) as f:
                tile(f, False, False)
            tile(NK - 1, False, True)

        @block.gpsimd
        def _(pool):
            def low(f, b):
                pool.wait_ge(g_hi_done[b], f + 1)
                pool.tensor_tensor(g_lo[:, b], g_raw[:, b], g_hi[:, b].bitcast(F32), ALU.subtract).then_inc(g_lo_done[b], 1)

            for b in range(1, BR):
                low(0, b)
            with pool.Fori(1, NK) as f:
                for b in range(BR):
                    low(f, b)

        @block.vector
        def _(dve):
            def tile(f, first):
                for u in range(UN):
                    b, half = u // 2, u % 2
                    at = UN * f + u
                    dve.wait_ge(gate_done, at + 1)
                    dve.wait_ge(out_summed, at + 1)
                    dve.tensor_tensor(gate[:, u % 2, :], ps[:, 2 * (u % 3) + 1, :], gate[:, u % 2, :], ALU.mult).then_inc(weighed, 1)
                    dve.wait_ge(weighed, at + 1)
                    dst = merged[:, bass.ds(f, 1), half * 512:(half + 1) * 512]
                    src = gate[:, u % 2:u % 2 + 1, :]
                    if b == 0:
                        dve.tensor_copy(dst, src).then_inc(added, 1)
                    else:
                        dve.wait_ge(added, at - 1)
                        dve.tensor_tensor(dst, dst, src, ALU.add).then_inc(added, 1)

            dve.wait_ge(g_hi_done[0], 1)
            dve.tensor_tensor(g_lo[:, 0], first_gate, g_hi[:, 0].bitcast(F32), ALU.subtract).then_inc(g_lo_done[0], 1)
            with dve.Fori(0, NK) as f:
                tile(f, False)

        @block.tensor
        def _(pe):
            def tile(f, first):
                for u in range(UN):
                    b, half = u // 2, u % 2
                    at = UN * f + u
                    cols = slice(half * 512, (half + 1) * 512)
                    if half == 0:
                        pe.wait_ge(g_lo_done[b], f + 1)
                    if not first or u >= 3:
                        pe.wait_ge(weighed, at - 2)
                    for k in range(NK):
                        for i, (w, a) in enumerate(((g_hi, act_hi), (g_hi, act_lo), (g_lo, act_hi))):
                            ins = pe.matmul(ps[:, 2 * (u % 3), :], w[:, b, k, :], a[:, k, cols],
                                            start=(k == 0 and i == 0), stop=(k == NK - 1 and i == 2))
                    ins.then_inc(gate_summed, 1)
                    if half == 1:
                        pe.wait_ge(gate_summed, at + 1)
                        pe.nop().then_inc(g_used[b], 1)
                    if u == 0:
                        pe.wait_ge(o_copied, f + 1)
                    t0, tiles = BRANCH_TILES[b]
                    for i in range(tiles):
                        ins = pe.matmul(ps[:, 2 * (u % 3) + 1, :], o_w[:, O_SLOT[b] + i, :], attn_out[:, t0 + i, cols],
                                        start=(i == 0), stop=(i == tiles - 1))
                    ins.then_inc(out_summed, 1)

            tile(0, True)
            with pe.Fori(1, NK) as f:
                tile(f, False)


def output_projection(nc, x_t, w_out, ffn_norm, conv_w, conv_b, w_up, ps, act_hi, act_lo, ident, half_power,
                      merged, x1, spare, wo_raw, wo_in, taps, f_raw, f_in):
    NT, NK, D = x1.shape[1], act_hi.shape[1], x1.shape[2]
    TAPS = taps.shape[2]
    taps_raw = spare[0:TAPS, 0, 0:4 * P].rearrange("p (j n) -> p j n", j=4)
    with ExitStack() as ctx:
        def sb(name, shape, dt=F32):
            return ctx.enter_context(nc.sbuf_tensor(name, shape, dt))

        def sem(name):
            return ctx.enter_context(nc.semaphore(name))

        wo_hi = sb("wo_hi", [P, 2, NK, 512], F32R)
        wo_lo = sb("wo_lo", [P, 2, NK, 512], F32R)
        gain = sb("ffn_gain", [P, NK])
        sums = sb("x1_sums", [P, NT])
        rstd = sb("x1_rstd", [P, NT])
        res_in = [sem(f"res_in{t}") for t in range(NT // 2)]
        taps_in, taps_turned = sem("taps_in"), sem("taps_turned")
        gain_in, wo_hi_done, wo_lo_done, m_hi, m_lo = (sem(n) for n in ("gain_in", "wo_hi_done", "wo_lo_done", "m_hi", "m_lo"))
        out_done, x1_done, x1_sq, x1_ms, x1_rs, x1_scaled, x1_turned, x1_gained, h_hi, h_lo = (
            sem(n) for n in ("out_done", "x1_done", "x1_sq", "x1_ms", "x1_rs", "x1_scaled", "x1_turned", "x1_gained", "h_hi", "h_lo"))
        NS = 2 * NK

        SUMS = [(t, 0) for t in range(4)] + [(t, 1) for t in range(4)] + [(t, h) for t in range(4, NT) for h in range(2)]

        def turned(t):
            return ps[:, 4 + 2 * (t % 2):6 + 2 * (t % 2), :].rearrange("p b n -> p (b n)")

        block = ctx.enter_context(nc.Block())

        @block.sync
        def _(sp):
            with nc.allow_non_contiguous_dma(reason="one gain per partition"):
                sp.dma_start(gain[:, :], ffn_norm[0].rearrange("(k p) -> p k", p=P)).then_inc(gain_in, 16)
            for n in range(NRAW_O, NS):
                sp.wait_ge(wo_lo_done, n - NRAW_O + 1)
                load_w_out(sp, w_out, wo_raw, wo_in, n)
                if n < NRAW_O + NT:
                    t = n - NRAW_O
                    sp.dma_start(x1[:, t, :], x_t[t]).then_inc(res_in[t // 2], 16)
            for j in range(3):
                sp.dma_start(taps_raw[:, j, :], conv_w[0, j].rearrange("(t n) -> t n", n=P)).then_inc(taps_in, 16)
            sp.dma_start(taps_raw[:, 3, :], conv_b[0].rearrange("(t n) -> t n", n=P)).then_inc(taps_in, 16)
            sp.wait_ge(m_lo, NK)
            for b in range(4):
                load_w_up(sp, w_up, f_raw[b], b, 0, f_in)

        @block.scalar
        def _(act):
            for n in range(NS):
                if n < NK:
                    act.activation(act_hi[:, n, :], merged[:, n, :], ACT.Copy).then_inc(m_hi, 1)
                act.wait_ge(wo_in[n % NRAW_O], 16 * (n // NRAW_O + 1))
                act.activation(wo_hi[:, n // NK, n % NK, :], wo_raw[:, n % NRAW_O, :], ACT.Copy).then_inc(wo_hi_done, 1)

            def high(t):
                act.wait_ge(x1_gained, t + 1)
                act.activation(act_hi[:, :, t * P:(t + 1) * P], merged[:, t % 2, :].rearrange("p (k n) -> p k n", n=P),
                               ACT.Copy).then_inc(h_hi, 1)

            for t in range(NT):
                if t == 0:
                    act.wait_ge(m_lo, NK)
                act.wait_ge(x1_done, SUMS.index((t, 1)) + 1)
                if t >= 2:
                    act.wait_ge(h_lo, t - 1)
                act.activation(merged[:, t % 2, :], x1[:, t, :], ACT.Square, accum_out=sums[:, t:t + 1]).then_inc(x1_sq, 1)
                if t >= 1:
                    high(t - 1)
            act.wait_ge(taps_turned, 1)
            act.activation(taps[:].rearrange("p j n -> p (j n)"), ps[:, 0, 0:4 * TAPS], ACT.Copy)
            high(NT - 1)

        @block.gpsimd
        def _(pool):
            for n in range(NS):
                pool.wait_ge(wo_hi_done, n + 1)
                pool.tensor_tensor(wo_lo[:, n // NK, n % NK, :], wo_raw[:, n % NRAW_O, :],
                                   wo_hi[:, n // NK, n % NK, :].bitcast(F32), ALU.subtract).then_inc(wo_lo_done, 1)

            def low(t):
                pool.wait_ge(h_hi, t + 1)
                pool.tensor_tensor(act_lo[:, :, t * P:(t + 1) * P], merged[:, t % 2, :].rearrange("p (k n) -> p k n", n=P),
                                   act_hi[:, :, t * P:(t + 1) * P].bitcast(F32), ALU.subtract).then_inc(h_lo, 1)

            for t in range(NT):
                pool.wait_ge(x1_sq, t + 1)
                pool.tensor_scalar(rstd[:, t:t + 1], sums[:, t:t + 1], 1.0 / D, EPS, ALU.mult, ALU.add).then_inc(x1_ms, 1)
                pool.wait_ge(x1_ms, t + 1)
                pool.tensor_tensor(rstd[:, t:t + 1], rstd[:, t:t + 1], half_power[:, 0:1], ALU.pow).then_inc(x1_rs, 1)
                if t >= 1:
                    low(t - 1)

        @block.vector
        def _(dve):
            def gained(t):
                dve.wait_ge(x1_turned, t + 1)
                dve.tensor_tensor(merged[:, t % 2, :].rearrange("p (k n) -> p k n", n=P),
                                  turned(t).rearrange("p (k n) -> p k n", n=P),
                                  gain[:].unsqueeze(2).to_broadcast([P, NK, P]), ALU.mult).then_inc(x1_gained, 1)

            for k in range(NK):
                dve.wait_ge(m_hi, k + 1)
                dve.tensor_tensor(act_lo[:, k, :], merged[:, k, :], act_hi[:, k, :].bitcast(F32), ALU.subtract).then_inc(m_lo, 1)
            dve.wait_ge(gain_in, 16)
            for n, (t, half) in enumerate(SUMS):
                if half == 0:
                    dve.wait_ge(res_in[t // 2], 32)
                dve.wait_ge(out_done, n + 1)
                dst = x1[:, t, half * 512:(half + 1) * 512]
                dve.tensor_tensor(dst, ps[:, n % 4, :], dst, ALU.add).then_inc(x1_done, 1)
                if half == 0:
                    continue
                if t >= 1:
                    gained(t - 1)
                dve.wait_ge(x1_rs, t + 1)
                dve.tensor_scalar(merged[:, t % 2, :], x1[:, t, :], rstd[:, t:t + 1], None, ALU.mult).then_inc(x1_scaled, 1)
            gained(NT - 1)
            t = NT - 1
            dve.wait_ge(h_hi, t + 1)
            dve.tensor_tensor(act_lo[:, :, t * P:(t + 1) * P], merged[:, t % 2, :].rearrange("p (k n) -> p k n", n=P),
                              act_hi[:, :, t * P:(t + 1) * P].bitcast(F32), ALU.subtract)

        @block.tensor
        def _(pe):
            def turn(t):
                pe.wait_ge(x1_scaled, t + 1)
                if t >= 2:
                    pe.wait_ge(x1_gained, t - 1)
                for k in range(NK):
                    ins = pe.transpose(turned(t)[:, k * P:(k + 1) * P], merged[:, t % 2, k * P:(k + 1) * P], ident[:])
                ins.then_inc(x1_turned, 1)

            def share(n, k):
                t, half = SUMS[n]
                for i, (a, w) in enumerate(((act_hi, wo_hi), (act_hi, wo_lo), (act_lo, wo_hi))):
                    ins = pe.matmul(ps[:, n % 4, :], a[:, k, t * P:(t + 1) * P], w[:, half, k, :],
                                    start=(k == 0 and i == 0), stop=(k == NK - 1 and i == 2))
                if k == NK - 1:
                    ins.then_inc(out_done, 1)

            for k in range(NK):
                pe.wait_ge(m_lo, k + 1)
                pe.wait_ge(wo_lo_done, k + 1)
                for n in range(4):
                    share(n, k)
            for n in range(4, 2 * NT):
                pe.wait_ge(x1_done, n - 3)
                for k in range(NK):
                    if n == 4:
                        pe.wait_ge(wo_lo_done, NK + k + 1)
                    share(n, k)
                t, half = SUMS[n]
                if half == 1 and t >= 1:
                    turn(t - 1)
            pe.wait_ge(taps_in, 64)
            pe.wait_ge(x1_done, 2 * NT - 3)
            for j in range(4):
                ins = pe.transpose(ps[:, 0, j * TAPS:(j + 1) * TAPS], taps_raw[:, j, :], ident[0:TAPS, 0:TAPS])
            ins.then_inc(taps_turned, 1)
            turn(NT - 1)


def feed_forward(nc, w_up, w_down, out_t, ps, act_hi, act_lo, x1, conv, taps, f_raw, f_in):
    NK, S, NT = act_hi.shape[1], act_hi.shape[2], x1.shape[1]
    FF = w_down.shape[1]
    FT = FF // P
    NC = FT // 2
    YN = 2 * NT
    with ExitStack() as ctx:
        def sb(name, shape, dt=F32):
            return ctx.enter_context(nc.sbuf_tensor(name, shape, dt))

        def sem(name):
            return ctx.enter_context(nc.semaphore(name))

        f_hi = sb("f_hi", [P, 6, 1024], F32R)
        f_lo = sb("f_lo", [P, 6, 1024], F32R)
        z_hi = sb("z_hi", [P, 2, S], F32R)
        z_lo = sb("z_lo", [P, 2, S], F32R)
        f_hi_done = [sem(f"f_hi_done{b}") for b in range(6)]
        f_lo_done = [sem(f"f_lo_done{b}") for b in range(6)]
        u_done = [sem(f"u_done{q}") for q in range(4)]
        tap2_done = [sem(f"tap2_done{q}") for q in range(4)]
        tap1_done = [sem(f"tap1_done{q}") for q in range(4)]
        tap0_done = [sem(f"tap0_done{q}") for q in range(4)]
        silu_done = [sem(f"silu_done{p}") for p in range(2)]
        z_done = [sem(f"z_done{p}") for p in range(2)]
        z_hi_done = [sem(f"z_hi_done{p}") for p in range(2)]
        z_lo_done = [sem(f"z_lo_done{p}") for p in range(2)]
        y_done, y_added, stored = sem("y_done"), sem("y_added"), sem("stored")

        HALVES = [slice(0, S // 2), slice(S // 2, S)]

        def block_low(eng, b, c):
            eng.wait_ge(f_hi_done[b], c + 1)
            eng.tensor_tensor(f_lo[:, b, :], f_raw[b], f_hi[:, b, :].bitcast(F32), ALU.subtract).then_inc(f_lo_done[b], 1)

        def up_psum(q):
            return ps[:, 2 * q:2 * q + 2, :].rearrange("p b n -> p (b n)")

        block = ctx.enter_context(nc.Block())

        @block.sync
        def _(sp):
            def load(b, c):
                sp.wait_ge(f_lo_done[b], c)
                if b < 4:
                    load_w_up(sp, w_up, f_raw[b], b, c, f_in)
                else:
                    sp.dma_start(f_raw[b], w_down[0, bass.ds((2 * c + b - 4) * P, P), :]).then_inc(f_in[b], 16)

            def chunk(c, down, more):
                if down:
                    load(4, c - 1)
                    load(5, c - 1)
                if down:
                    load(2, c)
                    load(3, c)
                if more:
                    load(0, c + 1)
                    load(1, c + 1)

            chunk(0, False, True)
            chunk(1, True, True)
            with sp.Fori(2, NC - 1) as c:
                chunk(c, True, True)
            chunk(NC - 1, True, False)
            load(4, NC - 1)
            load(5, NC - 1)
            for t in range(NT):
                sp.wait_ge(y_added, YN * (NC - 1) + 2 * t + 2)
                sp.dma_start(out_t[t], x1[:, t, :]).then_inc(stored, 16)
            sp.wait_ge(stored, 16 * NT)

        @block.gpsimd
        def _(pool):
            def low(b, c):
                block_low(pool, b, c)

            def z_low(p, c, part=0, tokens=slice(0, S)):
                pool.wait_ge(z_hi_done[p], c + 1 + part)
                pool.tensor_tensor(z_lo[:, p, tokens], conv[p][:, 0, tokens], z_hi[:, p, tokens].bitcast(F32),
                                   ALU.subtract).then_inc(z_lo_done[p], 1)

            def chunk(c, down, more):
                if down:
                    z_low(1, c - 1)
                    low(4, c - 1)
                    low(5, c - 1)
                low(2, c)
                low(3, c)
                if more:
                    low(0, c + 1)
                    low(1, c + 1)
                z_low(0, c)

            low(1, 0)
            chunk(0, False, True)
            with pool.Fori(1, NC - 1) as c:
                chunk(c, True, True)
            chunk(NC - 1, True, False)
            low(4, NC - 1)
            low(5, NC - 1)
            for part, tokens in enumerate(HALVES):
                z_low(1, NC - 1, part, tokens)

        @block.scalar
        def _(act):
            def high(b, c):
                act.wait_ge(f_in[b], 16 * (c + 1))
                if b < 4:
                    act.wait_ge(u_done[b], c)
                else:
                    act.wait_ge(y_done, YN * c)
                act.activation(f_hi[:, b, :], f_raw[b], ACT.Copy).then_inc(f_hi_done[b], 1)

            def last_own_taps(part):
                for e in range(2):
                    q, feature = 2 + e, 2 * NC - 1 + e * FT
                    act.wait_ge(u_done[q], NC + part)
                    if e == 0 and part == 0:
                        act.wait_ge(z_lo_done[1], NC - 1)
                    act.activation(conv[1][:, e, HALVES[part]], up_psum(q)[:, HALVES[part]], ACT.Identity,
                                   scale=taps[:, 2, feature:feature + 1], bias=taps[:, 3, feature:feature + 1]
                                   ).then_inc(tap2_done[q], 1)

            def last_silu(part):
                act.wait_ge(tap0_done[2], NC + part)
                a = conv[1][:, 0, HALVES[part]]
                act.activation(a, a, ACT.Silu).then_inc(silu_done[1], 1)

            def own_tap(p, c):
                for e in range(2):
                    q = 2 * p + e
                    act.wait_ge(u_done[q], c + 1)
                    if e == 0:
                        act.wait_ge(z_lo_done[p], c)
                    feature = 2 * c + p + e * FT if isinstance(c, int) else act.snap(2 * c + p + e * FT)
                    act.activation(conv[p][:, e, :], up_psum(q), ACT.Identity, scale=taps[:, 2, bass.ds(feature, 1)],
                                   bias=taps[:, 3, bass.ds(feature, 1)]).then_inc(tap2_done[q], 1)
                act.wait_ge(tap0_done[2 * p], c + 1)
                act.activation(conv[p][:, 0, :], conv[p][:, 0, :], ACT.Silu).then_inc(silu_done[p], 1)

            def z_high(p, c, part=0, tokens=slice(0, S)):
                act.wait_ge(z_done[p], c + 1 + part)
                act.wait_ge(y_done, YN * c)
                act.activation(z_hi[:, p, tokens], conv[p][:, 0, tokens], ACT.Copy).then_inc(z_hi_done[p], 1)

            def chunk(c, down, more):
                if down:
                    own_tap(1, c - 1)
                    z_high(1, c - 1)
                    high(4, c - 1)
                    high(5, c - 1)
                high(2, c)
                high(3, c)
                own_tap(0, c)
                if more:
                    high(0, c + 1)
                    high(1, c + 1)
                z_high(0, c)

            high(0, 0)
            high(1, 0)
            chunk(0, False, True)
            chunk(1, True, True)
            with act.Fori(2, NC - 1) as c:
                chunk(c, True, True)
            chunk(NC - 1, True, False)
            high(4, NC - 1)
            high(5, NC - 1)
            last_own_taps(0)
            last_silu(0)
            z_high(1, NC - 1, 0, HALVES[0])
            last_own_taps(1)
            last_silu(1)
            z_high(1, NC - 1, 1, HALVES[1])

        @block.vector
        def _(dve):
            def other_taps(q, c):
                p, e = q // 2, q % 2
                dst = conv[p][:, e, :]
                feature = 2 * c + p + e * FT
                dve.wait_ge(tap2_done[q], c + 1)
                dve.scalar_tensor_tensor(out=dst[:, 1:S], in0=up_psum(q)[:, 0:S - 1], scalar=taps[:, 1, bass.ds(feature, 1)],
                                         in1=dst[:, 1:S], op0=ALU.mult, op1=ALU.add).then_inc(tap1_done[q], 1)
                dve.wait_ge(tap1_done[q], c + 1)
                dve.scalar_tensor_tensor(out=dst[:, 2:S], in0=up_psum(q)[:, 0:S - 2], scalar=taps[:, 0, bass.ds(feature, 1)],
                                         in1=dst[:, 2:S], op0=ALU.mult, op1=ALU.add).then_inc(tap0_done[q], 1)

            def last_taps(q, part):
                dst, feature = conv[1][:, q - 2, :], 2 * NC - 1 + (q - 2) * FT
                hi = HALVES[part].stop
                for back, tap, before, done in ((1, 1, tap2_done, tap1_done), (2, 0, tap1_done, tap0_done)):
                    lo = max(HALVES[part].start, back)
                    dve.wait_ge(before[q], NC + part)
                    dve.scalar_tensor_tensor(out=dst[:, lo:hi], in0=up_psum(q)[:, lo - back:hi - back],
                                             scalar=taps[:, tap, feature:feature + 1], in1=dst[:, lo:hi],
                                             op0=ALU.mult, op1=ALU.add).then_inc(done[q], 1)

            def product(p, c, part=0, tokens=slice(0, S)):
                dve.wait_ge(silu_done[p], c + 1 + part)
                dve.wait_ge(tap0_done[2 * p + 1], c + 1 + part)
                dve.tensor_tensor(conv[p][:, 0, tokens], conv[p][:, 0, tokens], conv[p][:, 1, tokens], ALU.mult
                                  ).then_inc(z_done[p], 1)

            def last_add(i):
                dst = x1[:, i // 2, (i % 2) * 512:(i % 2 + 1) * 512]
                dve.wait_ge(y_done, YN * (NC - 1) + i + 1)
                dve.tensor_tensor(dst, ps[:, i % 4, :], dst, ALU.add).then_inc(y_added, 1)

            def add(i, c):
                dst = x1[:, i // 2, (i % 2) * 512:(i % 2 + 1) * 512]
                dve.wait_ge(y_done, YN * c + i + 1)
                dve.tensor_tensor(dst, ps[:, 4 + i % 4, :], dst, ALU.add).then_inc(y_added, 1)

            def chunk(c, down):
                if down:
                    other_taps(2, c - 1)
                    other_taps(3, c - 1)
                    product(1, c - 1)
                other_taps(0, c)
                if down:
                    add(0, c - 1)
                other_taps(1, c)
                if down:
                    for i in range(1, 4):
                        add(i, c - 1)
                product(0, c)
                if down:
                    for i in range(4, YN):
                        add(i, c - 1)
                    dve.wait_ge(y_added, YN * c)

            block_low(dve, 0, 0)
            chunk(0, False)
            chunk(1, True)
            with dve.Fori(2, NC) as c:
                chunk(c, True)
            for part, tokens in enumerate(HALVES):
                last_taps(2, part)
                last_taps(3, part)
                product(1, NC - 1, part, tokens)
            for i in range(YN):
                last_add(i)

        @block.tensor
        def _(pe):
            def up(q, c, first, last=False):
                pe.wait_ge(f_lo_done[q], c + 1)
                if q < 2:
                    pe.wait_ge(tap0_done[q], c)
                for half in range(2):
                    if q >= 2 and not first:
                        pe.wait_ge(y_added, YN * c - 3 + 2 * (q - 2) + half)
                    for k in range(NK):
                        for i, (w, a) in enumerate(((f_hi, act_hi), (f_hi, act_lo), (f_lo, act_hi))):
                            ins = pe.matmul(ps[:, 2 * q + half, :], w[:, q, k * P:(k + 1) * P],
                                            a[:, k, half * 512:(half + 1) * 512],
                                            start=(k == 0 and i == 0), stop=(k == NK - 1 and i == 2))
                    if last or half == 1:
                        ins.then_inc(u_done[q], 1)

            def down(c, last=False):
                for p in range(2):
                    pe.wait_ge(z_lo_done[p], c + 1)
                    pe.wait_ge(f_lo_done[4 + p], c + 1)
                    pe.wait_ge(tap0_done[p if last else 2 + p], c + 1)
                for i in range(YN):
                    t, half = i // 2, i % 2
                    if last and t == NT // 2 and half == 0:
                        pe.wait_ge(z_lo_done[1], c + 2)
                    if i >= 4:
                        pe.wait_ge(y_added, YN * c + i - 3)
                    for p in range(2):
                        for m, (z, w) in enumerate(((z_hi, f_hi), (z_hi, f_lo), (z_lo, f_hi))):
                            ins = pe.matmul(ps[:, (0 if last else 4) + i % 4, :], z[:, p, t * P:(t + 1) * P],
                                            w[:, 4 + p, half * 512:(half + 1) * 512],
                                            start=(p == 0 and m == 0), stop=(p == 1 and m == 2))
                    ins.then_inc(y_done, 1)

            up(0, 0, True)
            up(1, 0, True)
            up(2, 0, True)
            up(3, 0, True)
            with pe.Fori(1, NC - 1) as c:
                up(0, c, False)
                up(1, c, False)
                down(c - 1)
                up(2, c, False)
                up(3, c, False)
            up(0, NC - 1, False)
            up(1, NC - 1, False)
            down(NC - 2)
            up(2, NC - 1, False, True)
            up(3, NC - 1, False, True)
            down(NC - 1, True)


_INS = ['x', 'mem', 'positions', 'attn_norm', 'w_in', 'a_q_norm', 'a_k_norm', 'b_q_norm', 'b_k_norm', 'b_sinks',
        'mem_norm', 'w_mem_kv', 'm_q_norm', 'm_k_norm', 'w_o_a', 'w_o_b', 'w_o_m', 'w_gate', 'b_gate', 'w_out',
        'ffn_norm', 'w_up', 'conv_w', 'conv_b', 'w_down']
_OUTS = [((1, 1024, 1024), 'float32')]


def kernel(**inputs):
    import numpy as _np
    import concourse.bacc as _bacc
    from concourse import mybir as _mybir
    from concourse.bass_utils import run_bass_kernel_spmd as _run

    nc = _bacc.Bacc("TRN2", target_bir_lowering=False, num_devices=1)
    arrays, args = {}, []
    for name in _INS:
        a = _np.ascontiguousarray(inputs[name])
        arrays[f"in_{name}_dram"] = a
        args.append(nc.dram_tensor(f"in_{name}_dram", a.shape, _mybir.dt.from_np(a.dtype), kind="ExternalInput").ap())
    for i, (shape, dtype) in enumerate(_OUTS):
        dt = _mybir.dt.from_np(_np.dtype(dtype))
        args.append(nc.dram_tensor(f"out_{i}_dram", shape, dt, kind="ExternalOutput").ap())
    layer(nc, *args)
    r = _run(nc, [arrays], core_ids=[0])
    return r.results[0]["out_0_dram"]
```
